# Optimizing a Trainium2 kernel written in Bass

```python
import math
import jax
import jax.numpy as jnp
from jax import lax
import numpy as np
import jax, jax.numpy as jnp

D_MODEL = 2048
BATCH = 1
SEQ = 256
DEPTH = 1

CTX_LEN = 256
GRID_W = 64
EPS = 1e-6
N_MOD = 6
D_MIX = D_MODEL
HY_W = D_MIX // 2
HY_GROUPS = 8
HY_ORDER = 2
HY_PROJ = (HY_ORDER + 1) * HY_W
HY_CONV = 3
HY_POS_EMB = 33
HY_FILT_H = 64
HY_TARGET = 1e-2
HY_FAST = 0.3
HY_SLOW = 1.5
SSD_W = D_MIX - HY_W
SSD_HEADDIM = 64
SSD_HEADS = SSD_W // SSD_HEADDIM
SSD_GROUPS = 2
SSD_HPG = SSD_HEADS // SSD_GROUPS
SSD_STATE = 128
SSD_CONV = 3
SSD_CHUNK = 128
SSD_XBC = SSD_W + 2 * SSD_GROUPS * SSD_STATE
SSD_DT = 2 * SSD_HEADS
PROJ_W = HY_PROJ + SSD_XBC + SSD_DT + SSD_W
D_FF = 4 * D_MODEL


def rmsnorm(x, w):
    xf = x.astype(jnp.float32)
    y = xf * lax.rsqrt(jnp.mean(xf * xf, axis=-1, keepdims=True) + EPS)
    return (y * w).astype(x.dtype)

def centred_dwconv(u, w, bias, grid):
    b, L, C = u.shape
    if grid is not None:
        u = u.reshape(b, grid[0], grid[1], C)
    K = w.shape[0]
    pad = K // 2
    T = u.shape[-2]
    up = jnp.pad(u, [(0, 0)] * (u.ndim - 2) + [(pad, pad), (0, 0)])
    y = bias + w[0] * up[..., 0:T, :]
    for k in range(1, K):
        y = y + w[k] * up[..., k:k + T, :]
    return y.reshape(b, L, C)

def hyena_kernel_fft(L, fw1, fb1, freq, fw2, fb2, fw3):
    f32 = jnp.float32
    t = jnp.linspace(0.0, 1.0, L, dtype=f32)[:, None]
    bands = (HY_POS_EMB - 1) // 2
    w = 2.0 * math.pi * jnp.arange(L, dtype=f32)[:, None] / L
    f = jnp.linspace(1e-4, bands - 1, bands, dtype=f32)[None, :]
    feats = jnp.concatenate([t, jnp.cos(f * w), -jnp.sin(f * w)], axis=-1)
    hdn = jnp.sin(freq * (feats @ fw1 + fb1))
    hdn = jnp.sin(freq * (hdn @ fw2 + fb2))
    h = (hdn @ fw3).astype(f32).reshape(L, HY_ORDER, 2, HY_W)
    deltas = jnp.linspace(math.log(HY_TARGET) / HY_SLOW, math.log(HY_TARGET) / HY_FAST, HY_W, dtype=f32)
    h = h * jnp.exp(-t[:, :, None, None] * jnp.abs(deltas))
    k = jnp.concatenate([h[:, :, 0], jnp.zeros((1, HY_ORDER, HY_W), f32), h[:0:-1, :, 1]], axis=0)
    k = k / (jnp.sum(jnp.abs(k), axis=0, keepdims=True) + EPS)
    return jnp.fft.rfft(k, axis=0)

def fft_conv(z, kf):
    L = z.shape[1]
    zf = jnp.fft.rfft(z, n=2 * L, axis=1)
    return jnp.fft.irfft(zf * kf[None], n=2 * L, axis=1)[:, :L]

def segsum(a):
    T = a.shape[-1]
    cs = jnp.cumsum(a, axis=-1)
    diff = cs[..., :, None] - cs[..., None, :]
    mask = jnp.tril(jnp.ones((T, T), dtype=bool))
    return jnp.where(mask, diff, -jnp.inf)

def ssd_scan(xdt, da, bm, cm, init, want_y):
    b, l, g, r, p = xdt.shape
    nc = l // SSD_CHUNK
    xdt = xdt.reshape(b, nc, SSD_CHUNK, g, r, p)
    bc = bm.reshape(b, nc, SSD_CHUNK, g, -1)
    a = da.reshape(b, nc, SSD_CHUNK, g, r).transpose(0, 3, 4, 1, 2)
    a_cs = jnp.cumsum(a, axis=-1)
    decay_to_end = jnp.exp(a_cs[..., -1:] - a_cs)
    states = jnp.einsum('bcsgn,bgrcs,bcsgrp->bcgrpn', bc, decay_to_end, xdt)
    chunk_a = jnp.pad(a_cs[..., -1], ((0, 0), (0, 0), (0, 0), (1, 0)))
    states_all = jnp.concatenate([init[:, None], states], axis=1)
    carried = jnp.einsum('bgrzc,bcgrpn->bzgrpn', jnp.exp(segsum(chunk_a)), states_all)
    final = carried[:, -1]
    if not want_y:
        return final
    cc = cm.reshape(b, nc, SSD_CHUNK, g, -1)
    cb = jnp.einsum('bclgn,bcsgn->bgcls', cc, bc)
    y_diag = jnp.einsum('bgcls,bgrcls,bcsgrp->bclgrp', cb, jnp.exp(segsum(a)), xdt)
    y_off = jnp.einsum('bclgn,bcgrpn,bgrcl->bclgrp', cc, carried[:, :-1], jnp.exp(a_cs))
    y = (y_diag + y_off).reshape(b, l, g, r, p)
    return y, final

def ssd_branch(h, init_f, init_b, grid, lp, want_y):
    b, L, _ = h.shape
    f32 = jnp.float32
    w_in = lp['w_in']
    o0 = HY_PROJ
    o1 = o0 + SSD_XBC
    o2 = o1 + SSD_DT
    xbc = jax.nn.silu(centred_dwconv(h @ w_in[:, o0:o1], lp['ssd_conv_w'], lp['ssd_conv_b'], grid)).astype(f32)
    gn = SSD_GROUPS * SSD_STATE
    xs = xbc[..., :SSD_W].reshape(b, L, SSD_GROUPS, SSD_HPG, SSD_HEADDIM)
    bm = xbc[..., SSD_W:SSD_W + gn].reshape(b, L, SSD_GROUPS, SSD_STATE)
    cm = xbc[..., SSD_W + gn:].reshape(b, L, SSD_GROUPS, SSD_STATE)
    dt = jax.nn.softplus((h @ w_in[:, o1:o2]).astype(f32).reshape(b, L, 2, SSD_HEADS) + lp['dt_bias'])
    dt = dt.reshape(b, L, 2, SSD_GROUPS, SSD_HPG)
    a = (-jnp.exp(lp['a_log'].astype(f32))).reshape(2, SSD_GROUPS, SSD_HPG)

    def run(d, init, flip):
        dt_d = dt[:, :, d]
        seqs = (xs * dt_d[..., None], dt_d * a[d], bm, cm)
        if flip:
            seqs = tuple(s[:, ::-1] for s in seqs)
        return ssd_scan(seqs[0], seqs[1], seqs[2], seqs[3], init, want_y)

    if not want_y:
        return run(0, init_f, False), run(1, init_b, True)
    y_f, s_f = run(0, init_f, False)
    y_b, s_b = run(1, init_b, True)
    y = y_f + y_b[:, ::-1] + lp['ssd_d'].reshape(SSD_GROUPS, SSD_HPG)[..., None] * xs
    zg = jax.nn.silu((h @ w_in[:, o2:]).astype(f32))
    y = (y.reshape(b, L, SSD_W) * zg).reshape(b, L, SSD_GROUPS, SSD_W // SSD_GROUPS)
    y = rmsnorm(y, lp['ssd_norm_w'].reshape(SSD_GROUPS, -1)).reshape(b, L, SSD_W)
    return y.astype(h.dtype), s_f, s_b

def token_mixer(h, init_f, init_b, grid, lp):
    b, L, _ = h.shape
    u = centred_dwconv(h @ lp['w_in'][:, :HY_PROJ], lp['hy_conv_w'], lp['hy_conv_b'], grid).astype(jnp.float32)
    v, *gates = jnp.split(u, HY_ORDER + 1, axis=-1)
    kf = hyena_kernel_fft(L, lp['filt_w1'], lp['filt_b1'], lp['filt_freq'], lp['filt_w2'], lp['filt_b2'], lp['filt_w3'])
    z = v
    for o, gate in enumerate(gates):
        z = gate * (fft_conv(z, kf[:, o]) + z * lp['hy_bias'][o])
    y_hy = rmsnorm(z.reshape(b, L, HY_GROUPS, HY_W // HY_GROUPS), lp['hy_norm_w'].reshape(HY_GROUPS, -1))
    y_hy = y_hy.reshape(b, L, HY_W).astype(h.dtype)
    y_ssd, s_f, s_b = ssd_branch(h, init_f, init_b, grid, lp, True)
    out = jnp.concatenate([y_hy, y_ssd], axis=-1) @ lp['w_out']
    return out, s_f, s_b

def sqrelu_mlp(h, w1, w2):
    return jnp.square(jax.nn.relu(h @ w1)) @ w2

def first_inputs(seed: int = 0) -> dict:
    key = jax.random.key(seed)
    ks = jax.random.split(key, 32)

    def nrm(k, shape, scale):
        return scale * jax.random.normal(k, shape, jnp.float32)

    D = D_MODEL
    dt0 = jnp.exp(jax.random.uniform(ks[20], (DEPTH, 2, SSD_HEADS), jnp.float32, math.log(1e-3), math.log(1e-1)))
    return {
        'x': nrm(ks[0], (BATCH, SEQ, D), 1.0),
        'c': nrm(ks[1], (BATCH, D), 1.0),
        'ctx': nrm(ks[2], (BATCH, CTX_LEN, D), 1.0),
        'c_ctx': nrm(ks[3], (D,), 1.0),
        'w_ada': nrm(ks[4], (DEPTH, D, N_MOD * D), 0.5 * D ** -0.5),
        'b_ada': nrm(ks[5], (DEPTH, N_MOD * D), 0.02),
        'norm1_w': 1.0 + nrm(ks[6], (DEPTH, D), 0.05),
        'w_in': nrm(ks[7], (DEPTH, D, PROJ_W), D ** -0.5),
        'hy_conv_w': nrm(ks[8], (DEPTH, HY_CONV, HY_PROJ), HY_CONV ** -0.5),
        'hy_conv_b': nrm(ks[9], (DEPTH, HY_PROJ), 0.02),
        'filt_w1': nrm(ks[10], (DEPTH, HY_POS_EMB, HY_FILT_H), HY_POS_EMB ** -0.5),
        'filt_b1': nrm(ks[11], (DEPTH, HY_FILT_H), 0.1),
        'filt_freq': 1.0 + nrm(ks[12], (DEPTH, HY_FILT_H), 0.1),
        'filt_w2': nrm(ks[13], (DEPTH, HY_FILT_H, HY_FILT_H), HY_FILT_H ** -0.5),
        'filt_b2': nrm(ks[14], (DEPTH, HY_FILT_H), 0.1),
        'filt_w3': nrm(ks[15], (DEPTH, HY_FILT_H, HY_ORDER * 2 * HY_W), HY_FILT_H ** -0.5),
        'hy_bias': nrm(ks[16], (DEPTH, HY_ORDER, HY_W), 0.1),
        'hy_norm_w': 1.0 + nrm(ks[17], (DEPTH, HY_W), 0.05),
        'ssd_conv_w': nrm(ks[18], (DEPTH, SSD_CONV, SSD_XBC), SSD_CONV ** -0.5),
        'ssd_conv_b': nrm(ks[19], (DEPTH, SSD_XBC), 0.02),
        'dt_bias': dt0 + jnp.log(-jnp.expm1(-dt0)),
        'a_log': jnp.log(jax.random.uniform(ks[21], (DEPTH, 2, SSD_HEADS), jnp.float32, 1.0, 16.0)),
        'ssd_d': 1.0 + nrm(ks[22], (DEPTH, SSD_HEADS), 0.05),
        'ssd_norm_w': 1.0 + nrm(ks[23], (DEPTH, SSD_W), 0.05),
        'w_out': nrm(ks[24], (DEPTH, D_MIX, D), D_MIX ** -0.5),
        'norm2_w': 1.0 + nrm(ks[25], (DEPTH, D), 0.05),
        'w_mlp1': nrm(ks[26], (DEPTH, D, D_FF), D ** -0.5),
        'w_mlp2': nrm(ks[27], (DEPTH, D_FF, D), D_FF ** -0.5),
        'final_norm_w': 1.0 + nrm(ks[28], (D,), 0.05),
    }

def first_block(x, c, ctx, c_ctx, w_ada, b_ada, norm1_w, w_in, hy_conv_w, hy_conv_b, filt_w1, filt_b1,
              filt_freq, filt_w2, filt_b2, filt_w3, hy_bias, hy_norm_w, ssd_conv_w, ssd_conv_b, dt_bias,
              a_log, ssd_d, ssd_norm_w, w_out, norm2_w, w_mlp1, w_mlp2, final_norm_w):
    rows = x.shape[1] // GRID_W
    grid = (rows, GRID_W)
    zero_state = jnp.zeros((x.shape[0], SSD_GROUPS, SSD_HPG, SSD_HEADDIM, SSD_STATE), jnp.float32)
    h_ctx = ctx
    for i in range(DEPTH):
        lp = dict(w_in=w_in[i], hy_conv_w=hy_conv_w[i], hy_conv_b=hy_conv_b[i], filt_w1=filt_w1[i],
                  filt_b1=filt_b1[i], filt_freq=filt_freq[i], filt_w2=filt_w2[i], filt_b2=filt_b2[i],
                  filt_w3=filt_w3[i], hy_bias=hy_bias[i], hy_norm_w=hy_norm_w[i], ssd_conv_w=ssd_conv_w[i],
                  ssd_conv_b=ssd_conv_b[i], dt_bias=dt_bias[i], a_log=a_log[i], ssd_d=ssd_d[i],
                  ssd_norm_w=ssd_norm_w[i], w_out=w_out[i])
        mod = (jax.nn.silu(c) @ w_ada[i] + b_ada[i])[:, None, :]
        mod_c = jax.nn.silu(c_ctx) @ w_ada[i] + b_ada[i]
        sh1, sc1, g1, sh2, sc2, g2 = jnp.split(mod, N_MOD, axis=-1)
        csh1, csc1, cg1, csh2, csc2, cg2 = jnp.split(mod_c, N_MOD, axis=-1)
        hc = rmsnorm(h_ctx, norm1_w[i]) * (1.0 + csc1) + csh1
        if i < DEPTH - 1:
            out_c, s_f, s_b = token_mixer(hc, zero_state, zero_state, None, lp)
            h_ctx = h_ctx + cg1 * out_c
            hc2 = rmsnorm(h_ctx, norm2_w[i]) * (1.0 + csc2) + csh2
            h_ctx = h_ctx + cg2 * sqrelu_mlp(hc2, w_mlp1[i], w_mlp2[i])
        else:
            s_f, s_b = ssd_branch(hc, zero_state, zero_state, None, lp, False)
        hl = rmsnorm(x, norm1_w[i]) * (1.0 + sc1) + sh1
        out_l, _, _ = token_mixer(hl, s_f, s_b, grid, lp)
        x = x + g1 * out_l
        hl2 = rmsnorm(x, norm2_w[i]) * (1.0 + sc2) + sh2
        x = x + g2 * sqrelu_mlp(hl2, w_mlp1[i], w_mlp2[i])
    return rmsnorm(x, final_norm_w)


MEM_TOKENS = 256
RET_HEADS = 8
RET_QK_DIM = 128
RET_V_DIM = 128
RET_CHUNK = 128
DIL_PATTERNS = ((128, 1), (512, 4), (2048, 16))
DIL_HEADS_PER_GROUP = 4
DIL_HEAD_DIM = 128
DIL_BLOCK = 128
ROPE_THETA = 10000.0
MEM_HEADS = 4
MEM_HEAD_DIM = D_MODEL // MEM_HEADS
PEER_HEADS = 8
PEER_N_KEYS = 128
PEER_N_EXPERTS = PEER_N_KEYS * PEER_N_KEYS
PEER_QUERY_DIM = 256
PEER_TOPK = 16
PEER_TOKEN_BLOCK = 128
NORM_EPS = 1e-6

RET_QK_W = RET_HEADS * RET_QK_DIM
RET_V_W = RET_HEADS * RET_V_DIM
DIL_N_GROUPS = len(DIL_PATTERNS)
DIL_QKV_W = DIL_N_GROUPS * DIL_HEADS_PER_GROUP * DIL_HEAD_DIM
DIL_OUT_W = DIL_HEADS_PER_GROUP * DIL_HEAD_DIM
IN_SPLIT_SIZES = (RET_QK_W, RET_QK_W, RET_V_W, RET_V_W, DIL_QKV_W, DIL_QKV_W, DIL_QKV_W, D_MODEL, D_MODEL)
IN_WIDTH = sum(IN_SPLIT_SIZES)
IN_SPLIT_POINTS = tuple(int(c) for c in np.cumsum(IN_SPLIT_SIZES)[:-1])


def rms_norm(x, g):
    xf = x.astype(jnp.float32)
    y = xf * lax.rsqrt(jnp.mean(xf * xf, axis=-1, keepdims=True) + NORM_EPS)
    return (y * g.astype(jnp.float32)).astype(x.dtype)

def rotary(x, pos):
    dh = x.shape[-1]
    half = dh // 2
    inv = 1.0 / (ROPE_THETA ** (jnp.arange(half, dtype=jnp.float32) / half))
    ang = pos.astype(jnp.float32)[..., None] * inv
    cos = jnp.cos(ang)[:, :, None, :]
    sin = jnp.sin(ang)[:, :, None, :]
    xf = x.astype(jnp.float32)
    x1, x2 = xf[..., :half], xf[..., half:]
    return jnp.concatenate([x1 * cos - x2 * sin, x2 * cos + x1 * sin], axis=-1).astype(x.dtype)

def retnet_rotate(x, pos):
    dh = x.shape[-1]
    angle = 1.0 / (10000.0 ** jnp.linspace(0.0, 1.0, dh // 2, dtype=jnp.float32))
    angle = jnp.repeat(angle, 2)
    ang = pos.astype(jnp.float32)[..., None] * angle
    cos = jnp.cos(ang)[:, :, None, :]
    sin = jnp.sin(ang)[:, :, None, :]
    xf = x.astype(jnp.float32)
    rot = jnp.stack([-xf[..., 1::2], xf[..., 0::2]], axis=-1).reshape(xf.shape)
    return xf * cos + rot * sin

def retention(q, k, v, pos):
    b, s, h, dk = q.shape
    dv = v.shape[-1]
    c = RET_CHUNK
    n = s // c
    q = retnet_rotate(q, pos)
    k = retnet_rotate(k, pos) * (dk ** -0.5)
    v = v.astype(jnp.float32)
    to_chunks = lambda t: t.reshape(b, n, c, h, t.shape[-1]).transpose(0, 3, 1, 2, 4)
    qc, kc, vc = to_chunks(q), to_chunks(k), to_chunks(v)
    log_g = jnp.log1p(-jnp.exp2(-5.0 - jnp.arange(h, dtype=jnp.float32)))
    i = jnp.arange(c, dtype=jnp.float32)
    diff = i[:, None] - i[None, :]
    dmat = jnp.where(diff >= 0, jnp.exp(log_g[:, None, None] * jnp.maximum(diff, 0.0)), 0.0)
    scores = jnp.einsum('bhncd,bhnjd->bhncj', qc, kc) * dmat[None, :, None]
    inner = jnp.einsum('bhncj,bhnje->bhnce', scores, vc)
    k_w = jnp.exp(log_g[:, None] * (c - 1 - i))
    kv = jnp.einsum('bhncd,bhnce->bhnde', kc * k_w[None, :, None, :, None], vc)
    chunk_decay = jnp.exp(log_g * c)[None, :, None, None]

    def step(state, kv_n):
        return chunk_decay * state + kv_n, state

    init = jnp.zeros((b, h, dk, dv), kv.dtype)
    _, prev = lax.scan(step, init, jnp.moveaxis(kv, 2, 0))
    prev = jnp.moveaxis(prev, 0, 2)
    q_w = jnp.exp(log_g[:, None] * (i + 1.0))
    cross = jnp.einsum('bhncd,bhnde->bhnce', qc * q_w[None, :, None, :, None], prev)
    out = (inner + cross).transpose(0, 2, 3, 1, 4).reshape(b, s, h, dv)
    out = out * lax.rsqrt(jnp.mean(out * out, axis=-1, keepdims=True) + NORM_EPS)
    return out

def banded_attention(q, k, v, window):
    *lead, L, dh = q.shape
    blk = DIL_BLOCK
    nb = -(-L // blk)
    pad = nb * blk - L
    padw = [(0, 0)] * len(lead) + [(0, pad), (0, 0)]
    qb = jnp.pad(q, padw).reshape(*lead, nb, blk, dh)
    kb = jnp.pad(k, padw).reshape(*lead, nb, blk, dh)
    vb = jnp.pad(v, padw).reshape(*lead, nb, blk, dh)
    shift = lambda t: jnp.concatenate([jnp.zeros_like(t[..., :1, :, :]), t[..., :-1, :, :]], axis=-3)
    kcat = jnp.concatenate([shift(kb), kb], axis=-2)
    vcat = jnp.concatenate([shift(vb), vb], axis=-2)
    s = jnp.einsum('...nqd,...nkd->...nqk', qb, kcat).astype(jnp.float32) * (dh ** -0.5)
    nidx = jnp.arange(nb)[:, None, None]
    qpos = nidx * blk + jnp.arange(blk)[None, :, None]
    kpos = (nidx - 1) * blk + jnp.arange(2 * blk)[None, None, :]
    dist = qpos - kpos
    mask = (dist >= 0) & (dist <= window) & (kpos >= 0)
    s = jnp.where(mask, s, -jnp.inf)
    lse = jax.nn.logsumexp(s, axis=-1, keepdims=True)
    p = jnp.exp(s - lse)
    out = jnp.einsum('...nqk,...nkd->...nqd', p.astype(vcat.dtype), vcat)
    out = out.reshape(*lead, nb * blk, dh)[..., :L, :]
    lse = lse[..., 0].reshape(*lead, nb * blk)[..., :L]
    return out, lse

def dilated_attention(q, k, v):
    b, s, _, dh = q.shape
    hg = DIL_HEADS_PER_GROUP
    outs, lses = [], []
    for g, (w, r) in enumerate(DIL_PATTERNS):
        sl = slice(g * hg, (g + 1) * hg)
        sub = lambda t: t[:, :, sl].reshape(b, s // r, r, hg, dh).transpose(0, 2, 3, 1, 4)
        o, l = banded_attention(sub(q), sub(k), sub(v), w // r)
        outs.append(o.transpose(0, 3, 1, 2, 4).reshape(b, s, hg, dh))
        lses.append(l.transpose(0, 3, 1, 2).reshape(b, s, hg))
    outs = jnp.stack(outs, axis=0)
    wts = jax.nn.softmax(jnp.stack(lses, axis=0), axis=0)
    return jnp.sum(wts[..., None] * outs.astype(jnp.float32), axis=0)

def memory_cross_attention(h, memn, w_q, w_kv, w_o):
    b, s, d = h.shape
    m = memn.shape[1]
    q = (h @ w_q).reshape(b, s, MEM_HEADS, MEM_HEAD_DIM)
    k, v = jnp.split(memn @ w_kv, 2, axis=-1)
    k = k.reshape(b, m, MEM_HEADS, MEM_HEAD_DIM)
    v = v.reshape(b, m, MEM_HEADS, MEM_HEAD_DIM)
    sc = jnp.einsum('bshd,bmhd->bhsm', q, k).astype(jnp.float32) * (MEM_HEAD_DIM ** -0.5)
    p = jax.nn.softmax(sc, axis=-1)
    o = jnp.einsum('bhsm,bmhd->bshd', p.astype(v.dtype), v).reshape(b, s, d)
    return o @ w_o

def peer_ffn(h, w_q, subkeys, u_tab, v_tab):
    b, s, d = h.shape
    t = b * s
    ht = h.reshape(t, d)
    qh = (ht @ w_q).reshape(t, PEER_HEADS, 2, PEER_QUERY_DIM // 2)
    sc = jnp.einsum('thpd,hpnd->thpn', qh, subkeys).astype(jnp.float32)
    v_top, i_top = lax.top_k(sc, PEER_TOPK)
    combo = (v_top[:, :, 0, :, None] + v_top[:, :, 1, None, :]).reshape(t, PEER_HEADS, PEER_TOPK * PEER_TOPK)
    c_val, c_idx = lax.top_k(combo, PEER_TOPK)
    i1 = jnp.take_along_axis(i_top[:, :, 0, :], c_idx // PEER_TOPK, axis=-1)
    i2 = jnp.take_along_axis(i_top[:, :, 1, :], c_idx % PEER_TOPK, axis=-1)
    e_idx = i1 * PEER_N_KEYS + i2
    gates = jax.nn.softmax(c_val, axis=-1)
    nblk = t // PEER_TOKEN_BLOCK
    kk = PEER_HEADS * PEER_TOPK
    xb = ht.reshape(nblk, PEER_TOKEN_BLOCK, d)
    ib = e_idx.reshape(nblk, PEER_TOKEN_BLOCK, kk)
    gb = gates.reshape(nblk, PEER_TOKEN_BLOCK, kk).astype(h.dtype)

    def expert_block(args):
        x_, i_, g_ = args
        u = u_tab[i_]
        a = jax.nn.gelu(jnp.einsum('td,tkd->tk', x_, u), approximate=False)
        return jnp.einsum('tk,tkd->td', a * g_, v_tab[i_])

    return lax.map(expert_block, (xb, ib, gb)).reshape(b, s, d)

def second_inputs(seed: int = 0) -> dict:
    key = jax.random.key(seed)
    ks = jax.random.split(key, 20)
    f32 = jnp.float32
    nrm = lambda k, shape, scale: jax.random.normal(k, shape, f32) * scale
    gain = lambda k, shape: 1.0 + 0.02 * jax.random.normal(k, shape, f32)
    x = nrm(ks[0], (BATCH, SEQ, D_MODEL), 1.0)
    mem = nrm(ks[1], (BATCH, MEM_TOKENS, D_MODEL), 1.0)
    offset = jax.random.randint(ks[2], (BATCH, 1), 0, 4096, dtype=jnp.int32)
    positions = offset + jnp.arange(SEQ, dtype=jnp.int32)[None, :]
    return {
        'x': x,
        'mem': mem,
        'positions': positions,
        'g_mix': gain(ks[3], (DEPTH, D_MODEL)),
        'w_in': nrm(ks[4], (DEPTH, D_MODEL, IN_WIDTH), D_MODEL ** -0.5),
        'w_br_ret': nrm(ks[5], (DEPTH, RET_V_W, D_MODEL), RET_V_W ** -0.5),
        'w_br_dil': nrm(ks[6], (DEPTH, DIL_OUT_W, D_MODEL), DIL_OUT_W ** -0.5),
        'w_out': nrm(ks[7], (DEPTH, D_MODEL, D_MODEL), D_MODEL ** -0.5),
        'g_cross': gain(ks[8], (DEPTH, D_MODEL)),
        'g_mem': gain(ks[9], (DEPTH, D_MODEL)),
        'w_q_mem': nrm(ks[10], (DEPTH, D_MODEL, D_MODEL), D_MODEL ** -0.5),
        'w_kv_mem': nrm(ks[11], (DEPTH, D_MODEL, 2 * D_MODEL), D_MODEL ** -0.5),
        'w_o_mem': nrm(ks[12], (DEPTH, D_MODEL, D_MODEL), D_MODEL ** -0.5),
        'g_ffn': gain(ks[13], (DEPTH, D_MODEL)),
        'w_peer_q': nrm(ks[14], (DEPTH, D_MODEL, PEER_HEADS * PEER_QUERY_DIM), D_MODEL ** -0.5),
        'peer_subkeys': nrm(ks[15], (DEPTH, PEER_HEADS, 2, PEER_N_KEYS, PEER_QUERY_DIM // 2), (PEER_QUERY_DIM // 2) ** -0.5),
        'peer_u': nrm(ks[16], (DEPTH, PEER_N_EXPERTS, D_MODEL), D_MODEL ** -0.5),
        'peer_v': nrm(ks[17], (DEPTH, PEER_N_EXPERTS, D_MODEL), PEER_HEADS ** -0.5),
        'g_final': gain(ks[18], (D_MODEL,)),
    }

def second_block(x, mem, positions, g_mix, w_in, w_br_ret, w_br_dil, w_out, g_cross, g_mem, w_q_mem, w_kv_mem, w_o_mem, g_ffn, w_peer_q, peer_subkeys, peer_u, peer_v, g_final):
    b, s, d = x.shape
    for l in range(DEPTH):
        h = rms_norm(x, g_mix[l])
        proj = h @ w_in[l]
        rq, rk, rv, rg, dq, dk, dv, gate_ret, gate_dil = jnp.split(proj, IN_SPLIT_POINTS, axis=-1)
        ret = retention(rq.reshape(b, s, RET_HEADS, RET_QK_DIM), rk.reshape(b, s, RET_HEADS, RET_QK_DIM),
                        rv.reshape(b, s, RET_HEADS, RET_V_DIM), positions)
        ret = (ret.reshape(b, s, RET_V_W) * jax.nn.silu(rg.astype(jnp.float32))).astype(x.dtype)
        nh = DIL_N_GROUPS * DIL_HEADS_PER_GROUP
        dq = rotary(dq.reshape(b, s, nh, DIL_HEAD_DIM), positions)
        dk = rotary(dk.reshape(b, s, nh, DIL_HEAD_DIM), positions)
        dv = dv.reshape(b, s, nh, DIL_HEAD_DIM)
        dil = dilated_attention(dq, dk, dv).reshape(b, s, DIL_OUT_W).astype(x.dtype)
        merged = jax.nn.sigmoid(gate_ret) * (ret @ w_br_ret[l]) + jax.nn.sigmoid(gate_dil) * (dil @ w_br_dil[l])
        x = x + merged @ w_out[l]
        hc = rms_norm(x, g_cross[l])
        memn = rms_norm(mem, g_mem[l])
        x = x + memory_cross_attention(hc, memn, w_q_mem[l], w_kv_mem[l], w_o_mem[l])
        hf = rms_norm(x, g_ffn[l])
        x = x + peer_ffn(hf, w_peer_q[l], peer_subkeys[l], peer_u[l], peer_v[l])
    return rms_norm(x, g_final)


def setup_inputs(seed=0):
    out = dict(first_inputs(seed))
    for name, value in second_inputs(seed + 1).items():
        if name != "x":
            out[name + "_2"] = value
    return out


def reference(
    x, c, ctx, c_ctx, w_ada, b_ada, norm1_w, w_in, hy_conv_w, hy_conv_b, filt_w1, filt_b1,
    filt_freq, filt_w2, filt_b2, filt_w3, hy_bias, hy_norm_w, ssd_conv_w, ssd_conv_b, dt_bias,
    a_log, ssd_d, ssd_norm_w, w_out, norm2_w, w_mlp1, w_mlp2, final_norm_w, mem_2, positions_2,
    g_mix_2, w_in_2, w_br_ret_2, w_br_dil_2, w_out_2, g_cross_2, g_mem_2, w_q_mem_2, w_kv_mem_2,
    w_o_mem_2, g_ffn_2, w_peer_q_2, peer_subkeys_2, peer_u_2, peer_v_2, g_final_2,
):
    x = first_block(
        x, c, ctx, c_ctx, w_ada, b_ada, norm1_w, w_in, hy_conv_w, hy_conv_b, filt_w1, filt_b1,
        filt_freq, filt_w2, filt_b2, filt_w3, hy_bias, hy_norm_w, ssd_conv_w, ssd_conv_b,
        dt_bias, a_log, ssd_d, ssd_norm_w, w_out, norm2_w, w_mlp1, w_mlp2, final_norm_w,
    )
    return second_block(
        x, mem_2, positions_2, g_mix_2, w_in_2, w_br_ret_2, w_br_dil_2, w_out_2, g_cross_2,
        g_mem_2, w_q_mem_2, w_kv_mem_2, w_o_mem_2, g_ffn_2, w_peer_q_2, peer_subkeys_2,
        peer_u_2, peer_v_2, g_final_2,
    )


_drawn_inputs = setup_inputs


def setup_inputs(seed=0):
    import zlib

    import numpy as np

    out = dict(_drawn_inputs(seed))
    spreads = {}
    factors = {'ctx': 2.759,
     'c_ctx': 2.867,
     'ssd_conv_b': 3.356,
     'ssd_d': 3.361,
     'g_cross_2': 6.11,
     'g_mem_2': 5.886,
     'g_final_2': 7.662,
     'g_ffn_2': 8.0}
    for name, (base, spread) in spreads.items():
        noise = np.random.default_rng([zlib.crc32(name.encode()), seed]).standard_normal(out[name].shape)
        drawn = base * np.exp(spread * noise) if base else spread * noise
        out[name] = jnp.asarray(drawn.astype(out[name].dtype))
    for name, factor in factors.items():
        out[name] = (out[name] * factor).astype(out[name].dtype)
    return out
```

```python
import math
from contextlib import ExitStack

import numpy as np

import concourse.bass as bass
from concourse import mybir

F32 = mybir.dt.float32
F32R = mybir.dt.float32r
I32 = mybir.dt.int32
U32 = mybir.dt.uint32
ALU = mybir.AluOpType
ACT = mybir.ActivationFunctionType
AX = mybir.AxisListType

P = 128
T = 256
D = 2048
KC = D // P
EPS = 1e-6
TWO_PI = 2.0 * math.pi
PI_A = 6.28125
PI_B = 0.0019350051879882812
PI_C = TWO_PI - PI_A - PI_B
PI_IN = 3.1415925

N_ADA = 6 * KC
ADA_G = N_ADA // 4
HYENA = 24
HW = 8
XBC = 12
ZB = 8
GRID_W = 64
HEADS = 16
HD = 64
FILT = 64
FEATS = 33
MLP_H = 64
HID0 = 1
RET_H = 8
DIL_G, DIL_HG = 3, 4
DIL_H = DIL_G * DIL_HG
RET_TILES, DIL_TILES, GATE_TILES = 4 * RET_H, 3 * DIL_H, 2 * KC
MEM_H = 4
PEER_H = 8
TOPK = 16
EXPERT_B = 128
G_HALF = EXPERT_B // 2

COLUMNS = [("b_ada", N_ADA), ("norm1", KC), ("hy_w", 3 * HYENA), ("hy_b", HYENA), ("hy_bias", 2 * HW),
           ("hy_norm", HW), ("ssd_w", 3 * XBC), ("ssd_b", XBC), ("ssd_norm", ZB), ("ssd_d", ZB),
           ("norm2", KC), ("final1", KC), ("mix", KC), ("cross", KC), ("mem", KC), ("ffn", KC), ("final2", KC),
           ("zero", KC), ("angles", 2)]
COL = {}
for _name, _n in COLUMNS:
    COL[_name] = sum(n for _, n in COLUMNS[:len(COL)])
N_COL = sum(n for _, n in COLUMNS)

IDENT, ONES, LE, GE, GT, LT, PERM_RET, PERM_ROT, IOTA = range(9)

STREAM = [("ada", N_ADA), ("xbc", XBC), ("hy", HYENA), ("z", ZB), ("out1", KC), ("mlp", 2 * MLP_H),
          ("ret", RET_TILES), ("dil", DIL_TILES), ("gate", GATE_TILES), ("br_ret", KC // 2), ("br_dil", KC // 4),
          ("out2", KC), ("kv", 2 * KC), ("q", KC), ("o", KC), ("pq", KC), ("peer", 2 * EXPERT_B)]
FIRST = {}
for _name, _n in STREAM:
    FIRST[_name] = sum(n for _, n in STREAM[:len(FIRST)])
N_TILES = sum(n for _, n in STREAM)
RING = 4
SPLIT0 = FIRST["xbc"]


class Steps:

    def __init__(self, eng, sem):
        self.eng, self.sem, self.n = eng, sem, 0

    def did(self, ins):
        ins.then_inc(self.sem, 1)
        self.n = self.n + 1

    def settle(self):
        self.eng.wait_ge(self.sem, self.n)


def build(nc, a, out):
    ctx = ExitStack()

    def sem(name):
        return ctx.enter_context(nc.semaphore(name))

    psum = ctx.enter_context(nc.psum_tensor("psum", [P, 8, 512], F32))
    flat = psum[:].rearrange("p b n -> p (b n)")
    BASE = 16512

    def at(name, shape, kib, dt=F32):
        return nc.alloc_sbuf_tensor_at(name, shape, dt, offset=BASE + int(kib * 1024))

    const = at("const", [P, 9, P], 0)
    cols = at("cols", [P, N_COL], 4.5)
    mod = at("mod", [P, N_ADA, 2], 6.5)
    scales = at("scales", [P, 3, KC], 7.25)
    c_raw = at("c_raw", [P, KC, 2], 7.5)
    c_silu = at("c_silu", [P, KC, 2], 7.75)
    ring = at("ring", [P, RING, KC, P], 8)
    w_hi = at("w_hi", [P, 4, KC // 2, P], 40, F32R)
    w_lo = at("w_lo", [P, 4, KC // 2, P], 56, F32R)
    x = at("x", [P, KC, T], 72)
    h_hi = at("h_hi", [P, KC, T], 88, F32R)
    h_lo = at("h_lo", [P, KC, T], 104, F32R)
    ntmp = at("ntmp", [P, 2, 4, T], 192)
    nrt = at("nrt", [P, T], 200)
    nrstd = at("nrstd", [P, T], 201)
    mod_rows = at("mod_rows", [2, N_ADA * P], 88)
    ctx_raw = at("ctx_raw", [P, KC, T], 176)
    c_hi = at("c_hi", [P, KC, T], 120, F32R)
    c_lo = at("c_lo", [P, KC, T], 136, F32R)
    xbc = at("xbc", [P, XBC, 2, T], 152)
    wdt = at("wdt", [P, KC, 32], 176)
    wdt_hi = at("wdt_hi", [P, KC, 32], 178, F32R)
    wdt_lo = at("wdt_lo", [P, KC, 32], 180, F32R)
    u = at("u", [P, HYENA, T], 120)
    z = at("z", [P, ZB, T], 144)
    xs_nat = at("xs_nat", [P, 4, ZB, P], 88)
    state = at("state", [P, 2, 2, 512], 104)
    cb = at("cb", [P, 2, 768], 112)
    b_nat = at("b_nat", [P, 2, 2, P], 118)
    y_ssd = at("y_ssd", [P, ZB, T], 176)
    xw = at("xw", [P, 2, 512], 184)
    decay = at("decay", [P, 2, 768], 184)
    mix_m = at("mix_m", [P, 2, 512], 190)
    mix_t = at("mix_t", [P, 256], 194)
    c_off = at("c_off", [P, 2, 512], 195)
    off_e = at("off_e", [P, 2, 512], 203)
    y_sq = at("y_sq", [P, ZB, T], 184)
    g_rt = at("g_rt", [P, 2, T], 200)
    g_rstd = at("g_rstd", [P, 2, T], 202)
    dt_w = at("dt_w", [P, 4, 4, 32], 198)
    dt_p = at("dt_p", [P, 4, 32], 200)
    dt_u = at("dt_u", [P, 4, 32], 200.5)
    dt = at("dt", [P, 4, 32], 201)
    da = at("da", [P, 4, 32], 201.5)
    dt_bias = at("dt_bias", [P, 32], 202)
    a_exp = at("a_exp", [P, 32], 202.125)
    a_log = at("a_log", [P, 32], 202.25)
    cs = at("cs", [P, 2, 32], 202.375)
    wd = at("wd", [P, 2, 32], 202.625)

    dft = at("dft", [P, 4, 2, T], 88)
    window = at("window", [P, 2, 1024], 104)
    filt_w3 = at("filt_w3", [FILT, 4096], 72)
    filt = at("filt", [P, 2, 2, 512], 152)
    filt_abs = at("filt_abs", [P, 2, 512], 160)
    filt_sd = at("filt_sd", [P, 2, 2, 512], 164)
    z_nat = at("z_nat", [P, 2, 512], 172)
    k_spec = at("k_spec", [P, 2, 2, 512], 176)
    y_spec = at("y_spec", [P, 2, 2, 512], 184)
    y_part = at("y_part", [P, 2, 1024], 192)
    feats = at("feats", [FEATS, T], 200)
    hdn = at("hdn", [FILT, 2, T], 201)
    sin_a = at("sin_a", [P, T], 203)
    sin_k = at("sin_k", [P, T], 204)
    sin_i = at("sin_i", [P, T], 205, I32)
    filt_w12 = at("filt_w12", [FILT, 2 * FILT], 206)
    filt_cols = at("filt_cols", [FILT, 3], 206.5)
    filt_norm = at("filt_norm", [P, 4], 206.75)
    gn_q = at("gn_q", [P, 8, T], 160)
    gn_r = at("gn_r", [P, 8, T], 152)
    gn_i = at("gn_i", [P, 8, T], 168)
    hid_hi = at("hid_hi", [P, 8, T], 184, F32R)
    hid_lo = at("hid_lo", [P, 8, T], 192, F32R)
    gel = at("gel", [P, 2, T], 203)
    hid = at("hid", [P, 2, T], 205)
    trig = at("trig", [P, 4, T], 176)
    pos_i = at("pos_i", [P, T], 206, I32)
    pos = at("pos", [P, T], 201)
    t_half = at("t_half", [P, T], 202)
    pr = at("pr", [P, RET_TILES, T], 120)
    v_ret = at("v_ret", [P, 2, RET_H, P], 152)
    ret_decay = at("ret_decay", [P, RET_H, T], 160)
    ret_p = at("ret_p", [P, 2, 384], 168)
    rot_a = at("rot_a", [P, 2, T], 171)
    rot_b = at("rot_b", [P, 2, T], 173)
    ret_hi = at("ret_hi", [P, RET_H, T], 184, F32R)
    ret_lo = at("ret_lo", [P, RET_H, T], 192, F32R)
    pd = at("pd", [P, DIL_TILES, T], 120)
    v_dil = at("v_dil", [P, 2, DIL_H, P], 156)
    dil_mask = at("dil_mask", [P, 2, DIL_G, T], 168)
    rot_c = at("rot_c", [P, 2, T], 180)
    rot_d_ = at("rot_d", [P, 2, T], 182)
    dil_s = at("dil_s", [P, DIL_G * T], 200)
    dil_pt = at("dil_pt", [P, 6, P], 203)
    dil_n = at("dil_n", [P, 4], 206)
    dil_hi = at("dil_hi", [P, DIL_HG, T], 152, F32R)
    dil_lo = at("dil_lo", [P, DIL_HG, T], 180, F32R)
    pg = at("pg", [P, GATE_TILES, T], 120)
    mrg = at("mrg", [P, 2, T], 200)
    mem_raw = at("mem_raw", [P, KC, T], 156)
    mem_hi = at("mem_hi", [P, KC, T], 120, F32R)
    mem_lo = at("mem_lo", [P, KC, T], 136, F32R)
    kv = at("kv", [P, 2 * KC, T], 152)
    v_mem = at("v_mem", [P, 2, KC, P], 120)
    q_mem = at("q_mem", [P, KC, T], 136)
    mem_e = at("mem_e", [P, 2, 2, T], 184)
    mem_pt = at("mem_pt", [P, 2, 2, T], 188)
    mem_n = at("mem_n", [P, 2, 4], 206)
    q_peer = at("q_peer", [P, KC, T], 120)
    subkeys = at("subkeys", [P, 16, P], 136)
    psc = at("psc", [P, 16, P], 144)
    psc2 = at("psc2", [P, 16, P], 152)
    combo = at("combo", [P, PEER_H, T], 160)
    combo2 = at("combo2", [P, PEER_H, T], 168)
    pick = at("pick", [P, PEER_H, TOPK, TOPK], 176)
    top_v = at("top_v", [P, 16, TOPK], 184)
    top_u = at("top_u", [P, 16, TOPK], 185, U32)
    top_i = at("top_i", [P, 16, TOPK], 186)
    com_v = at("com_v", [P, PEER_H, TOPK], 187)
    com_u = at("com_u", [P, PEER_H, TOPK], 187.5, U32)
    com_q = at("com_q", [P, 2, PEER_H, TOPK], 188, U32)
    com_f = at("com_f", [P, 2, PEER_H, TOPK], 189)
    chosen = at("chosen", [P, 3, PEER_H, TOPK], 190)
    gate_n = at("gate_n", [P, PEER_H], 191.5)
    tabs = at("tabs", [P, 3, T], 200)
    gates = at("gates", [P, G_HALF, T], 120)
    hot2 = at("hot2", [P, 2, 8, P], 184)
    hot1 = at("hot1", [P, 2, 8, G_HALF], 192)

    landed = [sem(f"landed{s}") for s in range(RING)]
    s_const = sem("const_landed")
    half_done = sem("half_done")
    hi_ready, lo_ready = sem("hi_ready"), sem("lo_ready")
    bank_free, acc_free = sem("bank_free"), sem("acc_free")
    dve_step, act_step = sem("dve_step"), sem("act_step")
    s_csilu, s_mod = sem("c_silu_ready"), sem("mod_ready")
    ada_copied, ada_turned = sem("ada_copied"), sem("ada_turned")
    norm_in = sem("norm_in")
    norm_sq, norm_sum, norm_ms, norm_rt = sem("norm_sq"), sem("norm_sum"), sem("norm_ms"), sem("norm_rt")
    norm_t, norm_hi, norm_lo, plain_done = sem("norm_t"), sem("norm_hi"), sem("norm_lo"), sem("norm_plain")
    s_aux = [sem(f"aux{i}") for i in range(6)]
    s_silu = sem("xbc_silu")
    wdt_split = sem("wdt_split")
    wdt_h = sem("wdt_hi_ready")
    dt_sum, dt_e, dt_nab = sem("dt_sum"), sem("dt_e"), sem("dt_nab")
    dt_ready = sem("dt_ready")
    ssd_tp, ssd_tpc = sem("ssd_tp"), sem("ssd_tp_copied")
    cs_sum, cs_cp, cs_wd, cs_wx = sem("cs_sum"), sem("cs_copied"), sem("state_w_arg"), sem("state_w_exp")
    ssd_xw, ssd_st, ssd_stc = sem("ssd_xw"), sem("ssd_state"), sem("ssd_state_copied")
    ssd_cb, ssd_cbm = sem("ssd_cb"), sem("ssd_cb_masked")
    hd_row, hd_d, hd_e, hd_m, hd_o, hd_y, hd_yc = (sem(n) for n in (
        "head_rows", "head_diff", "head_exp", "head_m", "head_off", "head_y", "head_y_copied"))
    g_z, g_y, g_sq, g_sum, g_ms, g_srt, g_out = (sem(n) for n in (
        "gate_silu", "gate_y", "gate_sq", "gate_sum", "gate_ms", "gate_rt", "gate_out"))
    f_in, f_dense, f_arg, f_sin = sem("filter_in"), sem("filter_dense"), sem("sine_arg"), sem("sine")
    y_f, y_h, y_sd, y_k, y_kc, y_tp, y_zn, y_z, y_y, y_inv, y_new = (sem("hy_" + n) for n in (
        "filter", "windowed", "sum_diff", "spectra", "spectra_copied", "turned", "turned_copied", "z_spectra", "product",
        "inverse", "new_z"))
    gn_in, gn_sq, gn_sum, gn_ms, gn_rt, gn_out = (sem("gn_" + n) for n in ("in", "sq", "sum", "ms", "rt", "out"))
    x_back = sem("x_back")
    hid_ready = sem("hidden_ready")
    t_arg, t_sin, t_ready = sem("trig_arg"), sem("trig_sin"), sem("trig_ready")
    rot_p, rot_d = sem("rotated_half"), sem("rotated")
    v_tp, v_nat_ = sem("v_turned"), sem("v_natural")
    r_sc, r_p, r_o, r_oc = sem("ret_scores"), sem("ret_decayed"), sem("ret_out"), sem("ret_out_copied")
    r_g = sem("ret_gate")
    d_sc, d_mx, d_e, d_p, d_tp, d_pt, d_o, d_hi, d_lo = (sem("dil_" + n) for n in (
        "scores", "max", "exp", "prob", "turned", "prob_turned", "out", "hi", "lo"))
    s_sig = sem("gates_sigmoid")
    merged = sem("merged")
    k_half = sem("keys_done")
    m_tp, m_vn, m_sc, m_mx, m_e, m_p, m_pt_, m_pc, m_o, m_hi, m_lo = (sem("mem_" + n) for n in (
        "v_turned", "v_natural", "scores", "max", "exp", "prob", "turned", "prob_turned", "out", "hi", "lo"))
    p_sc, p_scc, p_cv, p_ge, p_tab, p_tt, p_tabs = (sem("peer_" + n) for n in (
        "scores", "scores_copied", "gate_arg", "gate_exp", "table", "table_turned", "tables"))
    e_oh, e_g, e_gc = sem("one_hot"), sem("gates_made"), sem("gates_copied")
    s_out = sem("out_stored")
    block = ctx.enter_context(nc.Block())

    def col(name, i, n=1):
        return cols[:, COL[name] + i:COL[name] + i + n] if isinstance(i, int) else cols[:, bass.ds(i + COL[name], n)]

    def sq(i):
        return const[:, i, :]

    bank_of, n_bank = {}, 0
    for name, n in STREAM:
        bank_of[name] = n_bank
        n_bank += {"ada": 0, "mlp": n // 2, "peer": n // 2, "br_ret": 2 * n, "br_dil": 4 * n}.get(name, n)
    n_acc = {"mlp": 0, "peer": KC * MLP_H // 8}

    norm_to = {"ctx": (c_hi, c_lo), "mem": (mem_hi, mem_lo)}
    NORMS = ["ctx", "x1", "x2", "f1", "mix", "mem", "cross", "ffn", "f2"]
    NI = {n: i for i, n in enumerate(NORMS)}
    NS = {n: i for i, n in enumerate(n for n in NORMS if n not in ("f1", "f2"))}

    @block.sync
    def _(sp):
        sp.dma_start(const[:], a["const"]).then_inc(s_const, 16)
        sp.dma_start(cols[:], a["cols"]).then_inc(s_const, 16)
        sp.dma_start(c_raw[:], a["c"]).then_inc(s_const, 16)

        def load(g, s):
            tile = a["stream"][bass.ds(g, 1)].rearrange("a p (k n) -> (a p) k n", n=P)
            sp.dma_start(ring[:, s], tile).then_inc(landed[s], 16)

        for s in range(RING):
            load(s, s)
        with sp.Fori(1, SPLIT0 // RING + 1) as i:
            for s in range(RING):
                sp.wait_ge(half_done, i * 8 + (2 * s - 6))
                load(i * RING + s, s)
        with sp.Fori(SPLIT0 // RING + 1, N_TILES // RING) as i:
            for s in range(RING):
                sp.wait_ge(lo_ready, i * 8 + (2 * s - 6 - 2 * SPLIT0))
                load(i * RING + s, s)

        sp.wait_ge(plain_done, 2)
        sp.dma_start(out, x[:]).then_inc(s_out, 16)
        sp.wait_ge(s_out, 16)

    @block.gpsimd
    def _(pool):
        with pool.Fori(0, (N_TILES - SPLIT0) // RING) as i:
            for s in range(RING):
                for h in range(2):
                    pool.wait_ge(hi_ready, i * 8 + (2 * s + h + 1))
                    k = slice(h * KC // 2, (h + 1) * KC // 2)
                    slot = 2 * (s % 2) + h
                    pool.tensor_tensor(w_lo[:, slot], ring[:, s, k], w_hi[:, slot].bitcast(F32),
                                       ALU.subtract).then_inc(lo_ready, 1)

    @block.tensor
    def _(pe):
        def half(g, s, h, start, stop, out_of, hi, lo):
            pe.wait_ge(lo_ready, g * 2 + (h + 1 - 2 * SPLIT0))
            slot = 2 * (s % 2) + h
            for c in range(KC // 2):
                o = out_of(c)
                pe.matmul(o, w_hi[:, slot, c], hi(c), start=start(c), stop=False)
                pe.matmul(o, w_hi[:, slot, c], lo(c), start=False, stop=False)
                m = pe.matmul(o, w_lo[:, slot, c], hi(c), start=False, stop=stop(c))
            m.then_inc(half_done, 1)

        def linear(name, hi, lo):
            g0, n = FIRST[name], dict(STREAM)[name]
            with pe.Fori(0, n // RING) as i:
                for j in range(RING):
                    pe.wait_ge(bank_free, i * RING + (bank_of[name] + j + 1))
                    for h in range(2):
                        half(i * RING + (g0 + j), j, h, lambda c: h == 0 and c == 0,
                             lambda c: h == 1 and c == KC // 2 - 1, lambda c: psum[:, j, 0:T],
                             lambda c: hi[:, h * 8 + c], lambda c: lo[:, h * 8 + c])

        def norm_pe(name, bank=7):
            n = NI[name]
            for q in range(4):
                pe.wait_ge(norm_sq, 4 * n + q + 1)
                for k in range(4):
                    m = pe.matmul(psum[:, bank, 0:T], sq(ONES), ntmp[:, q % 2, k], start=q + k == 0, stop=q + k == 6)
                m.then_inc(norm_sum, 1)

        pe.wait_ge(s_const, 48)
        pe.wait_ge(s_csilu, 1)
        pe.wait_ge(acc_free, 4)
        with pe.Fori(0, ADA_G // 2) as i:
            for b in range(2):
                pe.wait_ge(ada_copied, i * 2 + (b + 1))
                for j in range(RING):
                    pe.wait_ge(landed[j], i * 32 + (16 * b + 16))
                    wide = ring[:, j].rearrange("p k n -> p (k n)")
                    for k in range(4):
                        m = pe.matmul(psum[0:2, 4 + b, :], c_silu[:, 4 * j + k], wide[:, 512 * k:512 * k + 512],
                                      start=j + k == 0, stop=j + k == 6)
                        if k % 2:
                            m.then_inc(half_done, 1)
        pe.wait_ge(ada_copied, 2 + ADA_G)
        for n in range(N_ADA):
            m = pe.transpose(psum[:, 6, 2 * n:2 * n + 2], mod_rows[:, n * P:n * P + P], const[0:2, IDENT, 0:2])
        m.then_inc(ada_turned, 1)

        norm_pe("ctx")
        norm_pe("x1")

        pe.wait_ge(norm_lo, 8)
        with pe.Fori(0, XBC // RING) as i:
            for j in range(RING):
                pe.wait_ge(bank_free, i * RING + (bank_of["xbc"] + j + 1))
                for h in range(2):
                    pe.wait_ge(lo_ready, i * 8 + (2 * j + h + 1))
                    slot = 2 * (j % 2) + h
                    for side, (hi, lo) in enumerate(((h_hi, h_lo), (c_hi, c_lo))):
                        o = psum[:, j, side * T:side * T + T]
                        for c in range(8):
                            k = h * 8 + c
                            pe.matmul(o, w_hi[:, slot, c], hi[:, k], start=(k == 0 and side == 0), stop=False,
                                      skip_group_check=True)
                            pe.matmul(o, w_hi[:, slot, c], lo[:, k], start=False, stop=False, skip_group_check=True)
                            m = pe.matmul(o, w_lo[:, slot, c], hi[:, k], start=False, stop=k == KC - 1,
                                          skip_group_check=True)
                    m.then_inc(half_done, 1)

        pe.wait_ge(wdt_split, 1)
        for tb in range(4):
            hi, lo = ((h_hi, h_lo), (c_hi, c_lo))[tb // 2]
            tok = slice((tb % 2) * P, (tb % 2) * P + P)
            o = psum[:, 5, 32 * tb:32 * tb + 32]
            for k in range(KC):
                pe.matmul(o, hi[:, k, tok], wdt_hi[:, k], start=k == 0, stop=False)
                pe.matmul(o, hi[:, k, tok], wdt_lo[:, k], start=False, stop=False)
                m = pe.matmul(o, lo[:, k, tok], wdt_hi[:, k], start=False, stop=k == KC - 1)
        m.then_inc(dt_sum, 1)

        linear("hy", h_hi, h_lo)
        linear("z", h_hi, h_lo)

        pe.wait_ge(s_silu, 1)
        pe.wait_ge(bank_free, bank_of["out1"] + 4)
        for n in range(8):
            tb, q = n // 2, n % 2
            if n >= 2:
                pe.wait_ge(ssd_tpc, n - 1)
            for k in range(4):
                m = pe.transpose(psum[:, n % 2, k * P:k * P + P],
                                 xbc[:, 4 * q + k, tb // 2, (tb % 2) * P:(tb % 2) * P + P], sq(IDENT))
            m.then_inc(ssd_tp, 1)
        pe.wait_ge(ssd_tpc, 7)
        for g in range(2):
            for tb in range(2):
                m = pe.transpose(psum[:, 0, (2 * g + tb) * P:(2 * g + tb + 1) * P],
                                 xbc[:, 8 + g, 1, tb * P:tb * P + P], sq(IDENT))
        m.then_inc(ssd_tp, 1)
        pe.wait_ge(dt_ready, 1)
        F, B = slice(0, 16), slice(16, 32)
        sums = [
            (0, F, [(LE, 0)]), (32, F, [(ONES, 0), (LE, 1)]), (16, B, [(GE, 0), (ONES, 1)]), (48, B, [(GE, 1)]),
            (64, F, [(GT, 2), (ONES, 3)]), (96, F, [(GT, 3)]), (80, B, [(LT, 2)]), (112, B, [(ONES, 2), (LT, 3)])]
        for c0, d, parts in sums:
            for n, (mat, tb) in enumerate(parts):
                m = pe.matmul(psum[:, 4, c0:c0 + 16], sq(mat), da[:, tb, d], start=n == 0, stop=n == len(parts) - 1)
        m.then_inc(cs_sum, 1)
        pe.wait_ge(ssd_tpc, 9)
        for n in range(4):
            d, g = n // 2, n % 2
            if n >= 2:
                pe.wait_ge(ssd_stc, n - 1)
            for tb in range(2):
                pe.wait_ge(ssd_xw, 2 * n + tb + 1)
                m = pe.matmul(psum[:, 2 + n % 2, :], b_nat[:, g, tb], xw[:, tb, :], start=tb == 0, stop=tb == 1)
                m.then_inc(ssd_st, 1)
        for g in range(2):
            if g:
                pe.wait_ge(ssd_cbm, 4)
            for tb in range(2):
                m = pe.matmul(psum[:, 6, tb * T:tb * T + T], xbc[:, 8 + g, 0, tb * P:tb * P + P], xbc[:, 10 + g, 0, :],
                              start=True, stop=True)
            m.then_inc(ssd_cb, 1)

            def rows(hh):
                if hh >= 2:
                    pe.wait_ge(hd_d, hh - 1)
                    pe.wait_ge(hd_o, hh - 1)
                o = psum[:, hh % 2, :]

                def spread(tb, d):
                    return da[:, tb, 16 * d + hh:16 * d + hh + 1].broadcast_to([P, P])
                pe.matmul(o[:, 0:P], spread(0, 0), sq(LE), start=True, stop=False, skip_group_check=True)
                pe.matmul(o[:, P:T], spread(0, 0), sq(ONES), start=False, stop=False, skip_group_check=True)
                pe.matmul(o[:, P:T], spread(1, 0), sq(LE), start=False, stop=False, skip_group_check=True)
                pe.matmul(o[:, T:T + P], spread(0, 1), sq(GE), start=False, stop=False, skip_group_check=True)
                pe.matmul(o[:, T:T + P], spread(1, 1), sq(ONES), start=False, stop=False, skip_group_check=True)
                pe.matmul(o[:, T + P:], spread(1, 1), sq(GE), start=False, stop=True,
                          skip_group_check=True).then_inc(hd_row, 1)

            for hh in range(8 * g, 8 * g + 8):
                if hh == 0:
                    rows(0)
                if hh + 1 < HEADS:
                    rows(hh + 1)
                if hh == 0:
                    pe.wait_ge(ssd_stc, 4)
                if hh % 2 == 0 and hh >= 4:
                    pe.wait_ge(hd_yc, hh // 2 - 1)
                pe.wait_ge(hd_m, hh + 1)
                o = psum[64 * (hh % 2):64 * (hh % 2) + 64, 4 + (hh // 2) % 2, 0:T]
                blk, off = hh // 2, 64 * (hh % 2)
                ch = slice((hh % 8) * 64, (hh % 8) * 64 + 64)
                for tb in range(2):
                    pe.matmul(o, xs_nat[:, tb, blk, off:off + 64], mix_m[:, hh % 2, tb * T:tb * T + T],
                              start=tb == 0, stop=False)
                for d in range(2):
                    m = pe.matmul(o, state[:, d, g, ch], c_off[:, hh % 2, d * T:d * T + T], start=False, stop=d == 1)
                m.then_inc(hd_y, 1)
        pe.wait_ge(g_sq, 1)
        for g in range(2):
            for k in range(4):
                m = pe.matmul(psum[:, 2, g * T:g * T + T], sq(ONES), y_sq[:, 4 * g + k], start=k == 0, stop=k == 3)
        m.then_inc(g_sum, 1)

        pe.wait_ge(f_in, 96)
        pe.wait_ge(g_out, 1)
        pe.matmul(psum[0:FILT, 0, 0:T], filt_w12[0:FEATS, 0:FILT], feats[:], start=True, stop=True).then_inc(f_dense, 1)
        pe.wait_ge(f_sin, 1)
        pe.matmul(psum[0:FILT, 1, 0:T], filt_w12[:, FILT:], hdn[:, 0], start=True, stop=True).then_inc(f_dense, 1)
        pe.wait_ge(f_sin, 2)
        for n in range(4):
            q, o = n // 2, n % 2
            for tb in range(2):
                for sg in range(2):
                    w0 = o * 2048 + sg * 1024 + q * 512
                    m = pe.matmul(psum[:, 2 * tb + sg, :], hdn[:, 1, tb * P:tb * P + P], filt_w3[:, w0:w0 + 512],
                                  start=True, stop=True)
            m.then_inc(y_f, 1)
            for tb in range(2):
                for j in range(4):
                    m = pe.transpose(psum[:, 4 + tb, j * P:j * P + P], u[:, 4 * q + j, tb * P:tb * P + P], sq(IDENT))
            m.then_inc(y_tp, 1)
            pe.wait_ge(y_sd, n + 1)
            for ri in range(2):
                for fb in range(2):
                    for tb in range(2):
                        pe.matmul(psum[:, 2 * ri + fb, :], dft[:, ri, tb, fb * P:fb * P + P], filt_sd[:, ri, tb],
                                  start=tb == 0, stop=tb == 1)
            for j in range(4):
                for tb in range(2):
                    m = pe.matmul(psum[:, 6, j:j + 1], filt_abs[:, tb, j * P:j * P + P], const[:, ONES, 0:1],
                                  start=tb == 0, stop=tb == 1)
            m.then_inc(y_k, 1)
            pe.wait_ge(y_zn, n + 1)
            pe.wait_ge(y_kc, n + 1)
            for ri in range(2):
                for fb in range(2):
                    for tb in range(2):
                        m = pe.matmul(psum[:, 2 * ri + fb, :], dft[:, ri, tb, fb * P:fb * P + P], z_nat[:, tb],
                                      start=tb == 0, stop=tb == 1)
            m.then_inc(y_z, 1)
            pe.wait_ge(y_y, n + 1)
            for j in range(4):
                for k in range(4):
                    m = pe.matmul(psum[:, 4 + j // 2, (j % 2) * T:(j % 2) * T + T],
                                  y_spec[:, k // 2, k % 2, j * P:j * P + P], dft[:, 2 + k // 2, k % 2],
                                  start=k == 0, stop=k == 3)
            m.then_inc(y_inv, 1)
            pe.wait_ge(y_new, n + 1)

        def group_norm_pe(n):
            pe.wait_ge(gn_sq, n + 1)
            for k in range(8):
                m = pe.matmul(psum[:, k // 2, (k % 2) * T:(k % 2) * T + T], sq(ONES), gn_q[:, k], start=True, stop=True)
            m.then_inc(gn_sum, 1)

        group_norm_pe(0)
        pe.wait_ge(gn_out, 1)
        linear("out1", h_hi, h_lo)
        norm_pe("x2")
        pe.wait_ge(norm_lo, 4 * NS["x2"] + 4)

        def up_down_pe(g0, bank0, acc0, hid0, supers):
            with pe.Fori(0, supers) as i:
                for j in range(8):
                    pe.wait_ge(bank_free, i * 8 + (bank0 + j + 1))
                    for h in range(2):
                        half(i * 16 + (g0 + j), j % RING, h, lambda c: h == 0 and c == 0, lambda c: h == 1 and c == 7,
                             lambda c: psum[:, j % 4, 0:T], lambda c: h_hi[:, h * 8 + c], lambda c: h_lo[:, h * 8 + c])
                for j in range(8):
                    for h in range(2):
                        pe.wait_ge(acc_free, i * 16 + (acc0 + 2 * j + h + 1))

                        def hidden(c):
                            if j == 0 and h == 0:
                                pe.wait_ge(hid_ready, i * 8 + (hid0 + c + 1))
                            return hid_hi[:, c]
                        half(i * 16 + (g0 + 8 + j), j % RING, h, lambda c: c == 0, lambda c: c == 7,
                             lambda c: psum[:, 4 + (2 * j + h) % 4, 0:T], hidden, lambda c: hid_lo[:, c])

        up_down_pe(FIRST["mlp"], bank_of["mlp"], 0, HID0, dict(STREAM)["mlp"] // 16)
        norm_pe("f1")

        norm_pe("mix")
        pe.wait_ge(norm_lo, 4 * NS["mix"] + 4)
        linear("ret", h_hi, h_lo)

        def rotate_pe(src, perm, n0, pairs):
            for n in range(pairs):
                if n >= 2:
                    pe.wait_ge(rot_d, n0 + n - 1)
                pe.matmul(psum[:, n % 2, :], sq(perm), src[:, 2 * n:2 * n + 2].rearrange("p k t -> p (k t)"),
                          start=True, stop=True).then_inc(rot_p, 1)

        def turn_v_pe(src, heads, n0):
            for n in range(heads // 2):
                tb, g = n % 2, n // 2
                if n >= 2:
                    pe.wait_ge(v_nat_, n0 + n - 1)
                for k in range(4):
                    m = pe.transpose(psum[:, 2 + n % 2, k * P:k * P + P], src[:, 4 * g + k, tb * P:tb * P + P], sq(IDENT))
                m.then_inc(v_tp, 1)

        pe.wait_ge(bank_free, 4 + bank_of["dil"])
        rotate_pe(pr[:], PERM_RET, 0, 8)
        turn_v_pe(pr[:, 16:24], 8, 0)
        pe.wait_ge(rot_d, 8)
        pe.wait_ge(v_nat_, 4)
        for h in range(RET_H + 1):
            if h < RET_H:
                if h >= 2:
                    pe.wait_ge(r_p, h - 1)
                o = psum[:, 4 + h % 2, :]
                pe.matmul(o[:, 0:T], pr[:, 8 + h, 0:P], pr[:, h], start=True, stop=True)
                pe.matmul(o[:, T:T + P], pr[:, 8 + h, P:], pr[:, h, P:], start=True, stop=True).then_inc(r_sc, 1)
            if h >= 1:
                e = h - 1
                pe.wait_ge(r_p, e + 1)
                if e >= 2:
                    pe.wait_ge(r_oc, e - 1)
                o = psum[:, 6 + e % 2, :]
                pe.matmul(o[:, 0:T], v_ret[:, 0, e], ret_p[:, e % 2, 0:T], start=True, stop=False, skip_group_check=True)
                pe.matmul(o[:, P:T], v_ret[:, 1, e], ret_p[:, e % 2, T:], start=False, stop=True,
                          skip_group_check=True).then_inc(r_o, 1)
        group_norm_pe(1)
        pe.wait_ge(gn_out, 2)
        linear("dil", h_hi, h_lo)
        pe.wait_ge(bank_free, 4 + bank_of["gate"])
        rotate_pe(pd[:], PERM_ROT, 8, 12)
        turn_v_pe(pd[:, 24:36], 12, 4)
        pe.wait_ge(rot_d, 20)
        pe.wait_ge(v_nat_, 10)
        for m_ in range(2 * DIL_HG):
            h, tb = m_ // 2, m_ % 2
            keys = P * (tb + 1)
            b = 4 + 2 * (m_ % 2)
            if m_ >= 2:
                pe.wait_ge(d_mx, m_ - 1)
            for g in range(DIL_G):
                o = flat[:, 512 * b + T * g:512 * b + T * g + keys]
                m = pe.matmul(o, pd[:, 4 * g + h, tb * P:tb * P + P], pd[:, 12 + 4 * g + h, 0:keys], start=True, stop=True)
            m.then_inc(d_sc, 1)
            pe.wait_ge(d_p, m_ + 1)
            for g in range(DIL_G):
                for s in range(tb + 1):
                    n = g * (tb + 1) + s
                    m = pe.transpose(flat[:, n * P:n * P + P], dil_s[:, T * g + P * s:T * g + P * s + P], sq(IDENT))
            m.then_inc(d_tp, 1)
            pe.wait_ge(d_pt, m_ + 1)
            if tb == 0 and h >= 2:
                pe.wait_ge(d_lo, h - 1)
            last = DIL_G * (tb + 1) - 1
            for n in range(last + 1):
                g, s = n // (tb + 1), n % (tb + 1)
                m = pe.matmul(psum[:, 2 + h % 2, tb * P:tb * P + P], v_dil[:, s, 4 * g + h], dil_pt[:, n],
                              start=n == 0, stop=n == last)
            m.then_inc(d_o, 1)
        pe.wait_ge(d_lo, DIL_HG)
        linear("gate", h_hi, h_lo)
        g0 = FIRST["br_ret"]
        with pe.Fori(0, KC // 2 // RING) as i:
            for j in range(RING):
                for h in range(2):
                    pe.wait_ge(bank_free, i * 8 + (bank_of["br_ret"] + 2 * j + h + 1))
                    half(i * RING + (g0 + j), j, h, lambda c: c == 0, lambda c: c == 7,
                         lambda c: psum[:, (2 * j + h) % 4, 0:T], lambda c: ret_hi[:, c], lambda c: ret_lo[:, c])
        g0 = FIRST["br_dil"]
        for j in range(RING):
            for h in range(2):
                def target(c):
                    if c % 4 == 0:
                        pe.wait_ge(bank_free, bank_of["br_dil"] + 4 * j + 2 * h + c // 4 + 1)
                    return psum[:, 2 * h + c // 4, 0:T]
                half(g0 + j, j, h, lambda c: c % 4 == 0, lambda c: c % 4 == 3, target,
                     lambda c: dil_hi[:, c % 4], lambda c: dil_lo[:, c % 4])
        norm_pe("mem")
        pe.wait_ge(merged, 1)
        linear("out2", h_hi, h_lo)

        pe.wait_ge(norm_lo, 4 * NS["mem"] + 4)

        def linear_part(name, first, n, hi, lo):
            g0 = FIRST[name] + first
            with pe.Fori(0, n // RING) as i:
                for j in range(RING):
                    pe.wait_ge(bank_free, i * RING + (bank_of[name] + first + j + 1))
                    for h in range(2):
                        half(i * RING + (g0 + j), j, h, lambda c: h == 0 and c == 0,
                             lambda c: h == 1 and c == KC // 2 - 1, lambda c: psum[:, j, 0:T],
                             lambda c: hi[:, h * 8 + c], lambda c: lo[:, h * 8 + c])

        linear_part("kv", 0, KC, mem_hi, mem_lo)
        norm_pe("cross")
        linear_part("kv", KC, KC, mem_hi, mem_lo)
        pe.wait_ge(norm_lo, 4 * NS["cross"] + 4)
        linear("q", h_hi, h_lo)
        pe.wait_ge(bank_free, 4 + bank_of["o"])
        for n in range(8):
            mb, g = n % 2, n // 2
            if n >= 2:
                pe.wait_ge(m_vn, n - 1)
            for k in range(4):
                m = pe.transpose(psum[:, n % 2, k * P:k * P + P], kv[:, KC + 4 * g + k, mb * P:mb * P + P], sq(IDENT))
            m.then_inc(m_tp, 1)
        pe.wait_ge(m_vn, 8)

        def mem_scores(h):
            if h >= 2:
                pe.wait_ge(m_e, h - 1)
            for tb in range(2):
                for c in range(4):
                    m = pe.matmul(psum[:, 4 + h % 2, tb * T:tb * T + T], q_mem[:, 4 * h + c, tb * P:tb * P + P],
                                  kv[:, 4 * h + c], start=c == 0, stop=c == 3)
            m.then_inc(m_sc, 1)

        mem_scores(0)
        for h in range(MEM_H):
            if h + 1 < MEM_H:
                mem_scores(h + 1)
            pe.wait_ge(m_p, h + 1)
            if h >= 2:
                pe.wait_ge(m_pc, h - 1)
            for mb in range(2):
                for tb in range(2):
                    m = pe.transpose(psum[:, h % 2, mb * T + tb * P:mb * T + tb * P + P],
                                     mem_e[:, h % 2, tb, mb * P:mb * P + P], sq(IDENT))
            m.then_inc(m_pt_, 1)
            pe.wait_ge(m_pc, h + 1)
            if h >= 1:
                pe.wait_ge(m_lo, h)
            for c in range(4):
                for mb in range(2):
                    m = pe.matmul(psum[:, 2 + c // 2, (c % 2) * T:(c % 2) * T + T], v_mem[:, mb, 4 * h + c],
                                  mem_pt[:, h % 2, mb], start=mb == 0, stop=mb == 1)
            m.then_inc(m_o, 1)
        pe.wait_ge(m_lo, MEM_H)
        linear("o", h_hi, h_lo)

        norm_pe("ffn")
        pe.wait_ge(norm_lo, 4 * NS["ffn"] + 4)
        linear("pq", h_hi, h_lo)
        pe.wait_ge(s_aux[5], 16)
        pe.wait_ge(bank_free, 4 + bank_of["peer"])
        for tb in range(2):
            for k in range(16):
                m = pe.matmul(psum[:, 4 * tb + k // 4, (k % 4) * P:(k % 4) * P + P], q_peer[:, k, tb * P:tb * P + P],
                              subkeys[:, k], start=True, stop=True)
            m.then_inc(p_sc, 1)
        for tb in range(2):
            pe.wait_ge(p_tab, tb + 1)
            if tb:
                pe.wait_ge(p_tabs, 1)
            for k in range(3):
                m = pe.transpose(psum[:, 0, k * P:k * P + P], chosen[:, k].rearrange("p h r -> p (h r)"), sq(IDENT))
            m.then_inc(p_tt, 1)
        pe.wait_ge(p_tabs, 2)

        def spread_gates_pe(f):
            with pe.Fori(0, T // 16) as i:
                for b in range(2):
                    pe.wait_ge(e_oh, i * 2 + (32 * f + b + 1))
                    pe.wait_ge(e_gc, i * 2 + (32 * f + b + 1))
                    for t in range(8):
                        m = pe.matmul(psum[:, 4 + b, G_HALF * t:G_HALF * t + G_HALF], hot2[:, b, t], hot1[:, b, t],
                                      start=True, stop=True)
                    m.then_inc(e_g, 1)

        for f in range(2):
            spread_gates_pe(f)
            up_down_pe(FIRST["peer"] + EXPERT_B * f, bank_of["peer"] + G_HALF * f, n_acc["peer"] + 128 * f,
                       HID0 + MLP_H + G_HALF * f, G_HALF // 8)
        norm_pe("f2")

    @block.scalar
    def _(act):
        st = Steps(act, act_step)

        def split_half(g, s, h):
            act.wait_ge(half_done, g * 2 + (h - 3))
            k = slice(h * KC // 2, (h + 1) * KC // 2)
            act.activation(w_hi[:, 2 * (s % 2) + h], ring[:, s, k], ACT.Copy).then_inc(hi_ready, 1)

        def split_tile(g, turn, s):
            act.wait_ge(landed[s], turn * 16 + 16)
            split_half(g, s, 0)
            split_half(g, s, 1)

        def split_stage(name):
            g0, n = FIRST[name], dict(STREAM)[name]
            with act.Fori(0, n // RING) as i:
                for s in range(RING):
                    split_tile(i * RING + (g0 + s), i + g0 // RING, s)

        def norm_act(name, src, shift=None, split=True):
            n = NI[name]
            if shift is None:
                shift = lambda k: col("zero", k)
            for q in range(4):
                if q >= 2:
                    act.wait_ge(norm_sum, 4 * n + q - 1)
                act.activation(ntmp[:, q % 2], src[:, 4 * q:4 * q + 4], ACT.Square).then_inc(norm_sq, 1)
            act.wait_ge(norm_ms, n + 1)
            act.activation(nrt[:], nrt[:], ACT.Sqrt).then_inc(norm_rt, 1)
            if not split:
                return
            for q in range(4):
                act.wait_ge(norm_t, 4 * NS[name] + q + 1)
                for k in range(4):
                    m = act.activation(norm_to.get(name, (h_hi, h_lo))[0][:, 4 * q + k], ntmp[:, q % 2, k], ACT.Identity,
                                       bias=shift(4 * q + k))
                m.then_inc(norm_hi, 1)

        act.dma_start(ctx_raw[:], a["ctx"]).then_inc(norm_in, 16)
        act.dma_start(x[:], a["x"]).then_inc(norm_in, 16)
        act.dma_start(dt_bias[:], a["dt_bias"]).then_inc(s_aux[0], 16)
        act.dma_start(a_log[:], a["a_log"]).then_inc(s_aux[0], 16)
        act.wait_ge(s_const, 48)
        act.activation(c_silu[:], c_raw[:], ACT.Silu).then_inc(s_csilu, 1)
        act.wait_ge(s_aux[0], 32)
        act.activation(a_exp[:], a_log[:], ACT.Exp).then_inc(act_step, 1)
        st.n = 1
        act.wait_ge(norm_in, 32)
        act.wait_ge(s_mod, 1)
        norm_act("ctx", ctx_raw, lambda k: mod[:, k, 1:2])
        act.wait_ge(norm_lo, 4 * NS["ctx"] + 4)
        norm_act("x1", x, lambda k: mod[:, k, 0:1])
        act.wait_ge(norm_lo, 4 * NS["x1"] + 4)
        act.dma_start(wdt[:], a["wdt"]).then_inc(s_aux[1], 16)
        split_stage("xbc")
        act.wait_ge(s_aux[1], 16)
        act.activation(wdt_hi[:], wdt[:], ACT.Copy).then_inc(wdt_h, 1)
        split_stage("hy")
        split_stage("z")
        act.wait_ge(bank_free, 4 + bank_of["hy"])
        act.activation(xbc[:], xbc[:], ACT.Silu).then_inc(s_silu, 1)
        act.wait_ge(dt_nab, 1)
        act.activation(dt_w[:, 1], dt_w[:, 1], ACT.Exp).then_inc(dt_e, 1)
        act.wait_ge(cs_wd, 1)
        act.activation(wd[:], wd[:], ACT.Exp).then_inc(cs_wx, 1)
        for hh in range(HEADS):
            act.wait_ge(hd_d, hh + 1)
            act.activation(decay[:, hh % 2], decay[:, hh % 2], ACT.Exp).then_inc(act_step, 1)
            if hh >= 2:
                act.wait_ge(hd_m, hh - 1)
            act.activation(off_e[:, hh % 2], psum[:, hh % 2, :], ACT.Exp).then_inc(hd_o, 1)
            st.n += 1
        act.activation(z[:], z[:], ACT.Silu).then_inc(g_z, 1)
        act.wait_ge(g_y, 1)
        act.activation(y_sq[:], y_ssd[:], ACT.Square).then_inc(g_sq, 1)
        act.wait_ge(g_ms, 1)
        act.activation(g_rt[:], g_rt[:], ACT.Sqrt).then_inc(g_srt, 1)

        act.wait_ge(g_out, 1)
        act.dma_start(filt_w12[0:FEATS, 0:FILT], a["filt_w1"]).then_inc(f_in, 16)
        act.dma_start(filt_w12[:, FILT:], a["filt_w2"]).then_inc(f_in, 16)
        act.dma_start(filt_cols[:], a["filt_cols"]).then_inc(f_in, 16)
        act.dma_start(feats[:], a["feats"]).then_inc(f_in, 16)
        act.dma_start(filt_w3[:], a["filt_w3"]).then_inc(f_in, 16)
        act.dma_start(dft[:], a["dft"]).then_inc(f_in, 16)
        act.dma_start(window[:], a["window"]).then_inc(s_aux[2], 16)
        for n in range(2):
            act.wait_ge(f_arg, n + 1)
            act.activation(hdn[:, n], sin_a[0:FILT], ACT.Sin).then_inc(f_sin, 1)
        for n in range(4):
            act.wait_ge(y_k, n + 1)
            act.activation(k_spec[:].rearrange("p r f c -> p (r f c)"), flat[:, 0:2048], ACT.Copy).then_inc(y_kc, 1)

        def group_norm_act(n, src):
            act.wait_ge(gn_in, n + 1)
            act.activation(gn_q[:], src, ACT.Square).then_inc(gn_sq, 1)
            act.wait_ge(gn_ms, n + 1)
            act.activation(gn_r[:], gn_r[:], ACT.Sqrt).then_inc(gn_rt, 1)

        group_norm_act(0, u[:, 0:8])
        act.dma_start(x[:], a["x"]).then_inc(x_back, 16)
        split_stage("out1")
        act.wait_ge(bank_free, 4 + bank_of["mlp"])
        norm_act("x2", x, lambda k: mod[:, 3 * KC + k, 0:1])

        def up_down_act(g0, bank0, hid0, supers, gelu):
            with act.Fori(0, supers) as i:
                for j in range(16):
                    split_tile(i * 16 + (g0 + j), i * 4 + (g0 + j) // 4, j % RING)
                    if gelu and 2 <= j < 10:
                        act.wait_ge(half_done, i * 32 + (2 * (g0 + j - 2) + 2))
                        act.wait_ge(hid_ready, i * 8 + (hid0 + j - 3))
                        act.activation(gel[:, j % 2], psum[:, (j - 2) % 4, 0:T], ACT.Gelu).then_inc(bank_free, 1)

        up_down_act(FIRST["mlp"], bank_of["mlp"], HID0, dict(STREAM)["mlp"] // 16, False)
        act.wait_ge(acc_free, 4 + n_acc["peer"])
        norm_act("f1", x, split=False)

        act.dma_start(ret_decay[:], a["ret_decay"]).then_inc(s_aux[3], 16)
        act.wait_ge(plain_done, 1)
        act.dma_start(pos_i[:], a["pos"]).then_inc(s_aux[4], 16)
        norm_act("mix", x)
        for n in range(2):
            act.wait_ge(t_arg, n + 1)
            act.activation(trig[:, 2 * n], sin_a[:], ACT.Sin)
            act.activation(t_half[:], sin_a[:], ACT.Sin, scale=0.5).then_inc(t_sin, 1)
        split_stage("ret")
        act.wait_ge(bank_free, 4 + bank_of["dil"])
        act.activation(pr[:, 24:32], pr[:, 24:32], ACT.Silu).then_inc(r_g, 1)
        for h in range(RET_H):
            act.wait_ge(r_o, h + 1)
            act.activation(pr[:, h], psum[:, 6 + h % 2, 0:T], ACT.Copy).then_inc(r_oc, 1)
        act.wait_ge(r_oc, RET_H)
        act.activation(gn_q[:], pr[:, 0:8], ACT.Square).then_inc(gn_sq, 1)
        act.wait_ge(gn_ms, 2)
        act.activation(gn_r[:], gn_r[:], ACT.Sqrt).then_inc(gn_rt, 1)
        act.wait_ge(gn_out, 2)
        act.dma_start(dil_mask[:], a["dil_mask"]).then_inc(s_aux[3], 16)
        split_stage("dil")
        for m_ in range(2 * DIL_HG):
            h, tb = m_ // 2, m_ % 2
            keys = P * (tb + 1)
            act.wait_ge(d_mx, m_ + 1)
            s = dil_s[:].rearrange("p (g k) -> p g k", g=DIL_G)[:, :, 0:keys]
            act.activation(s, s, ACT.Exp, bias=dil_n[:, 0:1], accum_out=dil_n[:, 1:2]).then_inc(d_e, 1)
            if tb == 1:
                act.wait_ge(d_o, m_ + 1)
                act.activation(dil_hi[:, h], psum[:, 2 + h % 2, 0:T], ACT.Copy).then_inc(d_hi, 1)
        act.wait_ge(d_lo, DIL_HG)
        act.dma_start(mem_raw[:], a["mem"]).then_inc(norm_in, 16)
        split_stage("gate")
        act.wait_ge(bank_free, 4 + bank_of["br_ret"])
        act.activation(pg[:], pg[:], ACT.Sigmoid).then_inc(s_sig, 1)
        split_stage("br_ret")
        split_stage("br_dil")
        act.wait_ge(norm_in, 48)
        act.wait_ge(half_done, 2 * FIRST["br_dil"])
        norm_act("mem", mem_raw)
        split_stage("out2")

        def split_part(name, first, n):
            g0 = FIRST[name] + first
            with act.Fori(0, n // RING) as i:
                for s in range(RING):
                    split_tile(i * RING + (g0 + s), i + g0 // RING, s)

        split_part("kv", 0, KC)
        act.wait_ge(bank_free, 4 + bank_of["kv"])
        norm_act("cross", x)
        split_part("kv", KC, KC)
        split_stage("q")
        for h in range(MEM_H):
            act.wait_ge(m_mx, h + 1)
            for tb in range(2):
                m = act.activation(mem_e[:, h % 2, tb], psum[:, 4 + h % 2, tb * T:tb * T + T], ACT.Exp,
                                   bias=mem_n[:, h % 2, tb:tb + 1], scale=(D // MEM_H) ** -0.5,
                                   accum_out=mem_n[:, h % 2, 2 + tb:3 + tb])
            m.then_inc(m_e, 1)
            act.wait_ge(m_o, h + 1)
            act.activation(h_hi[:, 4 * h:4 * h + 4].rearrange("p k t -> p (k t)"), flat[:, 1024:2048],
                           ACT.Copy).then_inc(m_hi, 1)
        act.wait_ge(m_lo, MEM_H)
        act.dma_start(subkeys[:], a["subkeys"]).then_inc(s_aux[5], 16)
        split_stage("o")
        act.wait_ge(bank_free, 4 + bank_of["pq"])
        norm_act("ffn", x)
        split_stage("pq")
        for tb in range(2):
            act.wait_ge(p_sc, tb + 1)
            if tb:
                act.wait_ge(p_tab, tb)
            act.activation(psc[:].rearrange("p k n -> p (k n)"), flat[:, 2048 * tb:2048 * tb + 2048],
                           ACT.Copy).then_inc(p_scc, 1)
            act.wait_ge(p_cv, tb + 1)
            act.activation(chosen[:, 2], chosen[:, 2], ACT.Exp).then_inc(p_ge, 1)
        for f in range(2):
            if f:
                act.wait_ge(hid_ready, HID0 + MLP_H + G_HALF)
            else:
                act.wait_ge(p_tabs, 2)
            with act.Fori(0, T // 16) as i:
                for b in range(2):
                    act.wait_ge(e_g, i * 2 + (32 * f + b + 1))
                    to = gates[:, :, bass.ds(i * 16 + 8 * b, 8)].rearrange("p e t -> p t e")
                    act.activation(to, psum[:, 4 + b, :].rearrange("p (t e) -> p t e", t=8), ACT.Copy).then_inc(e_gc, 1)
            up_down_act(FIRST["peer"] + EXPERT_B * f, bank_of["peer"] + G_HALF * f, HID0 + MLP_H + G_HALF * f,
                        G_HALF // 8, True)
        act.wait_ge(acc_free, 4 + n_acc["peer"] + 256)
        norm_act("f2", x, split=False)

    @block.vector
    def _(dve):
        st = Steps(dve, dve_step)

        def norm_dve(name, src, scale, shift=None, plain=None):
            n = NI[name]
            if shift is None:
                shift = lambda k: col("zero", k)
            hi, lo = norm_to.get(name, (h_hi, h_lo))
            dve.wait_ge(norm_sum, 4 * n + 4)
            dve.tensor_scalar(nrt[:], psum[:, 7, 0:T], 1.0 / D, EPS, ALU.mult, ALU.add).then_inc(norm_ms, 1)
            dve.wait_ge(norm_rt, n + 1)
            st.did(dve.reciprocal(nrstd[:], nrt[:]))
            st.settle()
            if plain is not None:
                for k in range(KC):
                    m = dve.scalar_tensor_tensor(plain[:, k], src[:, k], scale(k), nrstd[:], ALU.mult, ALU.mult)
                m.then_inc(plain_done, 1)
                return

            def low(q):
                dve.wait_ge(norm_hi, 4 * NS[name] + q + 1)
                for k in range(4):
                    m = dve.scalar_tensor_tensor(lo[:, 4 * q + k], ntmp[:, q % 2, k], shift(4 * q + k),
                                                 hi[:, 4 * q + k].bitcast(F32), ALU.add, ALU.subtract)
                m.then_inc(norm_lo, 1)

            for q in range(4):
                if q >= 2:
                    low(q - 2)
                    dve.wait_ge(norm_lo, 4 * NS[name] + q - 1)
                for k in range(4):
                    m = dve.scalar_tensor_tensor(ntmp[:, q % 2, k], src[:, 4 * q + k], scale(4 * q + k), nrstd[:],
                                                 ALU.mult, ALU.mult)
                m.then_inc(norm_t, 1)
            low(2)
            low(3)

        def copy_stage(name, dst, d0=0):
            g0, n = FIRST[name], dict(STREAM)[name]
            with dve.Fori(0, n // RING) as i:
                for j in range(RING):
                    dve.wait_ge(half_done, i * 8 + (2 * (g0 + j) + 2))
                    dve.tensor_copy(dst[:, bass.ds(i * RING + (d0 + j), 1)].rearrange("p a t -> p (a t)"),
                                    psum[:, j, 0:T]).then_inc(bank_free, 1)

        def copy_part(name, dst, first, n):
            g0 = FIRST[name] + first
            with dve.Fori(0, n // RING) as i:
                for j in range(RING):
                    dve.wait_ge(half_done, i * 8 + (2 * (g0 + j) + 2))
                    dve.tensor_copy(dst[:, bass.ds(i * RING + (first + j), 1)].rearrange("p a t -> p (a t)"),
                                    psum[:, j, 0:T]).then_inc(bank_free, 1)

        def conv_tile(i, j, g, dst, w, b, nb, both):
            k = i * RING + j
            dve.wait_ge(half_done, i * 8 + (2 * (g + j) + 2))
            width = 2 * T if both else T
            src = psum[:, j, 0:width]
            n0 = k * (4 if both else 2) + conv_base[0]
            dve.tensor_scalar(dst, src, col(w, k + nb), col(b, k), ALU.mult, ALU.add).then_inc(dve_step, 1)
            pieces = [(dst[:, 0:T].rearrange("p (r w) -> p r w", w=GRID_W),
                       src[:, 0:T].rearrange("p (r w) -> p r w", w=GRID_W), GRID_W)]
            if both:
                pieces.append((dst[:, T:].rearrange("p (r w) -> p r w", w=T),
                               src[:, T:].rearrange("p (r w) -> p r w", w=T), T))
            step = 1
            for out_, in_, w_ in pieces:
                for tap in (0, 2):
                    dve.wait_ge(dve_step, n0 + step)
                    o, s = ((out_[:, :, 1:w_], in_[:, :, 0:w_ - 1]), None, (out_[:, :, 0:w_ - 1], in_[:, :, 1:w_]))[tap]
                    last = tap == 2 and w_ == pieces[-1][2]
                    dve.scalar_tensor_tensor(o, s, col(w, k + tap * nb), o, ALU.mult, ALU.add).then_inc(
                        bank_free if last else dve_step, 1)
                    step += 1

        conv_base = [0]
        def pair_out(j):
            dve.wait_ge(hd_y, 2 * j + 2)
            dve.scalar_tensor_tensor(y_ssd[:, j], xbc[:, j, 0], col("ssd_d", j), psum[:, 4 + j % 2, 0:T],
                                     ALU.mult, ALU.add).then_inc(hd_yc, 1)

        for b in range(8):
            dve.memset(psum[:, b, :], 0.0).then_inc(bank_free if b < 4 else acc_free, 1)
        dve.memset(hid[:], 0.0).then_inc(hid_ready, HID0)
        dve.wait_ge(acc_free, 4)
        for b in range(2):
            dve.memset(psum[:, 4 + b, :], 0.0).then_inc(ada_copied, 1)
        dve.wait_ge(s_const, 48)
        with dve.Fori(0, ADA_G // 2) as i:
            for b in range(2):
                dve.wait_ge(half_done, i * 16 + (8 * b + 8))
                dve.tensor_copy(mod_rows[:, bass.ds(i * 1024 + 512 * b, 512)], psum[0:2, 4 + b, :]).then_inc(ada_copied, 1)
        dve.wait_ge(ada_turned, 1)
        dve.tensor_tensor(mod[:], psum[:, 6, 0:2 * N_ADA].rearrange("p (n c) -> p n c", c=2),
                          col("b_ada", 0, N_ADA).unsqueeze(2).broadcast_to([P, N_ADA, 2]), ALU.add).then_inc(s_mod, 1)
        dve.wait_ge(s_mod, 1)
        for n, (w, at_, side) in enumerate((("norm1", KC, 0), ("norm1", KC, 1), ("norm2", 4 * KC, 0))):
            st.did(dve.scalar_tensor_tensor(scales[:, n], mod[:, at_:at_ + KC, side], 1.0, col(w, 0, KC),
                                            ALU.add, ALU.mult))
        st.settle()
        norm_dve("ctx", ctx_raw, lambda k: scales[:, 1, k:k + 1], lambda k: mod[:, k, 1:2])
        norm_dve("x1", x, lambda k: scales[:, 0, k:k + 1], lambda k: mod[:, k, 0:1])

        conv_base[0] = st.n
        with dve.Fori(0, XBC // RING) as i:
            for j in range(RING):
                conv_tile(i, j, FIRST["xbc"], xbc[:, bass.ds(i * RING + j, 1)].rearrange("p a s t -> p (a s t)"),
                          "ssd_w", "ssd_b", XBC, True)
        st.n += 4 * XBC
        dve.wait_ge(wdt_h, 1)
        dve.tensor_tensor(wdt_lo[:], wdt[:], wdt_hi[:].bitcast(F32), ALU.subtract).then_inc(wdt_split, 1)
        dve.wait_ge(dt_sum, 1)
        conv_base[0] = st.n
        with dve.Fori(0, HYENA // RING) as i:
            for j in range(RING):
                conv_tile(i, j, FIRST["hy"], u[:, bass.ds(i * RING + j, 1)].rearrange("p a t -> p (a t)"),
                          "hy_w", "hy_b", HYENA, False)
        st.n += 2 * HYENA
        copy_stage("z", z)

        v, e, w2, w3 = (dt_w[:, n] for n in range(4))
        st.did(dve.tensor_tensor(v, psum[:, 5, 0:P].rearrange("p (b h) -> p b h", h=32),
                                 dt_bias[:].unsqueeze(1).broadcast_to([P, 4, 32]), ALU.add))
        st.settle()
        dve.scalar_tensor_tensor(e, v, -1.0, v, ALU.mult, ALU.min).then_inc(dt_nab, 1)
        dve.wait_ge(dt_e, 1)
        st.did(dve.tensor_scalar(w2, e, 2.0, None, ALU.add))
        st.settle()
        st.did(dve.reciprocal(w3, w2))
        st.settle()
        st.did(dve.tensor_tensor(dt_u[:], e, w3, ALU.mult))
        st.settle()
        st.did(dve.tensor_tensor(w2, dt_u[:], dt_u[:], ALU.mult))
        st.settle()
        st.did(dve.tensor_scalar(dt_p[:], w2, 1.0 / 17, None, ALU.mult))
        for k in (15, 13, 11, 9, 7, 5, 3):
            st.settle()
            st.did(dve.scalar_tensor_tensor(dt_p[:], dt_p[:], 1.0 / k, w2, ALU.add, ALU.mult))
        st.settle()
        st.did(dve.scalar_tensor_tensor(dt_p[:], dt_p[:], 1.0, dt_u[:], ALU.add, ALU.mult))
        st.did(dve.tensor_scalar(v, v, 0.0, None, ALU.max))
        st.settle()
        st.did(dve.scalar_tensor_tensor(dt[:], dt_p[:], 2.0, v, ALU.mult, ALU.add))
        st.settle()
        dve.wait_ge(act_step, 1)
        dve.scalar_tensor_tensor(da[:], dt[:], -1.0, a_exp[:].unsqueeze(1).broadcast_to([P, 4, 32]),
                                 ALU.mult, ALU.mult).then_inc(dt_ready, 1)
        for n in range(8):
            tb, q = n // 2, n % 2
            dve.wait_ge(ssd_tp, n + 1)
            dve.tensor_copy(xs_nat[:, tb, 4 * q:4 * q + 4].rearrange("p k c -> p (k c)"),
                            psum[:, n % 2, :]).then_inc(ssd_tpc, 1)
        dve.wait_ge(ssd_tp, 9)
        dve.tensor_copy(b_nat[:].rearrange("p g b c -> p (g b c)"), psum[:, 0, :]).then_inc(ssd_tpc, 1)
        dve.wait_ge(cs_sum, 1)
        st.did(dve.tensor_copy(cs[:].rearrange("p b h -> p (b h)"), psum[:, 4, 0:64]))
        dve.tensor_copy(wd[:].rearrange("p b h -> p (b h)"), psum[:, 4, 64:128]).then_inc(cs_wd, 1)
        dve.wait_ge(cs_wx, 1)
        st.did(dve.tensor_tensor(wd[:], wd[:], dt[:, 2:4], ALU.mult))
        dve.wait_ge(ssd_tpc, 9)
        st.settle()
        for n in range(4):
            d, g = n // 2, n % 2
            for tb in range(2):
                if n >= 1:
                    dve.wait_ge(ssd_st, 2 * (n - 1) + tb + 1)
                hs = 16 * d + 8 * g
                dve.tensor_tensor(
                    xw[:, tb].rearrange("p (h c) -> p h c", c=HD),
                    xs_nat[:, 2 + tb, 4 * g:4 * g + 4].rearrange("p k c -> p (k c)").rearrange("p (h c) -> p h c", c=HD),
                    wd[:, tb, hs:hs + 8].unsqueeze(2).broadcast_to([P, 8, HD]), ALU.mult).then_inc(ssd_xw, 1)
            dve.wait_ge(ssd_st, 2 * n + 2)
            dve.tensor_copy(state[:, d, g], psum[:, 2 + n % 2, :]).then_inc(ssd_stc, 1)
        for g in range(2):
            dve.wait_ge(ssd_cb, g + 1)
            c_ = cb[:, g]
            p6 = psum[:, 6, :]
            dve.tensor_copy(c_[:, P:T], p6[:, P:T])
            dve.tensor_copy(c_[:, T + P:T + P + P], p6[:, T:T + P])
            for o, s, mask in ((0, 0, LE), (T, T + P, LE), (T + P + P, T + P, GE), (T + P + T, 0, GE)):
                dve.tensor_tensor(c_[:, o:o + P], p6[:, s:s + P], sq(mask), ALU.mult).then_inc(ssd_cbm, 1)
            dve.wait_ge(ssd_cbm, 4 * g + 4)
            for hh in range(8 * g, 8 * g + 8):
                dve.wait_ge(hd_row, hh + 1)
                rw = psum[:, hh % 2, :]
                dc, mm = decay[:, hh % 2], mix_m[:, hh % 2]
                f, b = hh, 16 + hh
                if hh >= 2:
                    dve.wait_ge(hd_y, hh - 1)
                for n, (o, r, wdt_, tb, c0) in enumerate(((0, 0, T, 0, f), (T, P, P, 1, f), (T + P, T, T, 1, b),
                                                          (2 * T + P, T, P, 0, b))):
                    m = dve.tensor_scalar(dc[:, o:o + wdt_], rw[:, r:r + wdt_], cs[:, tb, c0:c0 + 1], 0.0,
                                          ALU.subtract, ALU.min)
                m.then_inc(hd_d, 1)
                dve.wait_ge(hd_o, hh + 1)
                for o, wdt_, tb, c0, dst in ((0, T, 0, f, mm[:, 0:T]), (T + P, T, 1, b, mm[:, T:]),
                                             (T, P, 1, f, mix_t[:, 0:P]), (2 * T + P, P, 0, b, mix_t[:, P:])):
                    st.did(dve.scalar_tensor_tensor(dst, dc[:, o:o + wdt_], dt[:, tb, c0:c0 + 1], c_[:, o:o + wdt_],
                                                    ALU.mult, ALU.mult))
                st.did(dve.tensor_tensor(c_off[:, hh % 2].rearrange("p (d t) -> p d t", t=T),
                                         off_e[:, hh % 2].rearrange("p (d t) -> p d t", t=T),
                                         xbc[:, 10 + g, 0, :].unsqueeze(1).broadcast_to([P, 2, T]), ALU.mult))
                st.settle()
                st.did(dve.tensor_tensor(mm[:, T + P:], mm[:, T + P:], mix_t[:, 0:P], ALU.add))
                dve.tensor_tensor(mm[:, 0:P], mm[:, 0:P], mix_t[:, P:], ALU.add).then_inc(hd_m, 1)
                if hh % 2 == 1 and hh >= 3:
                    pair_out(hh // 2 - 1)
        pair_out(7)
        dve.wait_ge(hd_yc, 8)
        dve.wait_ge(g_z, 1)
        dve.tensor_tensor(y_ssd[:], y_ssd[:], z[:], ALU.mult).then_inc(g_y, 1)
        dve.wait_ge(g_sum, 1)
        dve.tensor_scalar(g_rt[:].rearrange("p g t -> p (g t)"), psum[:, 2, :], 1.0 / 512, EPS, ALU.mult,
                          ALU.add).then_inc(g_ms, 1)
        dve.wait_ge(g_srt, 1)
        st.did(dve.reciprocal(g_rstd[:], g_rt[:]))
        st.settle()
        for k in range(ZB):
            st.did(dve.scalar_tensor_tensor(y_ssd[:, k], y_ssd[:, k], col("ssd_norm", k), g_rstd[:, k // 4],
                                            ALU.mult, ALU.mult))
        st.settle()
        st.did(dve.tensor_copy(h_hi[:, 8:16], y_ssd[:]))
        st.settle()
        dve.tensor_tensor(h_lo[:, 8:16], y_ssd[:], h_hi[:, 8:16].bitcast(F32), ALU.subtract).then_inc(g_out, 1)

        def reduce_angle(rows, signal=f_arg):
            r, k, ki = sin_a[0:rows], sin_k[0:rows], sin_i[0:rows]
            st.settle()
            st.did(dve.tensor_scalar(k, r, 1.0 / TWO_PI, None, ALU.mult))
            st.settle()
            st.did(dve.tensor_copy(ki, k))
            st.settle()
            st.did(dve.tensor_copy(k, ki))
            for part in (PI_A, PI_B, PI_C):
                st.settle()
                st.did(dve.scalar_tensor_tensor(r, k, -part, r, ALU.mult, ALU.add))
            st.settle()
            dve.tensor_scalar(r, r, PI_IN, -PI_IN, ALU.min, ALU.max).then_inc(signal, 1)

        dve.wait_ge(f_in, 96)
        for n in range(2):
            dve.wait_ge(f_dense, n + 1)
            if n:
                dve.wait_ge(f_sin, n)
            st.did(dve.tensor_scalar(sin_a[0:FILT], psum[0:FILT, n, 0:T], filt_cols[:, 2 * n:2 * n + 1],
                                     filt_cols[:, 1:2], ALU.add, ALU.mult))
            reduce_angle(FILT)
        dve.wait_ge(s_aux[2], 16)
        for n in range(4):
            q, o = n // 2, n % 2
            dve.wait_ge(y_f, n + 1)
            st.did(dve.tensor_tensor(
                filt[:], flat[:, 0:2048].rearrange("p (b s c) -> p b s c", b=2, s=2),
                window[:, :, 512 * q:512 * q + 512].unsqueeze(2).broadcast_to([P, 2, 2, 512]), ALU.mult))
            st.settle()
            st.did(dve.memset(filt[0:1, 0, 1, :], 0.0))
            st.settle()
            st.did(dve.tensor_tensor(filt_sd[:, 0], filt[:, :, 0], filt[:, :, 1], ALU.add))
            st.did(dve.tensor_tensor(filt_sd[:, 1], filt[:, :, 1], filt[:, :, 0], ALU.subtract))
            st.settle()
            least = y_part[:, 0].rearrange("p (b c) -> p b c", b=2)
            st.did(dve.tensor_tensor(least, filt_sd[:, 0], filt_sd[:, 1], ALU.min))
            st.did(dve.tensor_tensor(filt_abs[:], filt_sd[:, 0], filt_sd[:, 1], ALU.max))
            st.settle()
            dve.scalar_tensor_tensor(filt_abs[:], least, -1.0, filt_abs[:], ALU.mult, ALU.max).then_inc(y_sd, 1)
            dve.wait_ge(y_tp, n + 1)
            dve.tensor_copy(z_nat[:].rearrange("p b c -> p (b c)"), flat[:, 2048:3072]).then_inc(y_zn, 1)
            dve.wait_ge(y_k, n + 1)
            st.did(dve.tensor_scalar(filt_norm[:], psum[:, 6, 0:4], EPS, None, ALU.add))
            st.settle()
            st.did(dve.reciprocal(filt_norm[:], filt_norm[:]))
            dve.wait_ge(y_z, n + 1)
            dve.wait_ge(y_kc, n + 1)
            zr, zi = flat[:, 0:1024], flat[:, 1024:2048]
            kr, ki = (k_spec[:, r].rearrange("p f c -> p (f c)") for r in range(2))
            for r, (a_, b_, op) in enumerate(((zr, zi, ALU.add), (zi, zr, ALU.subtract))):
                st.did(dve.tensor_tensor(y_part[:, 0], a_, kr, ALU.mult))
                st.did(dve.tensor_tensor(y_part[:, 1], b_, ki, ALU.mult))
                st.settle()
                m = dve.tensor_tensor(y_spec[:, r].rearrange("p f c -> p (f c)"), y_part[:, 0], y_part[:, 1], op)
                if r == 0:
                    st.did(m)
                    st.settle()
            m.then_inc(y_y, 1)
            dve.wait_ge(y_inv, n + 1)
            dve.wait_ge(y_y, n + 1)
            for j in range(4):
                t_ = y_part[:, 0, 256 * j:256 * j + 256]
                st.did(dve.tensor_scalar(t_, psum[:, 4 + j // 2, (j % 2) * T:(j % 2) * T + T], filt_norm[:, j:j + 1], None,
                                         ALU.mult))
            st.settle()
            for j in range(4):
                t_ = y_part[:, 0, 256 * j:256 * j + 256]
                st.did(dve.scalar_tensor_tensor(t_, u[:, 4 * q + j], col("hy_bias", 8 * o + 4 * q + j), t_, ALU.mult,
                                                ALU.add))
            st.settle()
            m = dve.tensor_tensor(u[:, 4 * q:4 * q + 4].rearrange("p k t -> p (k t)"), y_part[:, 0],
                                  u[:, 8 + 8 * o + 4 * q:12 + 8 * o + 4 * q].rearrange("p k t -> p (k t)"), ALU.mult)
            m.then_inc(y_new, 1)
            dve.wait_ge(y_new, n + 1)

        def group_norm_dve(n):
            dve.wait_ge(gn_sum, n + 1)
            dve.tensor_scalar(gn_r[:].rearrange("p k t -> p (k t)"), flat[:, 0:2048], 1.0 / P, EPS, ALU.mult,
                              ALU.add).then_inc(gn_ms, 1)
            dve.wait_ge(gn_rt, n + 1)
            st.did(dve.reciprocal(gn_i[:], gn_r[:]))
            st.settle()

        dve.memset(filt_norm[:], 0.0).then_inc(gn_in, 1)
        group_norm_dve(0)
        for k in range(8):
            st.did(dve.scalar_tensor_tensor(u[:, k], u[:, k], col("hy_norm", k), gn_i[:, k], ALU.mult, ALU.mult))
        st.settle()
        st.did(dve.tensor_copy(h_hi[:, 0:8], u[:, 0:8]))
        st.settle()
        dve.tensor_tensor(h_lo[:, 0:8], u[:, 0:8], h_hi[:, 0:8].bitcast(F32), ALU.subtract).then_inc(gn_out, 1)

        def residual(name, gate=None):
            g0, n = FIRST[name], dict(STREAM)[name]
            with dve.Fori(0, n // RING) as i:
                for j in range(RING):
                    dve.wait_ge(half_done, i * 8 + (2 * (g0 + j) + 2))
                    xk = x[:, bass.ds(i * RING + j, 1)].rearrange("p a t -> p (a t)")
                    if gate is None:
                        m = dve.tensor_tensor(xk, psum[:, j, 0:T], xk, ALU.add)
                    else:
                        m = dve.scalar_tensor_tensor(xk, psum[:, j, 0:T], mod[:, bass.ds(i * RING + (gate + j), 1), 0], xk,
                                                     ALU.mult, ALU.add)
                    m.then_inc(bank_free, 1)

        dve.wait_ge(x_back, 16)
        residual("out1", 2 * KC)
        dve.wait_ge(bank_free, 4 + bank_of["mlp"])
        norm_dve("x2", x, lambda k: scales[:, 2, k:k + 1], lambda k: mod[:, 3 * KC + k, 0:1])

        def up_down_dve(g0, bank0, acc0, hid0, supers, gate=None):
            first = st.n
            with dve.Fori(0, supers) as i:
                for j in range(8):
                    s = hid[:, j % 2]
                    dve.wait_ge(hid_ready, i * 8 + (hid0 + j))
                    if gate is not None:
                        dve.wait_ge(half_done, i * 32 + (2 * (g0 + j) + 2))
                        ps = psum[:, j % 4, 0:T]
                        dve.tensor_scalar(s, ps, 0.0, None, ALU.max).then_inc(dve_step, 1)
                        dve.wait_ge(dve_step, i * 16 + (first + 2 * j + 1))
                        dve.tensor_tensor(s, s, ps, ALU.mult).then_inc(bank_free, 1)
                        dve.wait_ge(bank_free, i * 8 + (4 + bank0 + j + 1))
                    else:
                        dve.wait_ge(bank_free, i * 8 + (4 + bank0 + j + 1))
                        dve.tensor_tensor(s, gel[:, j % 2], gates_of(i * 8 + j), ALU.mult).then_inc(dve_step, 1)
                        dve.wait_ge(dve_step, i * 16 + (first + 2 * j + 1))
                    dve.tensor_copy(hid_hi[:, j], s).then_inc(dve_step, 1)
                    dve.wait_ge(dve_step, i * 16 + (first + 2 * j + 2))
                    dve.tensor_tensor(hid_lo[:, j], s, hid_hi[:, j].bitcast(F32), ALU.subtract).then_inc(hid_ready, 1)
                for d in range(16):
                    dve.wait_ge(half_done, i * 32 + (2 * (g0 + 8) + d + 1))
                    dve.wait_ge(acc_free, i * 16 + (4 + acc0 + d))
                    ps = psum[:, 4 + d % 4, 0:T]
                    if gate is not None:
                        m = dve.scalar_tensor_tensor(x[:, d], ps, mod[:, gate + d, 0:1], x[:, d], ALU.mult, ALU.add)
                    else:
                        m = dve.tensor_tensor(x[:, d], ps, x[:, d], ALU.add)
                    m.then_inc(acc_free, 1)
            st.n = first + 16 * supers

        up_down_dve(FIRST["mlp"], bank_of["mlp"], 0, HID0, dict(STREAM)["mlp"] // 16, 5 * KC)
        norm_dve("f1", x, lambda k: col("final1", k), plain=x)

        dve.wait_ge(plain_done, 1)
        norm_dve("mix", x, lambda k: col("mix", k))
        dve.wait_ge(s_aux[4], 16)
        st.did(dve.tensor_copy(pos[:], pos_i[:]))
        for n in range(2):
            if n:
                dve.wait_ge(t_sin, n)
            st.settle()
            st.did(dve.tensor_scalar(sin_a[:], pos[:], col("angles", n), None, ALU.mult))
            reduce_angle(P, t_arg)
            dve.wait_ge(t_sin, n + 1)
            st.did(dve.tensor_tensor(t_half[:], t_half[:], t_half[:], ALU.mult))
            st.settle()
            st.did(dve.tensor_scalar(trig[:, 2 * n + 1], t_half[:], -2.0, 1.0, ALU.mult, ALU.add))
        copy_stage("ret", pr)

        def rotate_dve(src, n0, pairs, kind, a_, b_):
            for n in range(pairs):
                dve.wait_ge(rot_p, n0 + n + 1)
                if n:
                    dve.wait_ge(rot_d, n0 + n)
                sin, cos = (trig[:, 2 * kind + i].unsqueeze(1).broadcast_to([P, 2, T]) for i in range(2))
                x2 = src[:, 2 * n:2 * n + 2]
                st.did(dve.tensor_tensor(a_[:], psum[:, n % 2, :].rearrange("p (k t) -> p k t", k=2), sin, ALU.mult))
                st.did(dve.tensor_tensor(b_[:], x2, cos, ALU.mult))
                st.settle()
                dve.tensor_tensor(x2, a_[:], b_[:], ALU.add).then_inc(rot_d, 1)

        def turn_v_dve(dst, heads, n0):
            for n in range(heads // 2):
                dve.wait_ge(v_tp, n0 + n + 1)
                dve.tensor_copy(dst[:, n % 2, 4 * (n // 2):4 * (n // 2) + 4].rearrange("p k c -> p (k c)"),
                                psum[:, 2 + n % 2, :]).then_inc(v_nat_, 1)

        rotate_dve(pr, 0, 8, 0, rot_a, rot_b)
        turn_v_dve(v_ret, 8, 0)
        dve.wait_ge(s_aux[3], 16)
        for h in range(RET_H):
            dve.wait_ge(r_sc, h + 1)
            if h >= 2:
                dve.wait_ge(r_o, h - 1)
            dve.tensor_tensor(ret_p[:, h % 2, 0:T], psum[:, 4 + h % 2, 0:T], ret_decay[:, h], ALU.mult)
            dve.tensor_tensor(ret_p[:, h % 2, T:], psum[:, 4 + h % 2, T:T + P], ret_decay[:, h, 0:P],
                              ALU.mult).then_inc(r_p, 1)
        group_norm_dve(1)
        dve.wait_ge(r_g, 1)
        st.did(dve.tensor_tensor(pr[:, 0:8], pr[:, 0:8], gn_i[:], ALU.mult))
        st.settle()
        st.did(dve.tensor_tensor(pr[:, 0:8], pr[:, 0:8], pr[:, 24:32], ALU.mult))
        st.settle()
        st.did(dve.tensor_copy(ret_hi[:], pr[:, 0:8]))
        st.settle()
        dve.tensor_tensor(ret_lo[:], pr[:, 0:8], ret_hi[:].bitcast(F32), ALU.subtract).then_inc(gn_out, 1)
        dve.wait_ge(gn_out, 2)
        copy_stage("dil", pd)
        rotate_dve(pd, 8, 12, 1, rot_c, rot_d_)
        turn_v_dve(v_dil, 12, 4)
        dve.wait_ge(s_aux[3], 32)
        for m_ in range(2 * DIL_HG):
            h, tb = m_ // 2, m_ % 2
            keys = P * (tb + 1)
            b = 4 + 2 * (m_ % 2)
            s = dil_s[:].rearrange("p (g k) -> p g k", g=DIL_G)[:, :, 0:keys]
            dve.wait_ge(d_sc, m_ + 1)
            if m_:
                dve.wait_ge(d_tp, m_)
            ps = flat[:, 512 * b:512 * b + DIL_G * T].rearrange("p (g k) -> p g k", g=DIL_G)[:, :, 0:keys]
            st.did(dve.scalar_tensor_tensor(s, ps, P ** -0.5, dil_mask[:, tb, :, 0:keys], ALU.mult, ALU.add))
            st.settle()
            dve.tensor_reduce(dil_n[:, 0:1], s, AX.XY, ALU.max, negate=True).then_inc(d_mx, 1)
            dve.wait_ge(d_e, m_ + 1)
            st.did(dve.reciprocal(dil_n[:, 2:3], dil_n[:, 1:2]))
            st.settle()
            dve.tensor_scalar(s, s, dil_n[:, 2:3], None, ALU.mult).then_inc(d_p, 1)
            dve.wait_ge(d_tp, m_ + 1)
            n = DIL_G * (tb + 1)
            dve.tensor_copy(dil_pt[:, 0:n].rearrange("p n t -> p (n t)"), flat[:, 0:n * P]).then_inc(d_pt, 1)
            if tb == 1:
                dve.wait_ge(d_hi, h + 1)
                dve.tensor_tensor(dil_lo[:, h], psum[:, 2 + h % 2, 0:T], dil_hi[:, h].bitcast(F32),
                                  ALU.subtract).then_inc(d_lo, 1)
        dve.wait_ge(d_lo, DIL_HG)
        copy_stage("gate", pg)
        dve.wait_ge(s_sig, 1)
        g0 = FIRST["br_ret"]
        with dve.Fori(0, KC // 2 // RING) as i:
            for n in range(2 * RING):
                dve.wait_ge(half_done, i * 8 + (2 * g0 + n + 1))
                blk = pg[:, bass.ds(i * 8 + n, 1)].rearrange("p a t -> p (a t)")
                dve.tensor_tensor(blk, psum[:, n % 4, 0:T], blk, ALU.mult).then_inc(bank_free, 1)
        g0 = FIRST["br_dil"]
        dve.wait_ge(bank_free, 4 + bank_of["br_dil"])
        for k in range(KC):
            dve.wait_ge(half_done, 2 * g0 + k // 2 + 1)
            t_, m_ = mrg[:, 0], mrg[:, 1]
            dve.tensor_tensor(t_, psum[:, k % 4, 0:T], pg[:, KC + k], ALU.mult).then_inc(bank_free, 1)
            dve.wait_ge(bank_free, 4 + bank_of["br_dil"] + k + 1)
            st.did(dve.tensor_tensor(m_, t_, pg[:, k], ALU.add))
            st.settle()
            st.did(dve.tensor_copy(h_hi[:, k], m_))
            st.settle()
            m = dve.tensor_tensor(h_lo[:, k], m_, h_hi[:, k].bitcast(F32), ALU.subtract)
            if k < KC - 1:
                st.did(m)
                st.settle()
        m.then_inc(merged, 1)
        dve.wait_ge(merged, 1)
        norm_dve("mem", mem_raw, lambda k: col("mem", k))
        residual("out2")
        copy_part("kv", kv, 0, KC)
        norm_dve("cross", x, lambda k: col("cross", k))
        copy_part("kv", kv, KC, KC)
        copy_stage("q", q_mem)
        for n in range(8):
            mb, g = n % 2, n // 2
            dve.wait_ge(m_tp, n + 1)
            dve.tensor_copy(v_mem[:, mb, 4 * g:4 * g + 4].rearrange("p k c -> p (k c)"), psum[:, n % 2, :]).then_inc(m_vn, 1)
        for h in range(MEM_H):
            dve.wait_ge(m_sc, h + 1)
            st.did(dve.tensor_reduce(mem_n[:, h % 2, 0:2], psum[:, 4 + h % 2, :].rearrange("p (b k) -> p b k", b=2),
                                     AX.X, ALU.max, negate=True))
            st.settle()
            dve.tensor_scalar(mem_n[:, h % 2, 0:2], mem_n[:, h % 2, 0:2], (D // MEM_H) ** -0.5, None,
                              ALU.mult).then_inc(m_mx, 1)
            dve.wait_ge(m_e, h + 1)
            st.did(dve.reciprocal(mem_n[:, h % 2, 2:4], mem_n[:, h % 2, 2:4]))
            st.settle()
            dve.tensor_tensor(mem_e[:, h % 2], mem_e[:, h % 2], mem_n[:, h % 2, 2:4].unsqueeze(2).broadcast_to([P, 2, T]),
                              ALU.mult).then_inc(m_p, 1)
            dve.wait_ge(m_pt_, h + 1)
            dve.tensor_copy(mem_pt[:, h % 2].rearrange("p b t -> p (b t)"), psum[:, h % 2, :]).then_inc(m_pc, 1)
            dve.wait_ge(m_hi, h + 1)
            dve.tensor_tensor(h_lo[:, 4 * h:4 * h + 4].rearrange("p k t -> p (k t)"), flat[:, 1024:2048],
                              h_hi[:, 4 * h:4 * h + 4].bitcast(F32).rearrange("p k t -> p (k t)"),
                              ALU.subtract).then_inc(m_lo, 1)
        residual("o")
        dve.wait_ge(bank_free, 4 + bank_of["pq"])
        norm_dve("ffn", x, lambda k: col("ffn", k))
        copy_stage("pq", q_peer)
        LEAST = -3.0e38

        def top16(values, spare, best, index):
            for r in range(2):
                src = (values, spare)[r]
                st.settle()
                st.did(dve.max(best[:, 8 * r:8 * r + 8], src))
                st.settle()
                st.did(dve.max_index(index[:, 8 * r:8 * r + 8], best[:, 8 * r:8 * r + 8], src))
                if r == 0:
                    st.did(dve.match_replace(spare, best[:, 0:8], values, LEAST))

        iota16 = const[:, IOTA, 0:TOPK]
        wide = [P, PEER_H, TOPK, TOPK]
        for tb in range(2):
            dve.wait_ge(p_scc, tb + 1)
            for k in range(16):
                top16(psc[:, k], psc2[:, k], top_v[:, k], top_u[:, k])
            st.settle()
            st.did(dve.tensor_copy(top_i[:], top_u[:]))
            v4 = top_v[:].rearrange("p (h two) r -> p h two r", two=2)
            i4 = top_i[:].rearrange("p (h two) r -> p h two r", two=2)
            st.did(dve.tensor_tensor(combo[:].rearrange("p h (x y) -> p h x y", x=TOPK),
                                     v4[:, :, 0].unsqueeze(3).broadcast_to(wide),
                                     v4[:, :, 1].unsqueeze(2).broadcast_to(wide), ALU.add))
            for h in range(PEER_H):
                top16(combo[:, h], combo2[:, h], com_v[:, h], com_u[:, h])
            st.settle()
            st.did(dve.tensor_scalar(com_q[:, 0], com_u[:], 4, None, ALU.logical_shift_right))
            st.did(dve.tensor_scalar(com_q[:, 1], com_u[:], 15, None, ALU.bitwise_and))
            st.settle()
            st.did(dve.tensor_copy(com_f[:], com_q[:]))
            for s in range(2):
                st.settle()
                st.did(dve.tensor_tensor(pick[:], com_f[:, s].unsqueeze(3).broadcast_to(wide),
                                         iota16.unsqueeze(1).unsqueeze(1).broadcast_to(wide), ALU.is_equal))
                st.settle()
                st.did(dve.tensor_tensor(pick[:], pick[:], i4[:, :, s].unsqueeze(2).broadcast_to(wide), ALU.mult))
                st.settle()
                st.did(dve.tensor_reduce(chosen[:, s], pick[:], AX.X, ALU.add))
            dve.tensor_tensor(chosen[:, 2], com_v[:], com_v[:, :, 0:1].broadcast_to([P, PEER_H, TOPK]),
                              ALU.subtract).then_inc(p_cv, 1)
            dve.wait_ge(p_ge, tb + 1)
            st.did(dve.tensor_reduce(gate_n[:], chosen[:, 2], AX.X, ALU.add))
            st.settle()
            st.did(dve.reciprocal(gate_n[:], gate_n[:]))
            st.settle()
            dve.tensor_tensor(chosen[:, 2], chosen[:, 2], gate_n[:].unsqueeze(2).broadcast_to([P, PEER_H, TOPK]),
                              ALU.mult).then_inc(p_tab, 1)
            dve.wait_ge(p_tt, tb + 1)
            dve.tensor_copy(tabs[:, :, tb * P:tb * P + P], psum[:, 0, 0:3 * P].rearrange("p (k t) -> p k t", k=3)
                            ).then_inc(p_tabs, 1)
        dve.wait_ge(p_tabs, 2)
        for b in range(2):
            dve.memset(psum[:, 4 + b, :], 0.0).then_inc(e_gc, 1)

        def gates_of(b):
            return gates[:, bass.ds(b, 1)].rearrange("p a t -> p (a t)")

        for f in range(2):
            first = st.n
            dve.wait_ge(hid_ready, HID0 + MLP_H + G_HALF * f)
            if f:
                dve.wait_ge(acc_free, 4 + n_acc["peer"] + 128 * f)
            with dve.Fori(0, T // 16) as i:
                for b in range(2):
                    dve.wait_ge(e_gc, i * 2 + (32 * f + b + 1))
                    i1, i2, gt = (tabs[:, k, bass.ds(i * 16 + 8 * b, 8)].unsqueeze(2) for k in range(3))
                    st_n = i * 4 + (first + 2 * b)
                    dve.tensor_tensor(hot1[:, b], i1.broadcast_to([P, 8, G_HALF]),
                                      const[:, IOTA, G_HALF * f:G_HALF * f + G_HALF].unsqueeze(1).broadcast_to(
                                          [P, 8, G_HALF]), ALU.is_equal).then_inc(dve_step, 1)
                    dve.tensor_tensor(hot2[:, b], i2.broadcast_to([P, 8, P]),
                                      const[:, IOTA].unsqueeze(1).broadcast_to([P, 8, P]),
                                      ALU.is_equal).then_inc(dve_step, 1)
                    dve.wait_ge(dve_step, st_n + 1)
                    dve.tensor_tensor(hot1[:, b], hot1[:, b], gt.broadcast_to([P, 8, G_HALF]),
                                      ALU.mult).then_inc(e_oh, 1)
            st.n = first + 4 * (T // 16)
            up_down_dve(FIRST["peer"] + EXPERT_B * f, bank_of["peer"] + G_HALF * f, n_acc["peer"] + 128 * f,
                        HID0 + MLP_H + G_HALF * f, G_HALF // 8)
        norm_dve("f2", x, lambda k: col("final2", k), plain=x)

    ctx.close()


def column_blocks(tile_matrix):
    k, n = tile_matrix.shape
    return tile_matrix.reshape(k // P, P, n // P, P).transpose(2, 1, 0, 3).reshape(n // P, P, k)


def ada_rows(w):
    return w.reshape(4, 4, P, w.shape[1] // 512, 512).transpose(3, 0, 2, 1, 4).reshape(-1, P, D)


def packed_blocks(w, per):
    k, n = w.shape
    return w.reshape(k // P, P, n // (per * P), per, P).transpose(2, 1, 3, 0, 4).reshape(n // (per * P), P, per * k)


def down_blocks(w):
    g = w.shape[0] // (8 * P)
    return w.reshape(g, 8, P, 8, 2, P).transpose(0, 3, 2, 4, 1, 5).reshape(g * 8, P, D)


def up_down(w1, w2):
    up, down = column_blocks(w1), down_blocks(w2)
    g = up.shape[0] // 8
    return np.concatenate([up.reshape(g, 8, P, D), down.reshape(g, 8, P, D)], 1).reshape(-1, P, D)


def on_partitions(v):
    return np.ascontiguousarray(v.reshape(-1, P).T)


def acts(v):
    return np.ascontiguousarray(v.T.reshape(-1, P, v.shape[0]).transpose(1, 0, 2))


def constants():
    f = np.float32
    i, j = np.arange(P)[:, None], np.arange(P)[None, :]
    ret = np.zeros((P, P))
    rot = np.zeros((P, P))
    m = np.arange(HD)
    ret[2 * m + 1, 2 * m], ret[2 * m, 2 * m + 1] = -1, 1
    rot[m + HD, m], rot[m, m + HD] = -1, 1
    square = np.stack([i == j, np.ones((P, P)), i <= j, i >= j, i > j, i < j, ret, rot, np.broadcast_to(j, (P, P))], 1)
    t, k = np.arange(T)[:, None], np.arange(T)[None, :]
    ang = 2 * np.pi * t * (k + 0.5) / (2 * T)
    dft = np.stack([np.cos(ang), np.sin(ang), np.cos(ang).T / T, np.sin(ang).T / T])
    dft = dft.reshape(4, 2, P, T).transpose(2, 0, 1, 3)
    t = np.linspace(0.0, 1.0, T, dtype=f)[:, None]
    deltas = np.linspace(math.log(1e-2) / 1.5, math.log(1e-2) / 0.3, 1024, dtype=f)
    window = np.exp(-t * np.abs(deltas)).reshape(2, P, 1024).transpose(1, 0, 2)
    bands = (FEATS - 1) // 2
    w = f(2.0 * math.pi) * np.arange(T, dtype=f)[:, None] / f(T)
    fr = np.linspace(1e-4, bands - 1, bands, dtype=f)[None, :]
    feats = np.concatenate([t, np.cos(fr * w), -np.sin(fr * w)], -1).T
    log_g = np.log1p(-np.exp2(-5.0 - np.arange(RET_H)))
    diff = np.arange(T)[None, :] - np.arange(P)[:, None]
    decay = np.stack([np.where(diff >= 0, np.exp(lg * np.maximum(diff, 0)), 0.0) for lg in log_g], 1) * P ** -0.5
    q, key = np.arange(T)[:, None], np.arange(T)[None, :]
    masks = []
    for window_, rate in ((128, 1), (512, 4), (2048, 16)):
        d = q - key
        masks.append(np.where((d >= 0) & (d % rate == 0) & (d // rate <= window_ // rate), 0.0, -1e30))
    masks = np.stack(masks, 1).reshape(2, P, 3, T).transpose(1, 0, 2, 3)
    ret_angle = np.repeat(1.0 / (10000.0 ** np.linspace(0.0, 1.0, HD, dtype=f).astype(np.float64)), 2)
    rot_angle = np.tile(1.0 / (10000.0 ** (np.arange(HD) / HD)), 2)
    out = dict(const=square, dft=dft, window=window, feats=feats, ret_decay=decay, dil_mask=masks)
    return {n: np.ascontiguousarray(v, dtype=f) for n, v in out.items()}, np.stack([ret_angle, rot_angle], 1).astype(f)


def layout(**v):
    one = {n: np.asarray(v[n])[0] for n in v if np.asarray(v[n]).ndim > 1 and n not in ("c", "positions_2")}
    w_in = one["w_in"]
    hy, xbc_, dt_, z_ = np.split(w_in, [3072, 3072 + 1536, 3072 + 1536 + 32], axis=1)
    w2 = one["w_in_2"]
    stream = np.concatenate([
        ada_rows(one["w_ada"]), column_blocks(xbc_), column_blocks(hy), column_blocks(z_),
        column_blocks(one["w_out"]), up_down(one["w_mlp1"], one["w_mlp2"]), column_blocks(w2),
        packed_blocks(one["w_br_ret_2"], 2), packed_blocks(one["w_br_dil_2"], 4), column_blocks(one["w_out_2"]),
        column_blocks(one["w_kv_mem_2"]), column_blocks(one["w_q_mem_2"]), column_blocks(one["w_o_mem_2"]),
        column_blocks(one["w_peer_q_2"]), up_down(one["peer_u_2"].T, one["peer_v_2"])])
    consts, angles = constants()
    by_column = dict(
        b_ada=one["b_ada"], norm1=one["norm1_w"], hy_w=one["hy_conv_w"], hy_b=one["hy_conv_b"],
        hy_bias=one["hy_bias"], hy_norm=one["hy_norm_w"], ssd_w=one["ssd_conv_w"], ssd_b=one["ssd_conv_b"],
        ssd_norm=one["ssd_norm_w"], ssd_d=np.repeat(one["ssd_d"], HD), norm2=one["norm2_w"],
        final1=np.asarray(v["final_norm_w"]), mix=one["g_mix_2"], cross=one["g_cross_2"], mem=one["g_mem_2"],
        ffn=one["g_ffn_2"], final2=np.asarray(v["g_final_2"]), zero=np.zeros(D, np.float32), angles=angles.T)
    cols = np.concatenate([on_partitions(np.ascontiguousarray(by_column[n])) for n, _ in COLUMNS], 1)
    c = np.stack([np.asarray(v["c"])[0], np.asarray(v["c_ctx"])], 1).reshape(KC, P, 2).transpose(1, 0, 2)
    small = np.stack([one["filt_b1"], one["filt_freq"], one["filt_b2"]], 1)
    arrays = dict(
        consts, stream=stream, cols=cols, c=c, x=acts(one["x"]), ctx=acts(one["ctx"]), mem=acts(one["mem_2"]),
        wdt=dt_.reshape(KC, P, 32).transpose(1, 0, 2),
        dt_bias=np.broadcast_to(one["dt_bias"].reshape(1, 32), (P, 32)),
        a_log=np.broadcast_to(one["a_log"].reshape(1, 32), (P, 32)),
        filt_w1=one["filt_w1"], filt_w2=one["filt_w2"], filt_w3=one["filt_w3"], filt_cols=small,
        pos=np.broadcast_to(np.asarray(v["positions_2"])[0:1], (P, T)),
        subkeys=one["peer_subkeys_2"].reshape(16, P, P).transpose(2, 0, 1))
    return {n: np.ascontiguousarray(x_) for n, x_ in arrays.items()}


def kernel(**inputs):
    import concourse.bacc as bacc
    from concourse.bass_utils import run_bass_kernel_spmd

    arrays = layout(**inputs)
    nc = bacc.Bacc("TRN2", target_bir_lowering=False, num_devices=1)
    a = {n: nc.dram_tensor(n, v.shape, mybir.dt.from_np(v.dtype), kind="ExternalInput").ap() for n, v in arrays.items()}
    out = nc.dram_tensor("out", (P, KC, T), F32, kind="ExternalOutput").ap()
    build(nc, a, out)
    got = run_bass_kernel_spmd(nc, [arrays], core_ids=[0]).results[0]["out"]
    return np.ascontiguousarray(got.transpose(1, 0, 2).reshape(D, T).T)[None]
```

```python
import math
from contextlib import ExitStack

import numpy as np

import concourse.bass as bass
from concourse import mybir

F32 = mybir.dt.float32
F32R = mybir.dt.float32r
I32 = mybir.dt.int32
U32 = mybir.dt.uint32
ALU = mybir.AluOpType
ACT = mybir.ActivationFunctionType
AX = mybir.AxisListType

P = 128
T = 256
D = 2048
KC = D // P
EPS = 1e-6
TWO_PI = 2.0 * math.pi
PI_A = 6.28125
PI_B = 0.0019350051879882812
PI_C = TWO_PI - PI_A - PI_B
PI_IN = 3.1415925

N_ADA = 6 * KC
ADA_1 = 2 * KC
ADA_G = ADA_1 // 4
ADA_2 = N_ADA - ADA_1
HYENA = 24
HW = 8
XBC = 12
ZB = 8
GRID_W = 64
HEADS = 16
HD = 64
FILT = 64
FEATS = 33
MLP_H = 64
HID0 = 1
RET_H = 8
DIL_G, DIL_HG = 3, 4
DIL_H = DIL_G * DIL_HG
RET_TILES, DIL_TILES, GATE_TILES = 4 * RET_H, 3 * DIL_H, 2 * KC
MEM_H = 4
PEER_H = 8
TOPK = 16
EXPERT_B = 128
QUARTER = EXPERT_B // 4
EARLY = 24

COLUMNS = [("b_ada", N_ADA), ("norm1", KC), ("hy_w", 3 * HYENA), ("hy_b", HYENA), ("hy_bias", 2 * HW),
           ("hy_norm", HW), ("ssd_w", 3 * XBC), ("ssd_b", XBC), ("ssd_norm", ZB), ("ssd_d", ZB),
           ("norm2", KC), ("final1", KC), ("mix", KC), ("cross", KC), ("mem", KC), ("ffn", KC), ("final2", KC),
           ("zero", KC), ("angles", 2)]
COL = {}
for _name, _n in COLUMNS:
    COL[_name] = sum(n for _, n in COLUMNS[:len(COL)])
N_COL = sum(n for _, n in COLUMNS)

IDENT, ONES, LE, GE, GT, LT, PERM_RET, PERM_ROT, IOTA = range(9)

STREAM = [("ada", ADA_1), ("xbc", XBC), ("hy", HYENA), ("z", ZB), ("ada2", ADA_2), ("out1", KC), ("mlp", 2 * MLP_H),
          ("ret", RET_TILES), ("dil", DIL_TILES), ("gate", GATE_TILES), ("br_ret", KC // 2), ("br_dil", KC // 4),
          ("out2", KC), ("kv", 2 * KC), ("q", KC), ("o", KC), ("pq", KC), ("peer", 2 * EXPERT_B)]
FIRST = {}
for _name, _n in STREAM:
    FIRST[_name] = sum(n for _, n in STREAM[:len(FIRST)])
N_TILES = sum(n for _, n in STREAM)
RING = 4
SPLIT0 = FIRST["xbc"]


class Steps:

    def __init__(self, eng, sem):
        self.eng, self.sem, self.n = eng, sem, 0

    def did(self, ins):
        ins.then_inc(self.sem, 1)
        self.n = self.n + 1

    def settle(self):
        self.eng.wait_ge(self.sem, self.n)


def build(nc, a, out):
    ctx = ExitStack()

    def sem(name):
        return ctx.enter_context(nc.semaphore(name))

    psum = ctx.enter_context(nc.psum_tensor("psum", [P, 8, 512], F32))
    flat = psum[:].rearrange("p b n -> p (b n)")
    BASE = 16512

    def at(name, shape, kib, dt=F32):
        return nc.alloc_sbuf_tensor_at(name, shape, dt, offset=BASE + int(kib * 1024))

    const = at("const", [P, 9, P], 0)
    cols = at("cols", [P, N_COL], 4.5)
    mod = at("mod", [P, N_ADA, 2], 6.5)
    scales = at("scales", [P, 3, KC], 7.25)
    c_raw = at("c_raw", [P, KC, 2], 7.5)
    c_silu = at("c_silu", [P, KC, 2], 7.75)
    ring = at("ring", [P, RING, KC, P], 8)
    w_hi = at("w_hi", [P, 4, KC // 2, P], 40, F32R)
    w_lo = at("w_lo", [P, 4, KC // 2, P], 56, F32R)
    x = at("x", [P, KC, T], 72)
    h_hi = at("h_hi", [P, KC, T], 88, F32R)
    h_lo = at("h_lo", [P, KC, T], 104, F32R)
    ntmp = at("ntmp", [P, 2, 4, T], 192)
    nrt = at("nrt", [P, T], 200)
    nrstd = at("nrstd", [P, T], 201)
    norm_part = at("norm_part", [P, 2, T], 200)
    mod_rows = at("mod_rows", [2, ADA_1 * P], 88)
    ada_acc = at("ada_acc", [P, ADA_2 // KC, D], 40)
    ctx_raw = at("ctx_raw", [P, KC, T], 176)
    c_hi = at("c_hi", [P, KC, T], 120, F32R)
    c_lo = at("c_lo", [P, KC, T], 136, F32R)
    xbc = at("xbc", [P, XBC, 2, T], 152)
    wdt = at("wdt", [P, KC, 32], 176)
    wdt_s = at("wdt_s", [P, KC, 2, 32], 178, F32R)
    u = at("u", [P, HYENA, T], 120)
    z = at("z", [P, ZB, T], 144)
    xs_nat = at("xs_nat", [P, 4, ZB, P], 88)
    state = at("state", [P, 2, 2, 512], 104)
    cb = at("cb", [P, 2, 768], 112)
    b_nat = at("b_nat", [P, 2, 2, P], 118)
    y_ssd = at("y_ssd", [P, ZB, T], 176)
    xw = at("xw", [P, 2, 512], 184)
    decay = at("decay", [P, 2, 768], 184)
    mix_m = at("mix_m", [P, 2, 512], 190)
    mix_t = at("mix_t", [P, 256], 194)
    c_off = at("c_off", [P, 2, 512], 195)
    off_e = at("off_e", [P, 2, 512], 203)
    y_sq = at("y_sq", [P, ZB, T], 184)
    g_rt = at("g_rt", [P, 2, T], 192)
    g_rstd = at("g_rstd", [P, 2, T], 194)
    dt_w = at("dt_w", [P, 4, 4, 32], 198)
    dt_p = at("dt_p", [P, 4, 32], 200)
    dt_u = at("dt_u", [P, 4, 32], 200.5)
    dt = at("dt", [P, 4, 32], 201)
    da = at("da", [P, 4, 32], 201.5)
    dt_bias = at("dt_bias", [P, 32], 202)
    a_exp = at("a_exp", [P, 32], 202.125)
    a_log = at("a_log", [P, 32], 202.25)
    cs = at("cs", [P, 2, 32], 202.375)
    wd = at("wd", [P, 2, 32], 202.625)

    dft = at("dft", [P, 4, 2, T], 88)
    window = at("window", [P, 2, 1024], 104)
    filt_w3 = at("filt_w3", [FILT, 4096], 72)
    filt = at("filt", [P, 2, 2, 512], 152)
    filt_abs = at("filt_abs", [P, 2, 512], 160)
    filt_sd = at("filt_sd", [P, 2, 2, 512], 164)
    z_nat = at("z_nat", [P, 2, 512], 172)
    k_spec = at("k_spec", [P, 2, 2, 512], 176)
    y_spec = at("y_spec", [P, 2, 2, 512], 184)
    y_part = at("y_part", [P, 2, 1024], 192)
    feats = at("feats", [FEATS, T], 199)
    hdn = at("hdn", [FILT, 2, T], 201)
    sin_a = at("sin_a", [P, T], 203)
    sin_k = at("sin_k", [P, T], 204)
    sin_i = at("sin_i", [P, T], 205, I32)
    filt_w12 = at("filt_w12", [FILT, 2 * FILT], 206)
    filt_cols = at("filt_cols", [FILT, 3], 206.5)
    filt_norm = at("filt_norm", [P, 4], 206.75)
    gn_q = at("gn_q", [P, 8, T], 160)
    gn_r = at("gn_r", [P, 8, T], 152)
    gn_i = at("gn_i", [P, 8, T], 168)
    hid_hi = at("hid_hi", [P, 8, T], 184, F32R)
    hid_lo = at("hid_lo", [P, 8, T], 192, F32R)
    hid = at("hid", [P, T], 206)
    trig = at("trig", [P, 4, T], 176)
    pos_i = at("pos_i", [P, T], 206, I32)
    pos = at("pos", [P, T], 201)
    t_half = at("t_half", [P, T], 202)
    pr = at("pr", [P, RET_TILES, T], 120)
    v_ret = at("v_ret", [P, 2, RET_H, P], 152)
    ret_decay = at("ret_decay", [P, RET_H, T], 160)
    ret_p = at("ret_p", [P, 2, 384], 168)
    rot_a = at("rot_a", [P, 2, T], 171)
    rot_b = at("rot_b", [P, 2, T], 173)
    ret_hi = at("ret_hi", [P, RET_H, T], 184, F32R)
    ret_lo = at("ret_lo", [P, RET_H, T], 192, F32R)
    pd = at("pd", [P, DIL_TILES, T], 120)
    v_dil = at("v_dil", [P, 2, DIL_H, P], 156)
    dil_mask = at("dil_mask", [P, 2, DIL_G, T], 168)
    rot_c = at("rot_c", [P, 2, T], 180)
    rot_d_ = at("rot_d", [P, 2, T], 182)
    dil_s = at("dil_s", [P, 2, DIL_G * T], 174)
    dil_pt = at("dil_pt", [P, 6, P], 203)
    dil_n = at("dil_n", [P, 2, 4], 206)
    dil_hi = at("dil_hi", [P, DIL_HG, T], 152, F32R)
    dil_lo = at("dil_lo", [P, DIL_HG, T], 180, F32R)
    pg = at("pg", [P, GATE_TILES, T], 120)
    mrg = at("mrg", [P, 2, T], 200)
    mem_raw = at("mem_raw", [P, KC, T], 156)
    mem_hi = at("mem_hi", [P, KC, T], 120, F32R)
    mem_lo = at("mem_lo", [P, KC, T], 136, F32R)
    kv = at("kv", [P, 2 * KC, T], 152)
    v_mem = at("v_mem", [P, 2, KC, P], 120)
    q_mem = at("q_mem", [P, KC, T], 136)
    mem_e = at("mem_e", [P, 2, 2, T], 184)
    mem_pt = at("mem_pt", [P, 2, 2, T], 188)
    mem_n = at("mem_n", [P, 2, 4], 206)
    q_peer = at("q_peer", [P, KC, T], 120)
    subkeys = at("subkeys", [P, 16, P], 136)
    psc = at("psc", [P, 2, 16, P], 152)
    psc2 = at("psc2", [P, 16, P], 168)
    pick = at("pick", [P, PEER_H, TOPK, TOPK], 176)
    top_v = at("top_v", [P, 16, TOPK], 184)
    top_u = at("top_u", [P, 16, TOPK], 185, U32)
    top_i = at("top_i", [P, 16, TOPK], 186)
    com_v = at("com_v", [P, PEER_H, TOPK], 187)
    com_u = at("com_u", [P, PEER_H, TOPK], 187.5, U32)
    com_q = at("com_q", [P, 2, PEER_H, TOPK], 188, U32)
    com_f = at("com_f", [P, 2, PEER_H, TOPK], 189)
    chosen = at("chosen", [P, 3, 2, PEER_H, TOPK], 190)
    gate_n = at("gate_n", [P, 2, PEER_H], 193)
    tabs = at("tabs", [P, 2, T], 200)
    gate_t = at("gate_t", [P, 2, T], 202, F32R)
    before = at("before", [P, QUARTER, T], 120)
    gates = at("gates", [P, QUARTER, T], 152)
    hot2 = at("hot2", [P, 2, 8, P], 184, F32R)
    hot1 = at("hot1", [P, 2, 2, 8, QUARTER], 192, F32R)
    hot_e = at("hot_e", [P, 8, QUARTER], 196)

    landed = [sem(f"landed{s}") for s in range(RING)]
    s_const = sem("const_landed")
    half_done = sem("half_done")
    hi_ready, lo_ready = sem("hi_ready"), sem("lo_ready")
    bank_free, acc_free = sem("bank_free"), sem("acc_free")
    dve_step, act_step = sem("dve_step"), sem("act_step")
    s_csilu, s_mod = sem("c_silu_ready"), sem("mod_ready")
    ada_scaled = sem("ada_scaled")
    ada_copied, ada_turned = sem("ada_copied"), sem("ada_turned")
    norm_in = sem("norm_in")
    norm_sq, norm_sum, norm_ms, norm_rt = sem("norm_sq"), sem("norm_sum"), sem("norm_ms"), sem("norm_rt")
    norm_half = sem("norm_half")
    norm_t, norm_hi, norm_lo, plain_done = sem("norm_t"), sem("norm_hi"), sem("norm_lo"), sem("norm_plain")
    s_aux = [sem(f"aux{i}") for i in range(6)]
    s_silu = sem("xbc_silu")
    wdt_split = sem("wdt_split")
    wdt_h = sem("wdt_hi_ready")
    dt_sum, dt_e, dt_nab = sem("dt_sum"), sem("dt_e"), sem("dt_nab")
    dt_ready = sem("dt_ready")
    ssd_tp, ssd_tpc = sem("ssd_tp"), sem("ssd_tp_copied")
    cs_sum, cs_cp, cs_wd, cs_wx = sem("cs_sum"), sem("cs_copied"), sem("state_w_arg"), sem("state_w_exp")
    ssd_xw, ssd_st, ssd_stc = sem("ssd_xw"), sem("ssd_state"), sem("ssd_state_copied")
    ssd_cb, ssd_cbm = sem("ssd_cb"), sem("ssd_cb_masked")
    hd_row, hd_d, hd_e, hd_m, hd_o, hd_y, hd_yc = (sem(n) for n in (
        "head_rows", "head_diff", "head_exp", "head_m", "head_off", "head_y", "head_y_copied"))
    g_z, g_y, g_sq, g_sum, g_ms, g_srt, g_out = (sem(n) for n in (
        "gate_silu", "gate_y", "gate_sq", "gate_sum", "gate_ms", "gate_rt", "gate_out"))
    f_in, f_dense, f_arg, f_sin = sem("filter_in"), sem("filter_dense"), sem("sine_arg"), sem("sine")
    y_f, y_h, y_sd, y_k, y_kc, y_tp, y_zn, y_z, y_y, y_inv, y_new = (sem("hy_" + n) for n in (
        "filter", "windowed", "sum_diff", "spectra", "spectra_copied", "turned", "turned_copied", "z_spectra", "product",
        "inverse", "new_z"))
    gn_in, gn_sq, gn_sum, gn_ms, gn_rt, gn_out = (sem("gn_" + n) for n in ("in", "sq", "sum", "ms", "rt", "out"))
    x_back = sem("x_back")
    hid_ready = sem("hidden_ready")
    t_arg, t_sin, t_ready = sem("trig_arg"), sem("trig_sin"), sem("trig_ready")
    rot_p, rot_d = sem("rotated_half"), sem("rotated")
    v_tp, v_nat_ = sem("v_turned"), sem("v_natural")
    r_sc, r_p, r_o, r_oc = sem("ret_scores"), sem("ret_decayed"), sem("ret_out"), sem("ret_out_copied")
    r_g = sem("ret_gate")
    d_sc, d_mx, d_e, d_p, d_tp, d_pt, d_o, d_hi, d_lo = (sem("dil_" + n) for n in (
        "scores", "max", "exp", "prob", "turned", "prob_turned", "out", "hi", "lo"))
    s_sig = sem("gates_sigmoid")
    merged = sem("merged")
    k_half = sem("keys_done")
    m_tp, m_vn, m_sc, m_mx, m_e, m_p, m_pt_, m_pc, m_o, m_hi, m_lo = (sem("mem_" + n) for n in (
        "v_turned", "v_natural", "scores", "max", "exp", "prob", "turned", "prob_turned", "out", "hi", "lo"))
    p_sc, p_scc, p_cv, p_ge, p_tab, p_tt, p_tabs = (sem("peer_" + n) for n in (
        "scores", "scores_copied", "gate_arg", "gate_exp", "table", "table_turned", "tables"))
    e_oh, e_g, e_gc = sem("one_hot"), sem("gates_made"), sem("gates_copied")
    s_out = sem("out_stored")
    block = ctx.enter_context(nc.Block())

    def col(name, i, n=1):
        return cols[:, COL[name] + i:COL[name] + i + n] if isinstance(i, int) else cols[:, bass.ds(i + COL[name], n)]

    def sq(i):
        return const[:, i, :]

    bank_of, n_bank = {}, 0
    for name, n in STREAM:
        bank_of[name] = n_bank
        n_bank += {"ada": 0, "ada2": 0, "mlp": n // 2, "peer": n // 2, "br_ret": 2 * n, "br_dil": 4 * n}.get(name, n)
    n_acc = {"mlp": 0, "peer": KC * MLP_H // 8}

    norm_to = {"ctx": (c_hi, c_lo), "mem": (mem_hi, mem_lo)}
    NORMS = ["ctx", "x1", "x2", "f1", "mix", "mem", "cross", "ffn", "f2"]
    NI = {n: i for i, n in enumerate(NORMS)}
    NS = {n: i for i, n in enumerate(n for n in NORMS if n not in ("f1", "f2"))}

    @block.sync
    def _(sp):
        sp.dma_start(const[:], a["const"]).then_inc(s_const, 16)
        sp.dma_start(cols[:], a["cols"]).then_inc(s_const, 16)
        sp.dma_start(c_raw[:], a["c"]).then_inc(s_const, 16)

        def load(g, s):
            tile = a["stream"][bass.ds(g, 1)].rearrange("a p (k n) -> (a p) k n", n=P)
            sp.dma_start(ring[:, s], tile).then_inc(landed[s], 16)

        for s in range(RING):
            load(s, s)
        with sp.Fori(1, SPLIT0 // RING + 1) as i:
            for s in range(RING):
                sp.wait_ge(half_done, i * 8 + (2 * s - 6))
                load(i * RING + s, s)
        with sp.Fori(SPLIT0 // RING + 1, N_TILES // RING) as i:
            for s in range(RING):
                sp.wait_ge(lo_ready, i * 8 + (2 * s - 6 - 2 * SPLIT0))
                load(i * RING + s, s)

        for q in range(4):
            sp.wait_ge(plain_done, 4 + q + 1)
            sp.dma_start(out[:, 4 * q:4 * q + 4], x[:, 4 * q:4 * q + 4]).then_inc(s_out, 16)
        sp.wait_ge(s_out, 64)

    @block.gpsimd
    def _(pool):
        def split(tiles, hi0):
            with pool.Fori(0, tiles // RING) as i:
                for s in range(RING):
                    for h in range(2):
                        pool.wait_ge(hi_ready, i * 8 + (hi0 + 2 * s + h + 1))
                        k = slice(h * KC // 2, (h + 1) * KC // 2)
                        slot = 2 * (s % 2) + h
                        pool.tensor_tensor(w_lo[:, slot], ring[:, s, k], w_hi[:, slot].bitcast(F32),
                                           ALU.subtract).then_inc(lo_ready, 1)

        g0 = FIRST["ada2"]
        split(g0 - SPLIT0, 0)
        pool.wait_ge(half_done, 2 * g0)
        for n in range(ADA_2 // KC):
            for k in range(1, KC):
                g = g0 + KC * n + k
                rows, before_it = (ring[:, g_ % RING].rearrange("p k n -> p (k n)") for g_ in (g, g - 1))
                pool.wait_ge(ada_scaled, KC * n + k + 1)
                if k > 1:
                    pool.wait_ge(lo_ready, 2 * (g - SPLIT0))
                pool.tensor_tensor(ada_acc[:, n], before_it if k == 1 else ada_acc[:, n], rows,
                                   ALU.add).then_inc(lo_ready, 4 if k == 1 else 2)
        split(N_TILES - FIRST["out1"], 2 * (g0 - SPLIT0))

    @block.tensor
    def _(pe):
        def half(g, s, h, start, stop, out_of, hi, lo):
            pe.wait_ge(lo_ready, g * 2 + (h + 1 - 2 * SPLIT0))
            slot = 2 * (s % 2) + h
            for c in range(KC // 2):
                o, x_hi, x_lo = out_of(c), hi(c), lo(c)
                pe.matmul(o, w_hi[:, slot, c], x_hi, start=start(c), stop=False)
                pe.matmul(o, w_hi[:, slot, c], x_lo, start=False, stop=False)
                m = pe.matmul(o, w_lo[:, slot, c], x_hi, start=False, stop=stop(c))
            m.then_inc(half_done, 1)

        def linear(name, hi, lo, first=0, n=None, after=None):
            g0, n = FIRST[name] + first, n or dict(STREAM)[name]

            def moving(j, k):
                if after is not None and j == 0 and k % 4 == 0:
                    pe.wait_ge(norm_lo, 4 * NS[after] + k // 4 + 1)
                return hi[:, k]

            with pe.Fori(0, n // RING) as i:
                for j in range(RING):
                    pe.wait_ge(bank_free, i * RING + (bank_of[name] + first + j + 1))
                    for h in range(2):
                        half(i * RING + (g0 + j), j, h, lambda c: h == 0 and c == 0,
                             lambda c: h == 1 and c == KC // 2 - 1, lambda c: psum[:, j, 0:T],
                             lambda c: moving(j, h * 8 + c), lambda c: lo[:, h * 8 + c])

        def norm_pe(name, bank=7):
            n = NI[name]
            for s in range(2):
                pe.wait_ge(norm_half, 2 * n + s + 1)
                m = pe.matmul(psum[:, bank, 0:T], sq(ONES), norm_part[:, s], start=s == 0, stop=s == 1)
            m.then_inc(norm_sum, 1)

        pe.wait_ge(s_const, 48)
        pe.wait_ge(s_csilu, 1)
        pe.wait_ge(acc_free, 4)
        with pe.Fori(0, ADA_G // 2) as i:
            for b in range(2):
                pe.wait_ge(ada_copied, i * 2 + (b + 1))
                for j in range(RING):
                    pe.wait_ge(landed[j], i * 32 + (16 * b + 16))
                    wide = ring[:, j].rearrange("p k n -> p (k n)")
                    for k in range(4):
                        m = pe.matmul(psum[0:2, 4 + b, :], c_silu[:, 4 * j + k], wide[:, 512 * k:512 * k + 512],
                                      start=j + k == 0, stop=j + k == 6)
                        if k % 2:
                            m.then_inc(half_done, 1)
        pe.wait_ge(ada_copied, 2 + ADA_G)
        for n in range(ADA_1):
            m = pe.transpose(psum[:, 6, 2 * n:2 * n + 2], mod_rows[:, n * P:n * P + P], const[0:2, IDENT, 0:2])
        m.then_inc(ada_turned, 1)

        norm_pe("ctx")
        norm_pe("x1")

        pe.wait_ge(norm_lo, 8)
        with pe.Fori(0, XBC // RING) as i:
            for j in range(RING):
                pe.wait_ge(bank_free, i * RING + (bank_of["xbc"] + j + 1))
                for h in range(2):
                    pe.wait_ge(lo_ready, i * 8 + (2 * j + h + 1))
                    slot = 2 * (j % 2) + h
                    for side, (hi, lo) in enumerate(((h_hi, h_lo), (c_hi, c_lo))):
                        o = psum[:, j, side * T:side * T + T]
                        for c in range(8):
                            k = h * 8 + c
                            pe.matmul(o, w_hi[:, slot, c], hi[:, k], start=(k == 0 and side == 0), stop=False,
                                      skip_group_check=True)
                            pe.matmul(o, w_hi[:, slot, c], lo[:, k], start=False, stop=False, skip_group_check=True)
                            m = pe.matmul(o, w_lo[:, slot, c], hi[:, k], start=False, stop=k == KC - 1,
                                          skip_group_check=True)
                    m.then_inc(half_done, 1)

        pe.wait_ge(wdt_split, 1)
        for tb in range(4):
            hi, lo = ((h_hi, h_lo), (c_hi, c_lo))[tb // 2]
            tok = slice((tb % 2) * P, (tb % 2) * P + P)
            o = psum[:, 5, 64 * tb:64 * tb + 64]
            for k in range(KC):
                pe.matmul(o, hi[:, k, tok], wdt_s[:, k].rearrange("p s n -> p (s n)"), start=k == 0, stop=False,
                          skip_group_check=True)
                m = pe.matmul(o[:, 0:32], lo[:, k, tok], wdt_s[:, k, 0], start=False, stop=k == KC - 1,
                              skip_group_check=True)
        m.then_inc(dt_sum, 1)

        linear("hy", h_hi, h_lo)
        linear("z", h_hi, h_lo)

        pe.wait_ge(s_silu, 1)
        pe.wait_ge(bank_free, bank_of["out1"] + 4)
        for n in range(8):
            tb, q = n // 2, n % 2
            if n >= 2:
                pe.wait_ge(ssd_tpc, n - 1)
            for k in range(4):
                m = pe.transpose(psum[:, n % 2, k * P:k * P + P],
                                 xbc[:, 4 * q + k, tb // 2, (tb % 2) * P:(tb % 2) * P + P], sq(IDENT))
            m.then_inc(ssd_tp, 1)
        pe.wait_ge(ssd_tpc, 7)
        for g in range(2):
            for tb in range(2):
                m = pe.transpose(psum[:, 0, (2 * g + tb) * P:(2 * g + tb + 1) * P],
                                 xbc[:, 8 + g, 1, tb * P:tb * P + P], sq(IDENT))
        m.then_inc(ssd_tp, 1)
        pe.wait_ge(dt_ready, 1)
        F, B = slice(0, 16), slice(16, 32)
        sums = [
            (0, F, [(LE, 0)]), (32, F, [(ONES, 0), (LE, 1)]), (16, B, [(GE, 0), (ONES, 1)]), (48, B, [(GE, 1)]),
            (64, F, [(GT, 2), (ONES, 3)]), (96, F, [(GT, 3)]), (80, B, [(LT, 2)]), (112, B, [(ONES, 2), (LT, 3)])]
        for c0, d, parts in sums:
            for n, (mat, tb) in enumerate(parts):
                m = pe.matmul(psum[:, 4, c0:c0 + 16], sq(mat), da[:, tb, d], start=n == 0, stop=n == len(parts) - 1)
        m.then_inc(cs_sum, 1)
        pe.wait_ge(ssd_tpc, 9)
        for n in range(4):
            d, g = n // 2, n % 2
            if n >= 2:
                pe.wait_ge(ssd_stc, n - 1)
            for tb in range(2):
                pe.wait_ge(ssd_xw, 2 * n + tb + 1)
                m = pe.matmul(psum[:, 2 + n % 2, :], b_nat[:, g, tb], xw[:, tb, :], start=tb == 0, stop=tb == 1)
                m.then_inc(ssd_st, 1)
        for g in range(2):
            if g:
                pe.wait_ge(ssd_cbm, 4)
            for tb in range(2):
                m = pe.matmul(psum[:, 6, tb * T:tb * T + T], xbc[:, 8 + g, 0, tb * P:tb * P + P], xbc[:, 10 + g, 0, :],
                              start=True, stop=True)
            m.then_inc(ssd_cb, 1)

            def rows(hh):
                if hh >= 2:
                    pe.wait_ge(hd_d, hh - 1)
                    pe.wait_ge(hd_o, hh - 1)
                o = psum[:, hh % 2, :]

                def spread(tb, d):
                    return da[:, tb, 16 * d + hh:16 * d + hh + 1].broadcast_to([P, P])
                pe.matmul(o[:, 0:P], spread(0, 0), sq(LE), start=True, stop=False, skip_group_check=True)
                pe.matmul(o[:, P:T], spread(0, 0), sq(ONES), start=False, stop=False, skip_group_check=True)
                pe.matmul(o[:, P:T], spread(1, 0), sq(LE), start=False, stop=False, skip_group_check=True)
                pe.matmul(o[:, T:T + P], spread(0, 1), sq(GE), start=False, stop=False, skip_group_check=True)
                pe.matmul(o[:, T:T + P], spread(1, 1), sq(ONES), start=False, stop=False, skip_group_check=True)
                pe.matmul(o[:, T + P:], spread(1, 1), sq(GE), start=False, stop=True,
                          skip_group_check=True).then_inc(hd_row, 1)

            for hh in range(8 * g, 8 * g + 8):
                if hh == 0:
                    rows(0)
                if hh + 1 < HEADS:
                    rows(hh + 1)
                if hh == 0:
                    pe.wait_ge(ssd_stc, 4)
                if hh % 2 == 0 and hh >= 4:
                    pe.wait_ge(hd_yc, hh // 2 - 1)
                pe.wait_ge(hd_m, hh + 1)
                o = psum[64 * (hh % 2):64 * (hh % 2) + 64, 4 + (hh // 2) % 2, 0:T]
                blk, off = hh // 2, 64 * (hh % 2)
                ch = slice((hh % 8) * 64, (hh % 8) * 64 + 64)
                for tb in range(2):
                    pe.matmul(o, xs_nat[:, tb, blk, off:off + 64], mix_m[:, hh % 2, tb * T:tb * T + T],
                              start=tb == 0, stop=False)
                for d in range(2):
                    m = pe.matmul(o, state[:, d, g, ch], c_off[:, hh % 2, d * T:d * T + T], start=False, stop=d == 1)
                m.then_inc(hd_y, 1)
        pe.wait_ge(g_sq, 1)
        for g in range(2):
            for k in range(4):
                m = pe.matmul(psum[:, 2, g * T:g * T + T], sq(ONES), y_sq[:, 4 * g + k], start=k == 0, stop=k == 3)
        m.then_inc(g_sum, 1)

        pe.wait_ge(f_in, 96)
        pe.wait_ge(g_out, 1)
        pe.matmul(psum[0:FILT, 0, 0:T], filt_w12[0:FEATS, 0:FILT], feats[:], start=True, stop=True).then_inc(f_dense, 1)
        pe.wait_ge(f_sin, 1)
        pe.matmul(psum[0:FILT, 1, 0:T], filt_w12[:, FILT:], hdn[:, 0], start=True, stop=True).then_inc(f_dense, 1)
        pe.wait_ge(f_sin, 2)

        def filter_taps(n):
            q, o = n // 2, n % 2
            for tb in range(2):
                for sg in range(2):
                    w0 = o * 2048 + sg * 1024 + q * 512
                    m = pe.matmul(psum[:, 2 * tb + sg, :], hdn[:, 1, tb * P:tb * P + P], filt_w3[:, w0:w0 + 512],
                                  start=True, stop=True)
            m.then_inc(y_f, 1)

        filter_taps(0)
        for n in range(4):
            q = n // 2
            pe.wait_ge(y_sd, n + 1)
            for ri in range(2):
                for fb in range(2):
                    for tb in range(2):
                        pe.matmul(psum[:, 2 * ri + fb, :], dft[:, ri, tb, fb * P:fb * P + P], filt_sd[:, ri, tb],
                                  start=tb == 0, stop=tb == 1)
            for j in range(4):
                for tb in range(2):
                    m = pe.matmul(psum[:, 6, j:j + 1], filt_abs[:, tb, j * P:j * P + P], const[:, ONES, 0:1],
                                  start=tb == 0, stop=tb == 1)
            m.then_inc(y_k, 1)
            if n:
                pe.wait_ge(y_new, n)
            for tb in range(2):
                for j in range(4):
                    m = pe.transpose(psum[:, 4 + tb, j * P:j * P + P], u[:, 4 * q + j, tb * P:tb * P + P], sq(IDENT))
            m.then_inc(y_tp, 1)
            pe.wait_ge(y_zn, n + 1)
            pe.wait_ge(y_kc, n + 1)
            for ri in range(2):
                for fb in range(2):
                    for tb in range(2):
                        m = pe.matmul(psum[:, 2 * ri + fb, :], dft[:, ri, tb, fb * P:fb * P + P], z_nat[:, tb],
                                      start=tb == 0, stop=tb == 1)
            m.then_inc(y_z, 1)
            pe.wait_ge(y_y, n + 1)
            if n < 3:
                filter_taps(n + 1)
            for j in range(4):
                for k in range(4):
                    m = pe.matmul(psum[:, 4 + j // 2, (j % 2) * T:(j % 2) * T + T],
                                  y_spec[:, k // 2, k % 2, j * P:j * P + P], dft[:, 2 + k // 2, k % 2],
                                  start=k == 0, stop=k == 3)
            m.then_inc(y_inv, 1)
            g0 = FIRST["ada2"]
            pe.wait_ge(lo_ready, 2 * (g0 - SPLIT0 + KC * (n + 1)))
            for k in range(KC):
                pe.matmul(psum[:, 7, KC * n + k:KC * n + k + 1], ada_acc[:, n, k * P:k * P + P], const[:, ONES, 0:1],
                          start=True, stop=True).then_inc(half_done, 2)

        def group_norm_pe(n):
            pe.wait_ge(gn_sq, n + 1)
            for k in range(8):
                m = pe.matmul(psum[:, 4 * n + k // 2, (k % 2) * T:(k % 2) * T + T], sq(ONES), gn_q[:, k],
                              start=True, stop=True)
            m.then_inc(gn_sum, 1)

        group_norm_pe(0)
        pe.wait_ge(gn_out, 1)
        linear("out1", h_hi, h_lo)
        norm_pe("x2")

        def up_down_pe(g0, bank0, acc0, hid0, supers, after):
            def moving(j, k):
                if j == 0 and k % 4 == 0:
                    pe.wait_ge(norm_lo, 4 * NS[after] + k // 4 + 1)
                return h_hi[:, k]

            with pe.Fori(0, supers) as i:
                for j in range(8):
                    pe.wait_ge(bank_free, i * 8 + (bank0 + j + 1))
                    for h in range(2):
                        half(i * 16 + (g0 + j), j % RING, h, lambda c: h == 0 and c == 0, lambda c: h == 1 and c == 7,
                             lambda c: psum[:, j % 4, 0:T], lambda c: moving(j, h * 8 + c),
                             lambda c: h_lo[:, h * 8 + c])
                for j in range(8):
                    for h in range(2):
                        pe.wait_ge(acc_free, i * 16 + (acc0 + 2 * j + h + 1))

                        def hidden(c):
                            if j == 0 and h == 0:
                                pe.wait_ge(hid_ready, i * 8 + (hid0 + c + 1))
                            return hid_hi[:, c]
                        half(i * 16 + (g0 + 8 + j), j % RING, h, lambda c: c == 0, lambda c: c == 7,
                             lambda c: psum[:, 4 + (2 * j + h) % 4, 0:T], hidden, lambda c: hid_lo[:, c])

        up_down_pe(FIRST["mlp"], bank_of["mlp"], 0, HID0, dict(STREAM)["mlp"] // 16, "x2")
        norm_pe("f1")

        norm_pe("mix")
        linear("ret", h_hi, h_lo, after="mix")

        def rotate_pe(src, perm, n0, pairs):
            for n in range(pairs):
                if n >= 2:
                    pe.wait_ge(rot_d, n0 + n - 1)
                pe.matmul(psum[:, n % 2, :], sq(perm), src[:, 2 * n:2 * n + 2].rearrange("p k t -> p (k t)"),
                          start=True, stop=True).then_inc(rot_p, 1)

        def turn_v_pe(src, heads, n0):
            for n in range(heads // 2):
                tb, g = n % 2, n // 2
                if n >= 2:
                    pe.wait_ge(v_nat_, n0 + n - 1)
                for k in range(4):
                    m = pe.transpose(psum[:, 2 + n % 2, k * P:k * P + P], src[:, 4 * g + k, tb * P:tb * P + P], sq(IDENT))
                m.then_inc(v_tp, 1)

        pe.wait_ge(bank_free, 4 + bank_of["dil"])
        rotate_pe(pr[:], PERM_RET, 0, 8)
        turn_v_pe(pr[:, 16:24], 8, 0)
        pe.wait_ge(rot_d, 8)
        pe.wait_ge(v_nat_, 4)
        for h in range(RET_H + 1):
            if h < RET_H:
                if h >= 2:
                    pe.wait_ge(r_p, h - 1)
                o = psum[:, 4 + h % 2, :]
                pe.matmul(o[:, 0:T], pr[:, 8 + h, 0:P], pr[:, h], start=True, stop=True)
                pe.matmul(o[:, T:T + P], pr[:, 8 + h, P:], pr[:, h, P:], start=True, stop=True).then_inc(r_sc, 1)
            if h >= 1:
                e = h - 1
                pe.wait_ge(r_p, e + 1)
                if e >= 2:
                    pe.wait_ge(r_oc, e - 1)
                o = psum[:, 6 + e % 2, :]
                pe.matmul(o[:, 0:T], v_ret[:, 0, e], ret_p[:, e % 2, 0:T], start=True, stop=False, skip_group_check=True)
                pe.matmul(o[:, P:T], v_ret[:, 1, e], ret_p[:, e % 2, T:], start=False, stop=True,
                          skip_group_check=True).then_inc(r_o, 1)
        group_norm_pe(1)
        linear("dil", h_hi, h_lo)
        pe.wait_ge(bank_free, 4 + bank_of["gate"])
        rotate_pe(pd[:], PERM_ROT, 8, 12)
        turn_v_pe(pd[:, 24:36], 12, 4)
        pe.wait_ge(rot_d, 20)
        pe.wait_ge(v_nat_, 10)

        def dil_scores(m_):
            h, tb = m_ // 2, m_ % 2
            keys = P * (tb + 1)
            b = 4 + 2 * (m_ % 2)
            if m_ >= 2:
                pe.wait_ge(d_mx, m_ - 1)
            for g in range(DIL_G):
                o = flat[:, 512 * b + T * g:512 * b + T * g + keys]
                m = pe.matmul(o, pd[:, 4 * g + h, tb * P:tb * P + P], pd[:, 12 + 4 * g + h, 0:keys], start=True, stop=True)
            m.then_inc(d_sc, 1)

        dil_scores(0)
        for m_ in range(2 * DIL_HG):
            h, tb = m_ // 2, m_ % 2
            if m_ + 1 < 2 * DIL_HG:
                dil_scores(m_ + 1)
            pe.wait_ge(d_p, m_ + 1)
            for g in range(DIL_G):
                for s in range(tb + 1):
                    n = g * (tb + 1) + s
                    m = pe.transpose(flat[:, n * P:n * P + P], dil_s[:, m_ % 2, T * g + P * s:T * g + P * s + P],
                                     sq(IDENT))
            m.then_inc(d_tp, 1)
            pe.wait_ge(d_pt, m_ + 1)
            if tb == 0 and h >= 2:
                pe.wait_ge(d_lo, h - 1)
            last = DIL_G * (tb + 1) - 1
            for n in range(last + 1):
                g, s = n // (tb + 1), n % (tb + 1)
                m = pe.matmul(psum[:, 2 + h % 2, tb * P:tb * P + P], v_dil[:, s, 4 * g + h], dil_pt[:, n],
                              start=n == 0, stop=n == last)
            m.then_inc(d_o, 1)
        pe.wait_ge(d_lo, DIL_HG)
        linear("gate", h_hi, h_lo)
        g0 = FIRST["br_ret"]
        with pe.Fori(0, KC // 2 // RING) as i:
            for j in range(RING):
                for h in range(2):
                    pe.wait_ge(bank_free, i * 8 + (bank_of["br_ret"] + 2 * j + h + 1))
                    half(i * RING + (g0 + j), j, h, lambda c: c == 0, lambda c: c == 7,
                         lambda c: psum[:, (2 * j + h) % 4, 0:T], lambda c: ret_hi[:, c], lambda c: ret_lo[:, c])
        g0 = FIRST["br_dil"]
        for j in range(RING):
            for h in range(2):
                def target(c):
                    if c % 4 == 0:
                        pe.wait_ge(bank_free, bank_of["br_dil"] + 4 * j + 2 * h + c // 4 + 1)
                    return psum[:, 2 * h + c // 4, 0:T]
                half(g0 + j, j, h, lambda c: c % 4 == 0, lambda c: c % 4 == 3, target,
                     lambda c: dil_hi[:, c % 4], lambda c: dil_lo[:, c % 4])
        norm_pe("mem")
        pe.wait_ge(merged, 1)
        linear("out2", h_hi, h_lo)

        pe.wait_ge(norm_lo, 4 * NS["mem"] + 4)
        linear("kv", mem_hi, mem_lo, 0, KC)
        norm_pe("cross")
        linear("kv", mem_hi, mem_lo, KC, KC)
        linear("q", h_hi, h_lo, after="cross")
        pe.wait_ge(bank_free, 4 + bank_of["o"])
        for n in range(8):
            mb, g = n % 2, n // 2
            if n >= 2:
                pe.wait_ge(m_vn, n - 1)
            for k in range(4):
                m = pe.transpose(psum[:, n % 2, k * P:k * P + P], kv[:, KC + 4 * g + k, mb * P:mb * P + P], sq(IDENT))
            m.then_inc(m_tp, 1)
        pe.wait_ge(m_vn, 8)

        def mem_scores(h):
            if h >= 2:
                pe.wait_ge(m_e, h - 1)
            for tb in range(2):
                for c in range(4):
                    m = pe.matmul(psum[:, 4 + h % 2, tb * T:tb * T + T], q_mem[:, 4 * h + c, tb * P:tb * P + P],
                                  kv[:, 4 * h + c], start=c == 0, stop=c == 3)
            m.then_inc(m_sc, 1)

        mem_scores(0)
        for h in range(MEM_H):
            if h + 1 < MEM_H:
                mem_scores(h + 1)
            pe.wait_ge(m_p, h + 1)
            if h >= 2:
                pe.wait_ge(m_pc, h - 1)
            for mb in range(2):
                for tb in range(2):
                    m = pe.transpose(psum[:, h % 2, mb * T + tb * P:mb * T + tb * P + P],
                                     mem_e[:, h % 2, tb, mb * P:mb * P + P], sq(IDENT))
            m.then_inc(m_pt_, 1)
            pe.wait_ge(m_pc, h + 1)
            if h >= 1:
                pe.wait_ge(m_lo, h)
            for c in range(4):
                for mb in range(2):
                    m = pe.matmul(psum[:, 2 + c // 2, (c % 2) * T:(c % 2) * T + T], v_mem[:, mb, 4 * h + c],
                                  mem_pt[:, h % 2, mb], start=mb == 0, stop=mb == 1)
            m.then_inc(m_o, 1)
        pe.wait_ge(m_lo, MEM_H)
        linear("o", h_hi, h_lo)

        norm_pe("ffn")
        linear("pq", h_hi, h_lo, after="ffn")
        pe.wait_ge(s_aux[5], 16)
        pe.wait_ge(bank_free, 4 + bank_of["peer"])
        for tb in range(2):
            for k in range(16):
                m = pe.matmul(psum[:, 4 * tb + k // 4, (k % 4) * P:(k % 4) * P + P], q_peer[:, k, tb * P:tb * P + P],
                              subkeys[:, k], start=True, stop=True)
            m.then_inc(p_sc, 1)
        pe.wait_ge(p_scc, 2)

        def up_pe(q, first, tiles, groups):
            g0 = FIRST["peer"] + 2 * QUARTER * q + first
            bank0 = bank_of["peer"] + QUARTER * q + first

            def gate_group(i, j, r):
                n, b = i * (RING * groups) + (32 * q + j * groups + r), (j * groups + r) % 2
                pe.wait_ge(e_oh, n + 2)
                pe.wait_ge(e_gc, n + 1)
                for t in range(8):
                    m = pe.matmul(psum[:, 4 + b, 2 * QUARTER * t:2 * QUARTER * (t + 1)], hot2[:, b, t],
                                  hot1[:, b, :, t], start=True, stop=True)
                m.then_inc(e_g, 1)

            with pe.Fori(0, tiles // RING) as i:
                for j in range(RING):
                    pe.wait_ge(bank_free, i * RING + (bank0 + j + 1))
                    for h in range(2):
                        half(i * RING + (g0 + j), j, h, lambda c: h == 0 and c == 0,
                             lambda c: h == 1 and c == KC // 2 - 1, lambda c: psum[:, j, 0:T],
                             lambda c: h_hi[:, h * 8 + c], lambda c: h_lo[:, h * 8 + c])
                        for r in range((groups * h + 1) // 2, (groups * (h + 1) + 1) // 2):
                            gate_group(i, j, r)

        def down_pe(q):
            g0 = FIRST["peer"] + 2 * QUARTER * q + QUARTER
            with pe.Fori(0, QUARTER // 8) as i:
                for s in range(2):
                    for j in range(RING):
                        for h in range(2):
                            n = 8 * s + 2 * j + h
                            pe.wait_ge(acc_free, i * 16 + (n_acc["peer"] + 64 * q + n + 1))

                            def hidden(c):
                                if j == 0 and h == 0 and c < 4:
                                    pe.wait_ge(hid_ready, i * 8 + (HID0 + MLP_H + QUARTER * q + 4 * s + c + 1))
                                return hid_hi[:, 4 * s + c % 4]
                            half(i * 8 + (g0 + 4 * s + j), j, h, lambda c: c % 4 == 0, lambda c: c % 4 == 3,
                                 lambda c: psum[:, 4 + n % 4, (c // 4) * T:(c // 4) * T + T], hidden,
                                 lambda c: hid_lo[:, 4 * s + c % 4])

        up_pe(0, 0, EARLY, 0)
        pe.wait_ge(p_tab, 1)
        for tb in range(2):
            for k in range(3):
                m = pe.transpose(psum[:, 6 + tb, k * P:k * P + P], chosen[:, k, tb].rearrange("p h r -> p (h r)"),
                                 sq(IDENT))
        m.then_inc(p_tt, 1)
        up_pe(0, EARLY, QUARTER - EARLY, 32 // (QUARTER - EARLY))
        down_pe(0)
        for q in range(1, 4):
            pe.wait_ge(acc_free, 4 + n_acc["peer"] + 64 * q)
            up_pe(q, 0, QUARTER, 1)
            down_pe(q)
        norm_pe("f2")

    @block.scalar
    def _(act):
        st = Steps(act, act_step)

        def split_half(g, s, h):
            act.wait_ge(half_done, g * 2 + (h - 3))
            k = slice(h * KC // 2, (h + 1) * KC // 2)
            act.activation(w_hi[:, 2 * (s % 2) + h], ring[:, s, k], ACT.Copy).then_inc(hi_ready, 1)

        def split_tile(g, turn, s):
            act.wait_ge(landed[s], turn * 16 + 16)
            split_half(g, s, 0)
            split_half(g, s, 1)

        def split_stage(name, first=0, n=None, ahead=0):
            g0, n = FIRST[name] + first, n or dict(STREAM)[name]
            for s in range(ahead, RING if ahead else 0):
                split_tile(g0 + s, g0 // RING, s)
            with act.Fori(1 if ahead else 0, n // RING) as i:
                for s in range(RING):
                    split_tile(i * RING + (g0 + s), i + g0 // RING, s)

        def norm_act(name, src, shift=None, split=True, ready=None, ahead=None):
            n = NI[name]
            if shift is None:
                shift = lambda k: col("zero", k)
            for q in range(4):
                if ready is not None:
                    act.wait_ge(*ready(q))
                if q == 2:
                    act.wait_ge(norm_half, 2 * n + 1)
                act.activation(ntmp[:, q % 2], src[:, 4 * q:4 * q + 4], ACT.Square).then_inc(norm_sq, 1)
            if ahead is not None:
                split_tile(ahead, ahead // RING, 0)
            act.wait_ge(norm_ms, n + 1)
            act.activation(nrt[:], nrt[:], ACT.Sqrt).then_inc(norm_rt, 1)
            if ahead is not None:
                split_tile(ahead + 1, ahead // RING, 1)
            if not split:
                return
            for q in range(4):
                act.wait_ge(norm_t, 4 * NS[name] + q + 1)
                for k in range(4):
                    m = act.activation(norm_to.get(name, (h_hi, h_lo))[0][:, 4 * q + k], ntmp[:, q % 2, k], ACT.Identity,
                                       bias=shift(4 * q + k))
                m.then_inc(norm_hi, 1)

        act.dma_start(ctx_raw[:], a["ctx"]).then_inc(norm_in, 16)
        act.dma_start(x[:], a["x"]).then_inc(norm_in, 16)
        act.dma_start(dt_bias[:], a["dt_bias"]).then_inc(s_aux[0], 16)
        act.dma_start(a_log[:], a["a_log"]).then_inc(s_aux[0], 16)
        act.wait_ge(s_const, 48)
        act.activation(c_silu[:], c_raw[:], ACT.Silu).then_inc(s_csilu, 1)
        act.wait_ge(s_aux[0], 32)
        act.activation(a_exp[:], a_log[:], ACT.Exp).then_inc(act_step, 1)
        st.n = 1
        act.wait_ge(norm_in, 32)
        act.wait_ge(s_mod, 1)
        norm_act("ctx", ctx_raw, lambda k: mod[:, k, 1:2])
        act.wait_ge(norm_lo, 4 * NS["ctx"] + 4)
        norm_act("x1", x, lambda k: mod[:, k, 0:1], ahead=FIRST["xbc"])
        act.wait_ge(norm_lo, 4 * NS["x1"] + 4)
        act.dma_start(wdt[:], a["wdt"]).then_inc(s_aux[1], 16)
        act.wait_ge(s_aux[1], 16)
        act.activation(wdt_s[:, :, 0], wdt[:], ACT.Copy).then_inc(wdt_h, 1)
        split_stage("xbc", ahead=2)
        split_stage("hy")
        split_stage("z")
        act.wait_ge(bank_free, 4 + bank_of["hy"])
        act.activation(xbc[:], xbc[:], ACT.Silu).then_inc(s_silu, 1)
        rows_scaled = [0]

        def scale_rows(tiles):
            for n in range(rows_scaled[0], rows_scaled[0] + tiles):
                g = FIRST["ada2"] + n
                w = ring[:, g % RING].rearrange("p k n -> p (k n)")
                act.wait_ge(landed[g % RING], 16 * (g // RING + 1))
                act.activation(w, w, ACT.Copy, scale=c_silu[:, n % KC, 0:1]).then_inc(ada_scaled, 1)
            rows_scaled[0] += tiles

        act.wait_ge(dt_nab, 1)
        act.activation(dt_w[:, 1], dt_w[:, 1], ACT.Exp).then_inc(dt_e, 1)
        act.wait_ge(cs_wd, 1)
        act.activation(wd[:], wd[:], ACT.Exp).then_inc(cs_wx, 1)
        for hh in range(HEADS):
            act.wait_ge(hd_d, hh + 1)
            act.activation(decay[:, hh % 2], decay[:, hh % 2], ACT.Exp).then_inc(act_step, 1)
            if hh >= 2:
                act.wait_ge(hd_m, hh - 1)
            act.activation(off_e[:, hh % 2], psum[:, hh % 2, :], ACT.Exp).then_inc(hd_o, 1)
            st.n += 1
            scale_rows(1 + hh % 2)
        act.activation(z[:], z[:], ACT.Silu).then_inc(g_z, 1)
        act.wait_ge(hd_y, HEADS)
        act.wait_ge(hd_m, HEADS)
        act.dma_start(filt_w12[0:FEATS, 0:FILT], a["filt_w1"]).then_inc(f_in, 16)
        act.dma_start(filt_w12[:, FILT:], a["filt_w2"]).then_inc(f_in, 16)
        act.dma_start(filt_cols[:], a["filt_cols"]).then_inc(f_in, 16)
        act.dma_start(feats[:], a["feats"]).then_inc(f_in, 16)
        act.dma_start(filt_w3[:], a["filt_w3"]).then_inc(f_in, 16)
        act.dma_start(dft[:], a["dft"]).then_inc(f_in, 16)
        act.dma_start(window[:], a["window"]).then_inc(s_aux[2], 16)
        act.wait_ge(g_y, 1)
        act.activation(y_sq[:], y_ssd[:], ACT.Square).then_inc(g_sq, 1)
        act.wait_ge(g_ms, 1)
        act.activation(g_rt[:], g_rt[:], ACT.Sqrt).then_inc(g_srt, 1)
        scale_rows(4)

        for n in range(2):
            act.wait_ge(f_arg, n + 1)
            act.activation(hdn[:, n], sin_a[0:FILT], ACT.Sin).then_inc(f_sin, 1)
            scale_rows(2)
        for n in range(4):
            act.wait_ge(y_k, n + 1)
            act.activation(k_spec[:].rearrange("p r f c -> p (r f c)"), flat[:, 0:2048], ACT.Copy).then_inc(y_kc, 1)
            scale_rows((10, 10, 12, 0)[n])

        def group_norm_act(n, src):
            act.wait_ge(gn_in, n + 1)
            act.activation(gn_q[:], src, ACT.Square).then_inc(gn_sq, 1)
            split_tile(FIRST["out1"], FIRST["out1"] // RING, 0)
            act.wait_ge(gn_ms, n + 1)
            act.activation(gn_r[:], gn_r[:], ACT.Sqrt).then_inc(gn_rt, 1)
            split_tile(FIRST["out1"] + 1, FIRST["out1"] // RING, 1)

        group_norm_act(0, u[:, 0:8])
        act.dma_start(x[:], a["x"]).then_inc(x_back, 16)
        split_stage("out1", ahead=2)
        act.wait_ge(s_mod, 2)
        norm_act("x2", x, lambda k: mod[:, 3 * KC + k, 0:1],
                 ready=lambda q: (bank_free, 4 + bank_of["out1"] + 4 * (q + 1)), ahead=FIRST["mlp"])

        def up_down_act(g0, supers):
            for j in range(2, 16):
                split_tile(g0 + j, (g0 + j) // 4, j % RING)
            with act.Fori(1, supers) as i:
                for j in range(16):
                    split_tile(i * 16 + (g0 + j), i * 4 + (g0 + j) // 4, j % RING)

        up_down_act(FIRST["mlp"], dict(STREAM)["mlp"] // 16)
        act.wait_ge(acc_free, 4 + n_acc["peer"])
        norm_act("f1", x, split=False)

        act.dma_start(ret_decay[:], a["ret_decay"]).then_inc(s_aux[3], 16)
        norm_act("mix", x, ready=lambda q: (plain_done, q + 1), ahead=FIRST["ret"])
        act.dma_start(pos_i[:], a["pos"]).then_inc(s_aux[4], 16)
        for n in range(2):
            act.wait_ge(t_arg, n + 1)
            act.activation(trig[:, 2 * n], sin_a[:], ACT.Sin)
            act.activation(t_half[:], sin_a[:], ACT.Sin, scale=0.5).then_inc(t_sin, 1)
        split_stage("ret", ahead=2)
        act.wait_ge(bank_free, 4 + bank_of["dil"])
        act.activation(pr[:, 24:32], pr[:, 24:32], ACT.Silu).then_inc(r_g, 1)
        for h in range(RET_H):
            act.wait_ge(r_o, h + 1)
            act.activation(pr[:, h], psum[:, 6 + h % 2, 0:T], ACT.Copy).then_inc(r_oc, 1)
        act.wait_ge(r_oc, RET_H)
        act.activation(gn_q[:], pr[:, 0:8], ACT.Square).then_inc(gn_sq, 1)
        split_tile(FIRST["dil"], FIRST["dil"] // RING, 0)
        act.wait_ge(gn_ms, 2)
        act.activation(gn_r[:], gn_r[:], ACT.Sqrt).then_inc(gn_rt, 1)
        for s in range(1, RING):
            split_tile(FIRST["dil"] + s, FIRST["dil"] // RING, s)
        act.wait_ge(gn_out, 2)
        act.dma_start(dil_mask[:], a["dil_mask"]).then_inc(s_aux[3], 16)
        split_stage("dil", ahead=RING)
        for m_ in range(2 * DIL_HG):
            h, tb = m_ // 2, m_ % 2
            keys = P * (tb + 1)
            act.wait_ge(d_mx, m_ + 1)
            s, n = (t_[:, m_ % 2] for t_ in (dil_s, dil_n))
            s = s.rearrange("p (g k) -> p g k", g=DIL_G)[:, :, 0:keys]
            act.activation(s, s, ACT.Exp, bias=n[:, 0:1], accum_out=n[:, 1:2]).then_inc(d_e, 1)
            if tb == 1:
                act.wait_ge(d_o, m_ + 1)
                act.activation(dil_hi[:, h], psum[:, 2 + h % 2, 0:T], ACT.Copy).then_inc(d_hi, 1)
        act.wait_ge(d_lo, DIL_HG)
        act.dma_start(mem_raw[:], a["mem"]).then_inc(norm_in, 16)
        split_stage("gate")
        act.wait_ge(bank_free, 4 + bank_of["br_ret"])
        act.activation(pg[:], pg[:], ACT.Sigmoid).then_inc(s_sig, 1)
        split_stage("br_ret")
        split_stage("br_dil")
        act.wait_ge(norm_in, 48)
        act.wait_ge(half_done, 2 * FIRST["br_dil"])
        norm_act("mem", mem_raw, ahead=FIRST["out2"])
        split_stage("out2", ahead=2)
        split_stage("kv", 0, KC)
        act.wait_ge(bank_free, 4 + bank_of["kv"])
        norm_act("cross", x, ahead=FIRST["kv"] + KC)
        split_stage("kv", KC, KC, ahead=2)
        split_stage("q")
        for h in range(MEM_H):
            act.wait_ge(m_mx, h + 1)
            for tb in range(2):
                m = act.activation(mem_e[:, h % 2, tb], psum[:, 4 + h % 2, tb * T:tb * T + T], ACT.Exp,
                                   bias=mem_n[:, h % 2, tb:tb + 1], scale=(D // MEM_H) ** -0.5,
                                   accum_out=mem_n[:, h % 2, 2 + tb:3 + tb])
            m.then_inc(m_e, 1)
            act.wait_ge(m_o, h + 1)
            act.activation(h_hi[:, 4 * h:4 * h + 4].rearrange("p k t -> p (k t)"), flat[:, 1024:2048],
                           ACT.Copy).then_inc(m_hi, 1)
        act.wait_ge(m_lo, MEM_H)
        act.dma_start(subkeys[:], a["subkeys"]).then_inc(s_aux[5], 16)
        split_stage("o")
        norm_act("ffn", x, ready=lambda q: (bank_free, 4 + bank_of["o"] + 4 * (q + 1)), ahead=FIRST["pq"])
        split_stage("pq", ahead=2)
        for tb in range(2):
            act.wait_ge(p_sc, tb + 1)
            act.activation(psc[:, tb].rearrange("p k n -> p (k n)"), flat[:, 2048 * tb:2048 * tb + 2048],
                           ACT.Copy).then_inc(p_scc, 1)

        def up_act(q, first, tiles):
            g0 = FIRST["peer"] + 2 * QUARTER * q + first

            def gelu(i, j):
                act.wait_ge(half_done, i * 8 + (2 * (g0 + j) + 2))
                act.activation(before[:, bass.ds(i * RING + (first + j), 1)].rearrange("p a t -> p (a t)"),
                               psum[:, j % RING, 0:T], ACT.Gelu).then_inc(bank_free, 1)

            def split(i, j):
                split_tile(i * RING + (g0 + j), i + (g0 + j) // RING, (g0 + j) % RING)

            split(0, 0)
            split(0, 1)
            with act.Fori(0, tiles // RING - 1) as i:
                for j in range(RING):
                    split(i, j + 2)
                    gelu(i, j)
            for j in range(RING):
                if j < 2:
                    split(tiles // RING - 1, j + 2)
                gelu(tiles // RING - 1, j)

        def down_act(q):
            g0 = FIRST["peer"] + 2 * QUARTER * q + QUARTER
            with act.Fori(0, QUARTER // RING) as i:
                for s in range(RING):
                    split_tile(i * RING + (g0 + s), i + g0 // RING, s)

        up_act(0, 0, EARLY)
        act.wait_ge(p_cv, 1)
        act.activation(chosen[:, 2], chosen[:, 2], ACT.Exp).then_inc(p_ge, 1)
        up_act(0, EARLY, QUARTER - EARLY)
        down_act(0)
        for q in range(1, 4):
            act.wait_ge(hid_ready, HID0 + MLP_H + QUARTER * q)
            up_act(q, 0, QUARTER)
            down_act(q)
        act.wait_ge(acc_free, 4 + n_acc["peer"] + 256)
        norm_act("f2", x, split=False)

    @block.vector
    def _(dve):
        st = Steps(dve, dve_step)

        def norm_half_sum(name, s):
            dve.wait_ge(norm_sq, 4 * NI[name] + 2 * s + 2)
            dve.tensor_reduce(norm_part[:, s], ntmp[:].rearrange("p q k t -> p t (q k)"), AX.X, ALU.add
                              ).then_inc(norm_half, 1)

        def norm_dve(name, src, scale, shift=None, plain=None, summed=0):
            n = NI[name]
            if shift is None:
                shift = lambda k: col("zero", k)
            hi, lo = norm_to.get(name, (h_hi, h_lo))
            for s in range(summed, 2):
                norm_half_sum(name, s)
            dve.wait_ge(norm_sum, n + 1)
            dve.tensor_scalar(nrt[:], psum[:, 7, 0:T], 1.0 / D, EPS, ALU.mult, ALU.add).then_inc(norm_ms, 1)
            dve.wait_ge(norm_rt, n + 1)
            st.did(dve.reciprocal(nrstd[:], nrt[:]))
            st.settle()
            if plain is not None:
                for k in range(KC):
                    m = dve.scalar_tensor_tensor(plain[:, k], src[:, k], scale(k), nrstd[:], ALU.mult, ALU.mult)
                    if k % 4 == 3:
                        m.then_inc(plain_done, 1)
                return

            def low(q):
                dve.wait_ge(norm_hi, 4 * NS[name] + q + 1)
                for k in range(4):
                    m = dve.scalar_tensor_tensor(lo[:, 4 * q + k], ntmp[:, q % 2, k], shift(4 * q + k),
                                                 hi[:, 4 * q + k].bitcast(F32), ALU.add, ALU.subtract)
                m.then_inc(norm_lo, 1)

            for q in range(4):
                if q >= 2:
                    low(q - 2)
                    dve.wait_ge(norm_lo, 4 * NS[name] + q - 1)
                for k in range(4):
                    m = dve.scalar_tensor_tensor(ntmp[:, q % 2, k], src[:, 4 * q + k], scale(4 * q + k), nrstd[:],
                                                 ALU.mult, ALU.mult)
                m.then_inc(norm_t, 1)
            low(2)
            low(3)

        def copy_stage(name, dst, d0=0):
            g0, n = FIRST[name], dict(STREAM)[name]
            with dve.Fori(0, n // RING) as i:
                for j in range(RING):
                    dve.wait_ge(half_done, i * 8 + (2 * (g0 + j) + 2))
                    dve.tensor_copy(dst[:, bass.ds(i * RING + (d0 + j), 1)].rearrange("p a t -> p (a t)"),
                                    psum[:, j, 0:T]).then_inc(bank_free, 1)

        def copy_part(name, dst, first, n, norm=None):
            g0 = FIRST[name] + first

            def copy(i, j):
                dve.wait_ge(half_done, i * 8 + (2 * (g0 + j) + 2))
                dve.tensor_copy(dst[:, bass.ds(i * RING + (first + j), 1)].rearrange("p a t -> p (a t)"),
                                psum[:, j, 0:T]).then_inc(bank_free, 1)

            with dve.Fori(0, n // RING - 1) as i:
                for j in range(RING):
                    copy(i, j)
            for j in range(RING):
                if j == 2 and norm is not None:
                    norm_half_sum(norm, 0)
                copy(n // RING - 1, j)

        def conv_tile(i, j, g, dst, w, b, nb, both):
            k = i * RING + j
            dve.wait_ge(half_done, i * 8 + (2 * (g + j) + 2))
            width = 2 * T if both else T
            src = psum[:, j, 0:width]
            n0 = k * (4 if both else 2) + conv_base[0]
            dve.tensor_scalar(dst, src, col(w, k + nb), col(b, k), ALU.mult, ALU.add).then_inc(dve_step, 1)
            pieces = [(dst[:, 0:T].rearrange("p (r w) -> p r w", w=GRID_W),
                       src[:, 0:T].rearrange("p (r w) -> p r w", w=GRID_W), GRID_W)]
            if both:
                pieces.append((dst[:, T:].rearrange("p (r w) -> p r w", w=T),
                               src[:, T:].rearrange("p (r w) -> p r w", w=T), T))
            step = 1
            for out_, in_, w_ in pieces:
                for tap in (0, 2):
                    dve.wait_ge(dve_step, n0 + step)
                    o, s = ((out_[:, :, 1:w_], in_[:, :, 0:w_ - 1]), None, (out_[:, :, 0:w_ - 1], in_[:, :, 1:w_]))[tap]
                    last = tap == 2 and w_ == pieces[-1][2]
                    dve.scalar_tensor_tensor(o, s, col(w, k + tap * nb), o, ALU.mult, ALU.add).then_inc(
                        bank_free if last else dve_step, 1)
                    step += 1

        conv_base = [0]
        def pair_out(j):
            dve.wait_ge(hd_y, 2 * j + 2)
            dve.scalar_tensor_tensor(y_ssd[:, j], xbc[:, j, 0], col("ssd_d", j), psum[:, 4 + j % 2, 0:T],
                                     ALU.mult, ALU.add).then_inc(hd_yc, 1)

        for b in range(8):
            dve.memset(psum[:, b, :], 0.0).then_inc(bank_free if b < 4 else acc_free, 1)
        dve.memset(hid[:], 0.0).then_inc(hid_ready, HID0)
        dve.wait_ge(acc_free, 4)
        for b in range(2):
            dve.memset(psum[:, 4 + b, :], 0.0).then_inc(ada_copied, 1)
        dve.wait_ge(s_const, 48)
        with dve.Fori(0, ADA_G // 2) as i:
            for b in range(2):
                dve.wait_ge(half_done, i * 16 + (8 * b + 8))
                dve.tensor_copy(mod_rows[:, bass.ds(i * 1024 + 512 * b, 512)], psum[0:2, 4 + b, :]).then_inc(ada_copied, 1)
        dve.wait_ge(ada_turned, 1)
        dve.tensor_tensor(mod[:, 0:ADA_1], psum[:, 6, 0:2 * ADA_1].rearrange("p (n c) -> p n c", c=2),
                          col("b_ada", 0, ADA_1).unsqueeze(2).broadcast_to([P, ADA_1, 2]), ALU.add).then_inc(s_mod, 1)
        dve.wait_ge(s_mod, 1)
        for side in range(2):
            st.did(dve.scalar_tensor_tensor(scales[:, side], mod[:, KC:2 * KC, side], 1.0, col("norm1", 0, KC),
                                            ALU.add, ALU.mult))
        st.settle()
        norm_dve("ctx", ctx_raw, lambda k: scales[:, 1, k:k + 1], lambda k: mod[:, k, 1:2])
        norm_dve("x1", x, lambda k: scales[:, 0, k:k + 1], lambda k: mod[:, k, 0:1])

        conv_base[0] = st.n
        with dve.Fori(0, XBC // RING) as i:
            for j in range(RING):
                conv_tile(i, j, FIRST["xbc"], xbc[:, bass.ds(i * RING + j, 1)].rearrange("p a s t -> p (a s t)"),
                          "ssd_w", "ssd_b", XBC, True)
        st.n += 4 * XBC
        dve.wait_ge(wdt_h, 1)
        dve.tensor_tensor(wdt_s[:, :, 1], wdt[:], wdt_s[:, :, 0].bitcast(F32), ALU.subtract).then_inc(wdt_split, 1)
        dve.wait_ge(dt_sum, 1)
        conv_base[0] = st.n
        with dve.Fori(0, HYENA // RING) as i:
            for j in range(RING):
                conv_tile(i, j, FIRST["hy"], u[:, bass.ds(i * RING + j, 1)].rearrange("p a t -> p (a t)"),
                          "hy_w", "hy_b", HYENA, False)
        st.n += 2 * HYENA
        copy_stage("z", z)

        v, e, w2, w3 = (dt_w[:, n] for n in range(4))
        dt_ps = psum[:, 5, 0:2 * P].rearrange("p (b s h) -> p b s h", s=2, h=32)
        st.did(dve.tensor_tensor(v, dt_ps[:, :, 0], dt_bias[:].unsqueeze(1).broadcast_to([P, 4, 32]), ALU.add))
        st.settle()
        st.did(dve.tensor_tensor(v, dt_ps[:, :, 1], v, ALU.add))
        st.settle()
        dve.scalar_tensor_tensor(e, v, -1.0, v, ALU.mult, ALU.min).then_inc(dt_nab, 1)
        dve.wait_ge(dt_e, 1)
        st.did(dve.tensor_scalar(w2, e, 2.0, None, ALU.add))
        st.settle()
        st.did(dve.reciprocal(w3, w2))
        st.settle()
        st.did(dve.tensor_tensor(dt_u[:], e, w3, ALU.mult))
        st.settle()
        st.did(dve.tensor_tensor(w2, dt_u[:], dt_u[:], ALU.mult))
        st.settle()
        st.did(dve.tensor_scalar(dt_p[:], w2, 1.0 / 17, None, ALU.mult))
        for k in (15, 13, 11, 9, 7, 5, 3):
            st.settle()
            st.did(dve.scalar_tensor_tensor(dt_p[:], dt_p[:], 1.0 / k, w2, ALU.add, ALU.mult))
        st.settle()
        st.did(dve.scalar_tensor_tensor(dt_p[:], dt_p[:], 1.0, dt_u[:], ALU.add, ALU.mult))
        st.did(dve.tensor_scalar(v, v, 0.0, None, ALU.max))
        st.settle()
        st.did(dve.scalar_tensor_tensor(dt[:], dt_p[:], 2.0, v, ALU.mult, ALU.add))
        st.settle()
        dve.wait_ge(act_step, 1)
        dve.scalar_tensor_tensor(da[:], dt[:], -1.0, a_exp[:].unsqueeze(1).broadcast_to([P, 4, 32]),
                                 ALU.mult, ALU.mult).then_inc(dt_ready, 1)
        for n in range(8):
            tb, q = n // 2, n % 2
            dve.wait_ge(ssd_tp, n + 1)
            dve.tensor_copy(xs_nat[:, tb, 4 * q:4 * q + 4].rearrange("p k c -> p (k c)"),
                            psum[:, n % 2, :]).then_inc(ssd_tpc, 1)
        dve.wait_ge(ssd_tp, 9)
        dve.tensor_copy(b_nat[:].rearrange("p g b c -> p (g b c)"), psum[:, 0, :]).then_inc(ssd_tpc, 1)
        dve.wait_ge(cs_sum, 1)
        st.did(dve.tensor_copy(cs[:].rearrange("p b h -> p (b h)"), psum[:, 4, 0:64]))
        dve.tensor_copy(wd[:].rearrange("p b h -> p (b h)"), psum[:, 4, 64:128]).then_inc(cs_wd, 1)
        dve.wait_ge(cs_wx, 1)
        st.did(dve.tensor_tensor(wd[:], wd[:], dt[:, 2:4], ALU.mult))
        dve.wait_ge(ssd_tpc, 9)
        st.settle()
        for n in range(4):
            d, g = n // 2, n % 2
            for tb in range(2):
                if n >= 1:
                    dve.wait_ge(ssd_st, 2 * (n - 1) + tb + 1)
                hs = 16 * d + 8 * g
                dve.tensor_tensor(
                    xw[:, tb].rearrange("p (h c) -> p h c", c=HD),
                    xs_nat[:, 2 + tb, 4 * g:4 * g + 4].rearrange("p k c -> p (k c)").rearrange("p (h c) -> p h c", c=HD),
                    wd[:, tb, hs:hs + 8].unsqueeze(2).broadcast_to([P, 8, HD]), ALU.mult).then_inc(ssd_xw, 1)
            dve.wait_ge(ssd_st, 2 * n + 2)
            dve.tensor_copy(state[:, d, g], psum[:, 2 + n % 2, :]).then_inc(ssd_stc, 1)
        for g in range(2):
            dve.wait_ge(ssd_cb, g + 1)
            c_ = cb[:, g]
            p6 = psum[:, 6, :]
            dve.tensor_copy(c_[:, P:T], p6[:, P:T])
            dve.tensor_copy(c_[:, T + P:T + P + P], p6[:, T:T + P])
            for o, s, mask in ((0, 0, LE), (T, T + P, LE), (T + P + P, T + P, GE), (T + P + T, 0, GE)):
                dve.tensor_tensor(c_[:, o:o + P], p6[:, s:s + P], sq(mask), ALU.mult).then_inc(ssd_cbm, 1)
            dve.wait_ge(ssd_cbm, 4 * g + 4)
            for hh in range(8 * g, 8 * g + 8):
                dve.wait_ge(hd_row, hh + 1)
                rw = psum[:, hh % 2, :]
                dc, mm = decay[:, hh % 2], mix_m[:, hh % 2]
                f, b = hh, 16 + hh
                if hh >= 2:
                    dve.wait_ge(hd_y, hh - 1)
                for n, (o, r, wdt_, tb, c0) in enumerate(((0, 0, T, 0, f), (T, P, P, 1, f), (T + P, T, T, 1, b),
                                                          (2 * T + P, T, P, 0, b))):
                    m = dve.tensor_scalar(dc[:, o:o + wdt_], rw[:, r:r + wdt_], cs[:, tb, c0:c0 + 1], 0.0,
                                          ALU.subtract, ALU.min)
                m.then_inc(hd_d, 1)
                dve.wait_ge(hd_o, hh + 1)
                for o, wdt_, tb, c0, dst in ((0, T, 0, f, mm[:, 0:T]), (T + P, T, 1, b, mm[:, T:]),
                                             (T, P, 1, f, mix_t[:, 0:P]), (2 * T + P, P, 0, b, mix_t[:, P:])):
                    st.did(dve.scalar_tensor_tensor(dst, dc[:, o:o + wdt_], dt[:, tb, c0:c0 + 1], c_[:, o:o + wdt_],
                                                    ALU.mult, ALU.mult))
                st.did(dve.tensor_tensor(c_off[:, hh % 2].rearrange("p (d t) -> p d t", t=T),
                                         off_e[:, hh % 2].rearrange("p (d t) -> p d t", t=T),
                                         xbc[:, 10 + g, 0, :].unsqueeze(1).broadcast_to([P, 2, T]), ALU.mult))
                st.settle()
                st.did(dve.tensor_tensor(mm[:, T + P:], mm[:, T + P:], mix_t[:, 0:P], ALU.add))
                dve.tensor_tensor(mm[:, 0:P], mm[:, 0:P], mix_t[:, P:], ALU.add).then_inc(hd_m, 1)
                if hh % 2 == 1 and hh >= 3:
                    pair_out(hh // 2 - 1)
        pair_out(7)
        dve.wait_ge(hd_yc, 8)
        dve.wait_ge(g_z, 1)
        dve.tensor_tensor(y_ssd[:], y_ssd[:], z[:], ALU.mult).then_inc(g_y, 1)
        dve.wait_ge(g_sum, 1)
        dve.tensor_scalar(g_rt[:].rearrange("p g t -> p (g t)"), psum[:, 2, :], 1.0 / 512, EPS, ALU.mult,
                          ALU.add).then_inc(g_ms, 1)
        dve.wait_ge(g_srt, 1)
        st.did(dve.reciprocal(g_rstd[:], g_rt[:]))
        st.settle()
        for k in range(ZB):
            st.did(dve.scalar_tensor_tensor(y_ssd[:, k], y_ssd[:, k], col("ssd_norm", k), g_rstd[:, k // 4],
                                            ALU.mult, ALU.mult))
        st.settle()
        st.did(dve.tensor_copy(h_hi[:, 8:16], y_ssd[:]))
        st.settle()
        dve.tensor_tensor(h_lo[:, 8:16], y_ssd[:], h_hi[:, 8:16].bitcast(F32), ALU.subtract).then_inc(g_out, 1)

        def reduce_angle(rows, signal=f_arg):
            r, k, ki = sin_a[0:rows], sin_k[0:rows], sin_i[0:rows]
            st.settle()
            st.did(dve.tensor_scalar(k, r, 1.0 / TWO_PI, None, ALU.mult))
            st.settle()
            st.did(dve.tensor_copy(ki, k))
            st.settle()
            st.did(dve.tensor_copy(k, ki))
            for part in (PI_A, PI_B, PI_C):
                st.settle()
                st.did(dve.scalar_tensor_tensor(r, k, -part, r, ALU.mult, ALU.add))
            st.settle()
            dve.tensor_scalar(r, r, PI_IN, -PI_IN, ALU.min, ALU.max).then_inc(signal, 1)

        dve.wait_ge(f_in, 96)
        for n in range(2):
            dve.wait_ge(f_dense, n + 1)
            if n:
                dve.wait_ge(f_sin, n)
            st.did(dve.tensor_scalar(sin_a[0:FILT], psum[0:FILT, n, 0:T], filt_cols[:, 2 * n:2 * n + 1],
                                     filt_cols[:, 1:2], ALU.add, ALU.mult))
            reduce_angle(FILT)
        dve.wait_ge(s_aux[2], 16)

        def filter_parts(n):
            q = n // 2
            dve.wait_ge(y_f, n + 1)
            st.did(dve.tensor_tensor(
                filt[:], flat[:, 0:2048].rearrange("p (b s c) -> p b s c", b=2, s=2),
                window[:, :, 512 * q:512 * q + 512].unsqueeze(2).broadcast_to([P, 2, 2, 512]), ALU.mult))
            st.settle()
            st.did(dve.memset(filt[0:1, 0, 1, :], 0.0))
            st.settle()
            st.did(dve.tensor_tensor(filt_sd[:, 0], filt[:, :, 0], filt[:, :, 1], ALU.add))
            st.did(dve.tensor_tensor(filt_sd[:, 1], filt[:, :, 1], filt[:, :, 0], ALU.subtract))
            st.settle()
            least = y_part[:, 0].rearrange("p (b c) -> p b c", b=2)
            st.did(dve.tensor_tensor(least, filt_sd[:, 0], filt_sd[:, 1], ALU.min))
            st.did(dve.tensor_tensor(filt_abs[:], filt_sd[:, 0], filt_sd[:, 1], ALU.max))
            st.settle()
            dve.scalar_tensor_tensor(filt_abs[:], least, -1.0, filt_abs[:], ALU.mult, ALU.max).then_inc(y_sd, 1)

        filter_parts(0)
        for n in range(4):
            q, o = n // 2, n % 2
            dve.wait_ge(y_tp, n + 1)
            dve.tensor_copy(z_nat[:].rearrange("p b c -> p (b c)"), flat[:, 2048:3072]).then_inc(y_zn, 1)
            dve.wait_ge(y_k, n + 1)
            st.did(dve.tensor_scalar(filt_norm[:], psum[:, 6, 0:4], EPS, None, ALU.add))
            st.settle()
            st.did(dve.reciprocal(filt_norm[:], filt_norm[:]))
            dve.wait_ge(y_z, n + 1)
            dve.wait_ge(y_kc, n + 1)
            zr, zi = flat[:, 0:1024], flat[:, 1024:2048]
            kr, ki = (k_spec[:, r].rearrange("p f c -> p (f c)") for r in range(2))
            for r, (a_, b_, op) in enumerate(((zr, zi, ALU.add), (zi, zr, ALU.subtract))):
                st.did(dve.tensor_tensor(y_part[:, 0], a_, kr, ALU.mult))
                st.did(dve.tensor_tensor(y_part[:, 1], b_, ki, ALU.mult))
                st.settle()
                m = dve.tensor_tensor(y_spec[:, r].rearrange("p f c -> p (f c)"), y_part[:, 0], y_part[:, 1], op)
                if r == 0:
                    st.did(m)
                    st.settle()
            m.then_inc(y_y, 1)
            dve.wait_ge(y_y, n + 1)
            if n < 3:
                filter_parts(n + 1)
                dve.wait_ge(y_sd, n + 2)
            dve.wait_ge(y_inv, n + 1)
            for j in range(4):
                t_ = y_part[:, 0, 256 * j:256 * j + 256]
                st.did(dve.tensor_scalar(t_, psum[:, 4 + j // 2, (j % 2) * T:(j % 2) * T + T], filt_norm[:, j:j + 1], None,
                                         ALU.mult))
            st.settle()
            for j in range(4):
                t_ = y_part[:, 0, 256 * j:256 * j + 256]
                st.did(dve.scalar_tensor_tensor(t_, u[:, 4 * q + j], col("hy_bias", 8 * o + 4 * q + j), t_, ALU.mult,
                                                ALU.add))
            st.settle()
            m = dve.tensor_tensor(u[:, 4 * q:4 * q + 4].rearrange("p k t -> p (k t)"), y_part[:, 0],
                                  u[:, 8 + 8 * o + 4 * q:12 + 8 * o + 4 * q].rearrange("p k t -> p (k t)"), ALU.mult)
            m.then_inc(y_new, 1)
            dve.wait_ge(y_new, n + 1)

        def group_norm_dve(n):
            dve.wait_ge(gn_sum, n + 1)
            dve.tensor_scalar(gn_r[:].rearrange("p k t -> p (k t)"), flat[:, 2048 * n:2048 * n + 2048], 1.0 / P, EPS,
                              ALU.mult, ALU.add).then_inc(gn_ms, 1)
            dve.wait_ge(gn_rt, n + 1)
            st.did(dve.reciprocal(gn_i[:], gn_r[:]))
            st.settle()

        dve.memset(filt_norm[:], 0.0).then_inc(gn_in, 1)
        group_norm_dve(0)
        for k in range(8):
            st.did(dve.scalar_tensor_tensor(u[:, k], u[:, k], col("hy_norm", k), gn_i[:, k], ALU.mult, ALU.mult))
        st.settle()
        st.did(dve.tensor_copy(h_hi[:, 0:8], u[:, 0:8]))
        st.settle()
        dve.tensor_tensor(h_lo[:, 0:8], u[:, 0:8], h_hi[:, 0:8].bitcast(F32), ALU.subtract).then_inc(gn_out, 1)

        def residual(name, gate=None, norm=None):
            g0, n = FIRST[name], dict(STREAM)[name]

            def add(i, j):
                dve.wait_ge(half_done, i * 8 + (2 * (g0 + j) + 2))
                xk = x[:, bass.ds(i * RING + j, 1)].rearrange("p a t -> p (a t)")
                if gate is None:
                    m = dve.tensor_tensor(xk, psum[:, j, 0:T], xk, ALU.add)
                else:
                    m = dve.scalar_tensor_tensor(xk, psum[:, j, 0:T], mod[:, bass.ds(i * RING + (gate + j), 1), 0], xk,
                                                 ALU.mult, ALU.add)
                m.then_inc(bank_free, 1)

            with dve.Fori(0, n // RING - 1) as i:
                for j in range(RING):
                    add(i, j)
            for j in range(RING):
                if j == 2 and norm is not None:
                    norm_half_sum(norm, 0)
                add(n // RING - 1, j)

        dve.wait_ge(half_done, 2 * FIRST["out1"])
        dve.tensor_tensor(mod[:, ADA_1:, 0], psum[:, 7, 0:ADA_2], col("b_ada", ADA_1, ADA_2), ALU.add).then_inc(s_mod, 1)
        dve.wait_ge(s_mod, 2)
        st.did(dve.scalar_tensor_tensor(scales[:, 2], mod[:, 4 * KC:5 * KC, 0], 1.0, col("norm2", 0, KC),
                                        ALU.add, ALU.mult))
        dve.wait_ge(x_back, 16)
        residual("out1", 2 * KC, norm="x2")
        dve.wait_ge(bank_free, 4 + bank_of["mlp"])
        norm_dve("x2", x, lambda k: scales[:, 2, k:k + 1], lambda k: mod[:, 3 * KC + k, 0:1], summed=1)

        def up_down_dve(g0, bank0, acc0, hid0, supers, gate):
            first = st.n
            with dve.Fori(0, supers) as i:
                for j in range(8):
                    s = hid[:]
                    dve.wait_ge(hid_ready, i * 8 + (hid0 + j))
                    dve.wait_ge(half_done, i * 32 + (2 * (g0 + j) + 2))
                    ps = psum[:, j % 4, 0:T]
                    dve.tensor_scalar(s, ps, 0.0, None, ALU.max).then_inc(dve_step, 1)
                    dve.wait_ge(dve_step, i * 16 + (first + 2 * j + 1))
                    dve.tensor_tensor(s, s, ps, ALU.mult).then_inc(bank_free, 1)
                    dve.wait_ge(bank_free, i * 8 + (4 + bank0 + j + 1))
                    dve.tensor_copy(hid_hi[:, j], s).then_inc(dve_step, 1)
                    dve.wait_ge(dve_step, i * 16 + (first + 2 * j + 2))
                    dve.tensor_tensor(hid_lo[:, j], s, hid_hi[:, j].bitcast(F32), ALU.subtract).then_inc(hid_ready, 1)
                for d in range(16):
                    dve.wait_ge(half_done, i * 32 + (2 * (g0 + 8) + d + 1))
                    dve.wait_ge(acc_free, i * 16 + (4 + acc0 + d))
                    ps = psum[:, 4 + d % 4, 0:T]
                    dve.scalar_tensor_tensor(x[:, d], ps, mod[:, gate + d, 0:1], x[:, d], ALU.mult,
                                             ALU.add).then_inc(acc_free, 1)
            st.n = first + 16 * supers

        up_down_dve(FIRST["mlp"], bank_of["mlp"], 0, HID0, dict(STREAM)["mlp"] // 16, 5 * KC)
        norm_dve("f1", x, lambda k: col("final1", k), plain=x)

        dve.wait_ge(plain_done, 4)
        norm_dve("mix", x, lambda k: col("mix", k))
        dve.wait_ge(s_aux[4], 16)
        st.did(dve.tensor_copy(pos[:], pos_i[:]))
        for n in range(2):
            if n:
                dve.wait_ge(t_sin, n)
            st.settle()
            st.did(dve.tensor_scalar(sin_a[:], pos[:], col("angles", n), None, ALU.mult))
            reduce_angle(P, t_arg)
            dve.wait_ge(t_sin, n + 1)
            st.did(dve.tensor_tensor(t_half[:], t_half[:], t_half[:], ALU.mult))
            st.settle()
            st.did(dve.tensor_scalar(trig[:, 2 * n + 1], t_half[:], -2.0, 1.0, ALU.mult, ALU.add))
        copy_stage("ret", pr)

        def rotate_dve(src, n0, pairs, kind, a_, b_):
            for n in range(pairs):
                dve.wait_ge(rot_p, n0 + n + 1)
                if n:
                    dve.wait_ge(rot_d, n0 + n)
                sin, cos = (trig[:, 2 * kind + i].unsqueeze(1).broadcast_to([P, 2, T]) for i in range(2))
                x2 = src[:, 2 * n:2 * n + 2]
                st.did(dve.tensor_tensor(a_[:], psum[:, n % 2, :].rearrange("p (k t) -> p k t", k=2), sin, ALU.mult))
                st.did(dve.tensor_tensor(b_[:], x2, cos, ALU.mult))
                st.settle()
                dve.tensor_tensor(x2, a_[:], b_[:], ALU.add).then_inc(rot_d, 1)

        def turn_v_dve(dst, heads, n0):
            for n in range(heads // 2):
                dve.wait_ge(v_tp, n0 + n + 1)
                dve.tensor_copy(dst[:, n % 2, 4 * (n // 2):4 * (n // 2) + 4].rearrange("p k c -> p (k c)"),
                                psum[:, 2 + n % 2, :]).then_inc(v_nat_, 1)

        rotate_dve(pr, 0, 8, 0, rot_a, rot_b)
        turn_v_dve(v_ret, 8, 0)
        dve.wait_ge(s_aux[3], 16)
        for h in range(RET_H):
            dve.wait_ge(r_sc, h + 1)
            if h >= 2:
                dve.wait_ge(r_o, h - 1)
            dve.tensor_tensor(ret_p[:, h % 2, 0:T], psum[:, 4 + h % 2, 0:T], ret_decay[:, h], ALU.mult)
            dve.tensor_tensor(ret_p[:, h % 2, T:], psum[:, 4 + h % 2, T:T + P], ret_decay[:, h, 0:P],
                              ALU.mult).then_inc(r_p, 1)
        group_norm_dve(1)
        dve.wait_ge(r_g, 1)
        st.did(dve.tensor_tensor(pr[:, 0:8], pr[:, 0:8], gn_i[:], ALU.mult))
        st.settle()
        st.did(dve.tensor_tensor(pr[:, 0:8], pr[:, 0:8], pr[:, 24:32], ALU.mult))
        st.settle()
        st.did(dve.tensor_copy(ret_hi[:], pr[:, 0:8]))
        st.settle()
        dve.tensor_tensor(ret_lo[:], pr[:, 0:8], ret_hi[:].bitcast(F32), ALU.subtract).then_inc(gn_out, 1)
        dve.wait_ge(gn_out, 2)
        copy_stage("dil", pd)
        rotate_dve(pd, 8, 12, 1, rot_c, rot_d_)
        turn_v_dve(v_dil, 12, 4)
        dve.wait_ge(s_aux[3], 32)


        def dil_scaled(m_):
            tb = m_ % 2
            keys = P * (tb + 1)
            b = 4 + 2 * (m_ % 2)
            s = dil_s[:, m_ % 2].rearrange("p (g k) -> p g k", g=DIL_G)[:, :, 0:keys]
            dve.wait_ge(d_sc, m_ + 1)
            if m_ >= 2:
                dve.wait_ge(d_tp, m_ - 1)
            ps = flat[:, 512 * b:512 * b + DIL_G * T].rearrange("p (g k) -> p g k", g=DIL_G)[:, :, 0:keys]
            st.did(dve.scalar_tensor_tensor(s, ps, P ** -0.5, dil_mask[:, tb, :, 0:keys], ALU.mult, ALU.add))
            st.settle()
            dve.tensor_reduce(dil_n[:, m_ % 2, 0:1], s, AX.XY, ALU.max, negate=True).then_inc(d_mx, 1)

        dil_scaled(0)
        for m_ in range(2 * DIL_HG):
            h, tb = m_ // 2, m_ % 2
            s = dil_s[:, m_ % 2].rearrange("p (g k) -> p g k", g=DIL_G)[:, :, 0:P * (tb + 1)]
            if m_ + 1 < 2 * DIL_HG:
                dil_scaled(m_ + 1)
            dve.wait_ge(d_e, m_ + 1)
            st.did(dve.reciprocal(dil_n[:, m_ % 2, 2:3], dil_n[:, m_ % 2, 1:2]))
            st.settle()
            dve.tensor_scalar(s, s, dil_n[:, m_ % 2, 2:3], None, ALU.mult).then_inc(d_p, 1)
            dve.wait_ge(d_tp, m_ + 1)
            n = DIL_G * (tb + 1)
            dve.tensor_copy(dil_pt[:, 0:n].rearrange("p n t -> p (n t)"), flat[:, 0:n * P]).then_inc(d_pt, 1)
            if tb == 1:
                dve.wait_ge(d_hi, h + 1)
                dve.tensor_tensor(dil_lo[:, h], psum[:, 2 + h % 2, 0:T], dil_hi[:, h].bitcast(F32),
                                  ALU.subtract).then_inc(d_lo, 1)
        dve.wait_ge(d_lo, DIL_HG)
        copy_stage("gate", pg)
        dve.wait_ge(s_sig, 1)
        g0 = FIRST["br_ret"]
        with dve.Fori(0, KC // 2 // RING) as i:
            for n in range(2 * RING):
                dve.wait_ge(half_done, i * 8 + (2 * g0 + n + 1))
                blk = pg[:, bass.ds(i * 8 + n, 1)].rearrange("p a t -> p (a t)")
                dve.tensor_tensor(blk, psum[:, n % 4, 0:T], blk, ALU.mult).then_inc(bank_free, 1)
        g0 = FIRST["br_dil"]
        dve.wait_ge(bank_free, 4 + bank_of["br_dil"])
        for k in range(KC):
            dve.wait_ge(half_done, 2 * g0 + k // 2 + 1)
            t_, m_ = mrg[:, 0], mrg[:, 1]
            dve.tensor_tensor(t_, psum[:, k % 4, 0:T], pg[:, KC + k], ALU.mult).then_inc(bank_free, 1)
            dve.wait_ge(bank_free, 4 + bank_of["br_dil"] + k + 1)
            st.did(dve.tensor_tensor(m_, t_, pg[:, k], ALU.add))
            st.settle()
            st.did(dve.tensor_copy(h_hi[:, k], m_))
            st.settle()
            m = dve.tensor_tensor(h_lo[:, k], m_, h_hi[:, k].bitcast(F32), ALU.subtract)
            if k < KC - 1:
                st.did(m)
                st.settle()
        m.then_inc(merged, 1)
        dve.wait_ge(merged, 1)
        norm_dve("mem", mem_raw, lambda k: col("mem", k))
        residual("out2")
        copy_part("kv", kv, 0, KC, norm="cross")
        norm_dve("cross", x, lambda k: col("cross", k), summed=1)
        copy_part("kv", kv, KC, KC)
        copy_stage("q", q_mem)
        for n in range(8):
            mb, g = n % 2, n // 2
            dve.wait_ge(m_tp, n + 1)
            dve.tensor_copy(v_mem[:, mb, 4 * g:4 * g + 4].rearrange("p k c -> p (k c)"), psum[:, n % 2, :]).then_inc(m_vn, 1)
        for h in range(MEM_H):
            dve.wait_ge(m_sc, h + 1)
            st.did(dve.tensor_reduce(mem_n[:, h % 2, 0:2], psum[:, 4 + h % 2, :].rearrange("p (b k) -> p b k", b=2),
                                     AX.X, ALU.max, negate=True))
            st.settle()
            dve.tensor_scalar(mem_n[:, h % 2, 0:2], mem_n[:, h % 2, 0:2], (D // MEM_H) ** -0.5, None,
                              ALU.mult).then_inc(m_mx, 1)
            dve.wait_ge(m_e, h + 1)
            st.did(dve.reciprocal(mem_n[:, h % 2, 2:4], mem_n[:, h % 2, 2:4]))
            st.settle()
            dve.tensor_tensor(mem_e[:, h % 2], mem_e[:, h % 2], mem_n[:, h % 2, 2:4].unsqueeze(2).broadcast_to([P, 2, T]),
                              ALU.mult).then_inc(m_p, 1)
            dve.wait_ge(m_pt_, h + 1)
            dve.tensor_copy(mem_pt[:, h % 2].rearrange("p b t -> p (b t)"), psum[:, h % 2, :]).then_inc(m_pc, 1)
            dve.wait_ge(m_hi, h + 1)
            dve.tensor_tensor(h_lo[:, 4 * h:4 * h + 4].rearrange("p k t -> p (k t)"), flat[:, 1024:2048],
                              h_hi[:, 4 * h:4 * h + 4].bitcast(F32).rearrange("p k t -> p (k t)"),
                              ALU.subtract).then_inc(m_lo, 1)
        residual("o", norm="ffn")
        dve.wait_ge(bank_free, 4 + bank_of["pq"])
        norm_dve("ffn", x, lambda k: col("ffn", k), summed=1)
        copy_stage("pq", q_peer)
        LEAST = -3.0e38

        def top16(values, spare, best, index, rows):
            for r in range(2):
                src, e = (values, spare)[r], slice(8 * r, 8 * r + 8)
                st.settle()
                for k in range(rows):
                    st.did(dve.max(best[:, k, e], src[:, k]))
                st.settle()
                for k in range(rows):
                    st.did(dve.max_index(index[:, k, e], best[:, k, e], src[:, k]))
                for k in range(rows if r == 0 else 0):
                    st.did(dve.match_replace(spare[:, k], best[:, k, e], values[:, k], LEAST))

        iota16 = const[:, IOTA, 0:TOPK]
        wide = [P, PEER_H, TOPK, TOPK]
        for tb in range(2):
            dve.wait_ge(p_scc, tb + 1)
            top16(psc[:, tb], psc2, top_v, top_u, 16)
            st.settle()
            st.did(dve.tensor_copy(top_i[:], top_u[:]))
            combo, combo2 = (t_.rearrange("p (h x) n -> p h (x n)", x=2) for t_ in (psc[:, tb], psc2[:]))
            v4 = top_v[:].rearrange("p (h two) r -> p h two r", two=2)
            i4 = top_i[:].rearrange("p (h two) r -> p h two r", two=2)
            st.did(dve.tensor_tensor(combo.rearrange("p h (x y) -> p h x y", x=TOPK),
                                     v4[:, :, 0].unsqueeze(3).broadcast_to(wide),
                                     v4[:, :, 1].unsqueeze(2).broadcast_to(wide), ALU.add))
            top16(combo, combo2, com_v, com_u, PEER_H)
            st.settle()
            st.did(dve.tensor_scalar(com_q[:, 0], com_u[:], 4, None, ALU.logical_shift_right))
            st.did(dve.tensor_scalar(com_q[:, 1], com_u[:], 15, None, ALU.bitwise_and))
            st.settle()
            st.did(dve.tensor_copy(com_f[:], com_q[:]))
            for s in range(2):
                st.settle()
                st.did(dve.tensor_tensor(pick[:], com_f[:, s].unsqueeze(3).broadcast_to(wide),
                                         iota16.unsqueeze(1).unsqueeze(1).broadcast_to(wide), ALU.is_equal))
                st.settle()
                st.did(dve.tensor_tensor(pick[:], pick[:], i4[:, :, s].unsqueeze(2).broadcast_to(wide), ALU.mult))
                st.settle()
                st.did(dve.tensor_reduce(chosen[:, s, tb], pick[:], AX.X, ALU.add))
            m = dve.tensor_tensor(chosen[:, 2, tb], com_v[:], com_v[:, :, 0:1].broadcast_to([P, PEER_H, TOPK]),
                                  ALU.subtract)
            if tb == 0:
                st.did(m)
        m.then_inc(p_cv, 1)
        dve.wait_ge(p_ge, 1)
        st.did(dve.tensor_reduce(gate_n[:], chosen[:, 2], AX.X, ALU.add))
        st.settle()
        st.did(dve.reciprocal(gate_n[:], gate_n[:]))
        st.settle()
        dve.tensor_tensor(chosen[:, 2], chosen[:, 2], gate_n[:].unsqueeze(3).broadcast_to([P, 2, PEER_H, TOPK]),
                          ALU.mult).then_inc(p_tab, 1)
        dve.wait_ge(p_tt, 1)
        turned = psum[:, 6:8, 0:3 * P].rearrange("p b (k t) -> p k b t", k=3)
        g_hi, g_lo = (gate_t[:, n].rearrange("p (b t) -> p b t", b=2) for n in range(2))
        for k in range(2):
            st.did(dve.tensor_copy(tabs[:, k].rearrange("p (b t) -> p b t", b=2), turned[:, k]))
        st.did(dve.tensor_copy(g_hi, turned[:, 2]))
        st.settle()
        st.did(dve.tensor_tensor(g_lo, turned[:, 2], g_hi.bitcast(F32), ALU.subtract))
        st.settle()
        for b in range(2):
            dve.memset(psum[:, 4 + b, :], 0.0).then_inc(e_gc, 1)
        dve.memset(hot_e[:], 0.0).then_inc(e_oh, 1)

        def one_hot(q, n, b, first):
            tok = bass.ds(n * 8, 8)
            to1, to2 = [P, 8, QUARTER], [P, 8, P]
            dve.wait_ge(e_oh, n + (32 * q + 1))
            dve.tensor_tensor(hot_e[:], tabs[:, 0, tok].unsqueeze(2).broadcast_to(to1),
                              const[:, IOTA, QUARTER * q:QUARTER * (q + 1)].unsqueeze(1).broadcast_to(to1),
                              ALU.is_equal).then_inc(dve_step, 1)
            dve.tensor_tensor(hot2[:, b], tabs[:, 1, tok].unsqueeze(2).broadcast_to(to2),
                              const[:, IOTA].unsqueeze(1).broadcast_to(to2), ALU.is_equal).then_inc(dve_step, 1)
            dve.wait_ge(dve_step, first + 1)
            to3 = [P, 2, 8, QUARTER]
            dve.tensor_tensor(hot1[:, b], hot_e[:].unsqueeze(1).broadcast_to(to3),
                              gate_t[:, :, tok].bitcast(F32).unsqueeze(3).broadcast_to(to3), ALU.mult).then_inc(e_oh, 1)

        def gates_out(q, n, b):
            dve.wait_ge(e_g, n + (32 * q + 1))
            dve.tensor_reduce(gates[:, :, bass.ds(n * 8, 8)].rearrange("p e t -> p t e"),
                              psum[:, 4 + b, :].rearrange("p (t s e) -> p t e s", t=8, s=2), AX.X, ALU.add
                              ).then_inc(e_gc, 1)

        def hidden_four(q, s, buf, first):
            for j in range(4):
                dve.wait_ge(hid_ready, s * 4 + (HID0 + MLP_H + QUARTER * q + j))
                b0, g0 = (t_[:, bass.ds(s * 4 + j, 1)].rearrange("p a t -> p (a t)") for t_ in (before, gates))
                dve.tensor_tensor(hid[:], b0, g0, ALU.mult).then_inc(dve_step, 1)
                dve.wait_ge(dve_step, first + (2 * j + 1))
                dve.tensor_copy(hid_hi[:, 4 * buf + j], hid[:]).then_inc(dve_step, 1)
                dve.wait_ge(dve_step, first + (2 * j + 2))
                dve.tensor_tensor(hid_lo[:, 4 * buf + j], hid[:], hid_hi[:, 4 * buf + j].bitcast(F32),
                                  ALU.subtract).then_inc(hid_ready, 1)

        def sums_out(q, s):
            g0 = FIRST["peer"] + 2 * QUARTER * q + QUARTER
            for n in range(8):
                dve.wait_ge(half_done, s * 8 + (2 * g0 + n + 1))
                dve.wait_ge(acc_free, s * 8 + (4 + n_acc["peer"] + 64 * q + n))
                x2 = x[:, 2 * n:2 * n + 2].rearrange("p k t -> p (k t)")
                dve.tensor_tensor(x2, psum[:, 4 + n % 4, :], x2, ALU.add).then_inc(acc_free, 1)

        for q in range(4):
            dve.wait_ge(hid_ready, HID0 + MLP_H + QUARTER * q)
            dve.wait_ge(acc_free, 4 + n_acc["peer"] + 64 * q)
            f0 = st.n
            one_hot(q, 0, 0, f0)
            with dve.Fori(0, 15) as i:
                one_hot(q, i * 2 + 1, 1, i * 4 + (f0 + 2))
                gates_out(q, i * 2, 0)
                one_hot(q, i * 2 + 2, 0, i * 4 + (f0 + 4))
                gates_out(q, i * 2 + 1, 1)
            one_hot(q, 31, 1, f0 + 62)
            gates_out(q, 30, 0)
            gates_out(q, 31, 1)
            f0 += 64
            dve.wait_ge(e_gc, 32 * q + 34)
            dve.wait_ge(bank_free, 4 + bank_of["peer"] + QUARTER * (q + 1))
            hidden_four(q, 0, 0, f0)
            with dve.Fori(0, 3) as i:
                hidden_four(q, i * 2 + 1, 1, i * 16 + (f0 + 8))
                sums_out(q, i * 2)
                hidden_four(q, i * 2 + 2, 0, i * 16 + (f0 + 16))
                sums_out(q, i * 2 + 1)
            hidden_four(q, 7, 1, f0 + 56)
            sums_out(q, 6)
            sums_out(q, 7)
            st.n = f0 + 64
        norm_dve("f2", x, lambda k: col("final2", k), plain=x)

    ctx.close()


def column_blocks(tile_matrix):
    k, n = tile_matrix.shape
    return tile_matrix.reshape(k // P, P, n // P, P).transpose(2, 1, 0, 3).reshape(n // P, P, k)


def ada_rows(w):
    return w.reshape(4, 4, P, w.shape[1] // 512, 512).transpose(3, 0, 2, 1, 4).reshape(-1, P, D)


def ada_sums(w):
    return w.reshape(KC, P, w.shape[1] // D, D).transpose(2, 0, 1, 3).reshape(-1, P, D)


def packed_blocks(w, per):
    k, n = w.shape
    return w.reshape(k // P, P, n // (per * P), per, P).transpose(2, 1, 3, 0, 4).reshape(n // (per * P), P, per * k)


def down_blocks(w):
    g = w.shape[0] // (8 * P)
    return w.reshape(g, 8, P, 8, 2, P).transpose(0, 3, 2, 4, 1, 5).reshape(g * 8, P, D)


def quarters(w1, w2):
    down = w2.reshape(EXPERT_B // 4, 4, P, 4, 4, P).transpose(0, 3, 2, 4, 1, 5).reshape(4, QUARTER, P, D)
    return np.concatenate([column_blocks(w1).reshape(4, QUARTER, P, D), down], 1).reshape(-1, P, D)


def up_down(w1, w2):
    up, down = column_blocks(w1), down_blocks(w2)
    g = up.shape[0] // 8
    return np.concatenate([up.reshape(g, 8, P, D), down.reshape(g, 8, P, D)], 1).reshape(-1, P, D)


def on_partitions(v):
    return np.ascontiguousarray(v.reshape(-1, P).T)


def acts(v):
    return np.ascontiguousarray(v.T.reshape(-1, P, v.shape[0]).transpose(1, 0, 2))


def constants():
    f = np.float32
    i, j = np.arange(P)[:, None], np.arange(P)[None, :]
    ret = np.zeros((P, P))
    rot = np.zeros((P, P))
    m = np.arange(HD)
    ret[2 * m + 1, 2 * m], ret[2 * m, 2 * m + 1] = -1, 1
    rot[m + HD, m], rot[m, m + HD] = -1, 1
    square = np.stack([i == j, np.ones((P, P)), i <= j, i >= j, i > j, i < j, ret, rot, np.broadcast_to(j, (P, P))], 1)
    t, k = np.arange(T)[:, None], np.arange(T)[None, :]
    ang = 2 * np.pi * t * (k + 0.5) / (2 * T)
    dft = np.stack([np.cos(ang), np.sin(ang), np.cos(ang).T / T, np.sin(ang).T / T])
    dft = dft.reshape(4, 2, P, T).transpose(2, 0, 1, 3)
    t = np.linspace(0.0, 1.0, T, dtype=f)[:, None]
    deltas = np.linspace(math.log(1e-2) / 1.5, math.log(1e-2) / 0.3, 1024, dtype=f)
    window = np.exp(-t * np.abs(deltas)).reshape(2, P, 1024).transpose(1, 0, 2)
    bands = (FEATS - 1) // 2
    w = f(2.0 * math.pi) * np.arange(T, dtype=f)[:, None] / f(T)
    fr = np.linspace(1e-4, bands - 1, bands, dtype=f)[None, :]
    feats = np.concatenate([t, np.cos(fr * w), -np.sin(fr * w)], -1).T
    log_g = np.log1p(-np.exp2(-5.0 - np.arange(RET_H)))
    diff = np.arange(T)[None, :] - np.arange(P)[:, None]
    decay = np.stack([np.where(diff >= 0, np.exp(lg * np.maximum(diff, 0)), 0.0) for lg in log_g], 1) * P ** -0.5
    q, key = np.arange(T)[:, None], np.arange(T)[None, :]
    masks = []
    for window_, rate in ((128, 1), (512, 4), (2048, 16)):
        d = q - key
        masks.append(np.where((d >= 0) & (d % rate == 0) & (d // rate <= window_ // rate), 0.0, -1e30))
    masks = np.stack(masks, 1).reshape(2, P, 3, T).transpose(1, 0, 2, 3)
    ret_angle = np.repeat(1.0 / (10000.0 ** np.linspace(0.0, 1.0, HD, dtype=f).astype(np.float64)), 2)
    rot_angle = np.tile(1.0 / (10000.0 ** (np.arange(HD) / HD)), 2)
    out = dict(const=square, dft=dft, window=window, feats=feats, ret_decay=decay, dil_mask=masks)
    return {n: np.ascontiguousarray(v, dtype=f) for n, v in out.items()}, np.stack([ret_angle, rot_angle], 1).astype(f)


def layout(**v):
    one = {n: np.asarray(v[n])[0] for n in v if np.asarray(v[n]).ndim > 1 and n not in ("c", "positions_2")}
    w_in = one["w_in"]
    hy, xbc_, dt_, z_ = np.split(w_in, [3072, 3072 + 1536, 3072 + 1536 + 32], axis=1)
    w2 = one["w_in_2"]
    stream = np.concatenate([
        ada_rows(one["w_ada"][:, :ADA_1 * P]), column_blocks(xbc_), column_blocks(hy), column_blocks(z_),
        ada_sums(one["w_ada"][:, ADA_1 * P:]),
        column_blocks(one["w_out"]), up_down(one["w_mlp1"], one["w_mlp2"]), column_blocks(w2),
        packed_blocks(one["w_br_ret_2"], 2), packed_blocks(one["w_br_dil_2"], 4), column_blocks(one["w_out_2"]),
        column_blocks(one["w_kv_mem_2"]), column_blocks(one["w_q_mem_2"]), column_blocks(one["w_o_mem_2"]),
        column_blocks(one["w_peer_q_2"]), quarters(one["peer_u_2"].T, one["peer_v_2"])])
    consts, angles = constants()
    by_column = dict(
        b_ada=one["b_ada"], norm1=one["norm1_w"], hy_w=one["hy_conv_w"], hy_b=one["hy_conv_b"],
        hy_bias=one["hy_bias"], hy_norm=one["hy_norm_w"], ssd_w=one["ssd_conv_w"], ssd_b=one["ssd_conv_b"],
        ssd_norm=one["ssd_norm_w"], ssd_d=np.repeat(one["ssd_d"], HD), norm2=one["norm2_w"],
        final1=np.asarray(v["final_norm_w"]), mix=one["g_mix_2"], cross=one["g_cross_2"], mem=one["g_mem_2"],
        ffn=one["g_ffn_2"], final2=np.asarray(v["g_final_2"]), zero=np.zeros(D, np.float32), angles=angles.T)
    cols = np.concatenate([on_partitions(np.ascontiguousarray(by_column[n])) for n, _ in COLUMNS], 1)
    c = np.stack([np.asarray(v["c"])[0], np.asarray(v["c_ctx"])], 1).reshape(KC, P, 2).transpose(1, 0, 2)
    small = np.stack([one["filt_b1"], one["filt_freq"], one["filt_b2"]], 1)
    arrays = dict(
        consts, stream=stream, cols=cols, c=c, x=acts(one["x"]), ctx=acts(one["ctx"]), mem=acts(one["mem_2"]),
        wdt=dt_.reshape(KC, P, 32).transpose(1, 0, 2),
        dt_bias=np.broadcast_to(one["dt_bias"].reshape(1, 32), (P, 32)),
        a_log=np.broadcast_to(one["a_log"].reshape(1, 32), (P, 32)),
        filt_w1=one["filt_w1"], filt_w2=one["filt_w2"], filt_w3=one["filt_w3"], filt_cols=small,
        pos=np.broadcast_to(np.asarray(v["positions_2"])[0:1], (P, T)),
        subkeys=one["peer_subkeys_2"].reshape(16, P, P).transpose(2, 0, 1))
    return {n: np.ascontiguousarray(x_) for n, x_ in arrays.items()}


def kernel(**inputs):
    import concourse.bacc as bacc
    from concourse.bass_utils import run_bass_kernel_spmd

    arrays = layout(**inputs)
    nc = bacc.Bacc("TRN2", target_bir_lowering=False, num_devices=1)
    a = {n: nc.dram_tensor(n, v.shape, mybir.dt.from_np(v.dtype), kind="ExternalInput").ap() for n, v in arrays.items()}
    out = nc.dram_tensor("out", (P, KC, T), F32, kind="ExternalOutput").ap()
    build(nc, a, out)
    got = run_bass_kernel_spmd(nc, [arrays], core_ids=[0]).results[0]["out"]
    return np.ascontiguousarray(got.transpose(1, 0, 2).reshape(D, T).T)[None]
```
